# Optimizing a Trainium2 kernel written in Bass

```python
import jax, jax.numpy as jnp
from jax import lax
import numpy as np

D_MODEL = 1024
BATCH = 1
SEQ = 1024
DEPTH = 1
DEC_BATCH = 1
DEC_SEQ = 32
PAST_LEN = 512

CHUNK = 64
D_LRU = 1024
N_LRU_BLOCKS = 8
LRU_BLOCK = D_LRU // N_LRU_BLOCKS
CONV_WIDTH = 4
LRU_C = 8.0
N_RET_HEADS = 8
RET_QK_DIM = 128
RET_V_DIM = 128
D_RET_QK = N_RET_HEADS * RET_QK_DIM
D_RET_V = N_RET_HEADS * RET_V_DIM
ROPE_BASE = 10000.0
N_GROUPS = 4
EXPERTS_PER_GROUP = 8
N_EXPERTS = N_GROUPS * EXPERTS_PER_GROUP
TOP_K = 2
D_EXPERT = 512
MOE_BLOCK = 128
EPS = 1e-6
IN_WIDTHS = (D_LRU, D_LRU, D_RET_QK, D_RET_QK, D_RET_V, D_RET_V, D_MODEL, D_MODEL)
D_IN = sum(IN_WIDTHS)

kernel_name = "hybrid_rglru_retention_hmoe_stream_step"

def rms_norm(x, g):
    xf = x.astype(jnp.float32)
    y = xf * lax.rsqrt(jnp.mean(xf * xf, axis=-1, keepdims=True) + EPS)
    return (y * g.astype(jnp.float32)).astype(x.dtype)

def rope(x, pos):
    half = x.shape[-1] // 2
    inv = jnp.power(ROPE_BASE, -jnp.arange(half, dtype=jnp.float32) / half)
    ang = pos.astype(jnp.float32)[:, None] * inv[None, :]
    cos = jnp.cos(ang)[None, :, None, :]
    sin = jnp.sin(ang)[None, :, None, :]
    x1, x2 = x[..., :half], x[..., half:]
    return jnp.concatenate([x1 * cos - x2 * sin, x1 * sin + x2 * cos], axis=-1)

def lru_scan(a, b, h0):
    b = b.at[:, 0].add(a[:, 0] * h0)
    def comb(l, r):
        return (l[0] * r[0], r[0] * l[1] + r[1])
    _, h = lax.associative_scan(comb, (a, b), axis=1)
    return h

def retention(q, k, v, s0, chunk):
    B, L, H, DK = q.shape
    DV = v.shape[-1]
    nc = L // chunk
    log_g = jnp.log1p(-jnp.power(2.0, -5.0 - jnp.arange(H, dtype=jnp.float32)))
    idx = jnp.arange(chunk, dtype=jnp.float32)
    intra = jnp.exp(log_g[:, None, None] * jnp.abs(idx[:, None] - idx[None, :]))
    q_dec = jnp.exp(log_g[None, :] * (idx[:, None] + 1.0))
    k_dec = jnp.exp(log_g[None, :] * (chunk - 1.0 - idx[:, None]))
    chunk_dec = jnp.exp(log_g * chunk)
    qc = q.reshape(B, nc, chunk, H, DK)
    kc = k.reshape(B, nc, chunk, H, DK)
    vc = v.reshape(B, nc, chunk, H, DV)
    scores = jnp.einsum('bnihd,bnjhd->bnhij', qc, kc) * intra[None, None]
    o_intra = jnp.einsum('bnhij,bnjhe->bnihe', scores, vc)
    kv = jnp.einsum('bnjhd,bnjhe->bnhde', kc * k_dec[None, None, :, :, None], vc)

    def step(s, kv_n):
        return chunk_dec[None, :, None, None] * s + kv_n, s

    s_final, s_in = lax.scan(step, s0, jnp.moveaxis(kv, 1, 0))
    s_in = jnp.moveaxis(s_in, 0, 1)
    o_cross = jnp.einsum('bnihd,bnhde->bnihe', qc * q_dec[None, None, :, :, None], s_in)
    return (o_intra + o_cross).reshape(B, L, H, DV), s_final

def head_group_norm(o, g):
    mu = jnp.mean(o, axis=-1, keepdims=True)
    var = jnp.mean(jnp.square(o - mu), axis=-1, keepdims=True)
    return (o - mu) * lax.rsqrt(var + EPS) * g.astype(jnp.float32).reshape(N_RET_HEADS, RET_V_DIM)

def mixer(xn, pos, conv_state, lru_h0, ret_s0, chunk, w_in, conv_w, conv_b, lru_wa, lru_ba,
          lru_wx, lru_bx, lru_lambda, ret_gn_g, w_lru_o, w_ret_o, w_out):
    B, L, _ = xn.shape
    dt = xn.dtype
    f32 = jnp.float32
    split_idx = [int(s) for s in np.cumsum(IN_WIDTHS)[:-1]]
    proj = xn @ w_in
    lx, lg, q, k, v, rg, ga, gb = jnp.split(proj, split_idx, axis=-1)

    xp = jnp.concatenate([conv_state.astype(lx.dtype), lx], axis=1)
    xc = conv_b + sum(xp[:, j:j + L] * conv_w[j] for j in range(CONV_WIDTH))
    new_conv = xp[:, -(CONV_WIDTH - 1):]
    xb = xc.reshape(B, L, N_LRU_BLOCKS, LRU_BLOCK)
    r = jax.nn.sigmoid((jnp.einsum('blnc,ncd->blnd', xb, lru_wa).reshape(B, L, D_LRU) + lru_ba).astype(f32))
    i = jax.nn.sigmoid((jnp.einsum('blnc,ncd->blnd', xb, lru_wx).reshape(B, L, D_LRU) + lru_bx).astype(f32))
    log_a = -LRU_C * r * jax.nn.softplus(-lru_lambda.astype(f32))
    a = jnp.exp(log_a)
    mult = jnp.sqrt(-jnp.expm1(2.0 * log_a))
    mult = jnp.where((pos == 0)[None, :, None], 1.0, mult)
    hs = lru_scan(a, mult * i * xc.astype(f32), lru_h0.astype(f32))
    new_h = hs[:, -1]
    y_lru = (jax.nn.gelu(lg.astype(f32)) * hs).astype(dt) @ w_lru_o

    qh = rope(q.reshape(B, L, N_RET_HEADS, RET_QK_DIM).astype(f32), pos)
    kh = rope(k.reshape(B, L, N_RET_HEADS, RET_QK_DIM).astype(f32), pos) * (RET_QK_DIM ** -0.5)
    vh = v.reshape(B, L, N_RET_HEADS, RET_V_DIM).astype(f32)
    o, new_s = retention(qh, kh, vh, ret_s0.astype(f32), chunk)
    o = head_group_norm(o, ret_gn_g).reshape(B, L, D_RET_V)
    y_ret = (jax.nn.silu(rg.astype(f32)) * o).astype(dt) @ w_ret_o

    merged = jax.nn.sigmoid(ga.astype(f32)) * y_lru.astype(f32) + jax.nn.sigmoid(gb.astype(f32)) * y_ret.astype(f32)
    out = merged.astype(dt) @ w_out
    return out, new_conv, new_h, new_s

def hier_moe(x, w_rg, b_rg, w_re, b_re, w_gate, w_up, w_down):
    T = x.shape[0]
    dt = x.dtype
    f32 = jnp.float32
    g_logits = (x @ w_rg).astype(f32) + b_rg.astype(f32)
    g_prob = jax.nn.softmax(g_logits, axis=-1)
    _, grp = lax.top_k(g_logits, 1)
    g_top = jnp.take_along_axis(g_prob, grp, axis=1)[:, 0]
    e_logits = ((x @ w_re).astype(f32) + b_re.astype(f32)).reshape(T, N_GROUPS, EXPERTS_PER_GROUP)
    sel = jnp.take_along_axis(e_logits, grp[:, :, None], axis=1)[:, 0]
    e_prob = jax.nn.softmax(sel, axis=-1)
    topv, topi = lax.top_k(e_prob, TOP_K)
    topv = topv / jnp.sum(topv, axis=-1, keepdims=True)
    gate = g_top[:, None] * topv
    eid = grp * EXPERTS_PER_GROUP + topi

    A = T * TOP_K
    flat_e = eid.reshape(A)
    flat_tok = jnp.repeat(jnp.arange(T, dtype=jnp.int32), TOP_K)
    flat_w = gate.reshape(A)
    order = jnp.argsort(flat_e, stable=True)
    se = flat_e[order]
    counts = jnp.bincount(flat_e, length=N_EXPERTS)
    padded = (counts + MOE_BLOCK - 1) // MOE_BLOCK * MOE_BLOCK
    pad_end = jnp.cumsum(padded)
    pad_start = pad_end - padded
    start = jnp.cumsum(counts) - counts
    dest = pad_start[se] + jnp.arange(A, dtype=jnp.int32) - start[se]
    nb = (A + N_EXPERTS * (MOE_BLOCK - 1) + MOE_BLOCK - 1) // MOE_BLOCK
    P = nb * MOE_BLOCK
    row_tok = jnp.zeros((P,), jnp.int32).at[dest].set(flat_tok[order])
    row_w = jnp.zeros((P,), f32).at[dest].set(flat_w[order])
    block_e = jnp.minimum(jnp.searchsorted(pad_end, jnp.arange(nb) * MOE_BLOCK, side='right'), N_EXPERTS - 1)
    xbuf = x[row_tok].reshape(nb, MOE_BLOCK, x.shape[1])

    def block_fn(args):
        xb, e = args
        h = jax.nn.silu((xb @ w_gate[e]).astype(f32)) * (xb @ w_up[e]).astype(f32)
        return h.astype(dt) @ w_down[e]

    ybuf = lax.map(block_fn, (xbuf, block_e)).reshape(P, x.shape[1])
    out = jnp.zeros((T, x.shape[1]), f32).at[row_tok].add(ybuf.astype(f32) * row_w[:, None])
    return out.astype(dt)

def run_trunk(x, pos, conv_s, lru_s, ret_s, chunk, norm_mix_g, w_in, conv_w, conv_b, lru_wa, lru_ba,
              lru_wx, lru_bx, lru_lambda, ret_gn_g, w_lru_o, w_ret_o, w_out, norm_ffn_g,
              w_router_group, b_router_group, w_router_expert, b_router_expert,
              w_exp_gate, w_exp_up, w_exp_down, norm_final_g):
    B, L, D = x.shape
    convs, lrus, rets = [], [], []
    h = x
    for l in range(DEPTH):
        mix, c_new, h_new, s_new = mixer(
            rms_norm(h, norm_mix_g[l]), pos, conv_s[l], lru_s[l], ret_s[l], chunk,
            w_in[l], conv_w[l], conv_b[l], lru_wa[l], lru_ba[l], lru_wx[l], lru_bx[l],
            lru_lambda[l], ret_gn_g[l], w_lru_o[l], w_ret_o[l], w_out[l])
        h = h + mix
        ffn = hier_moe(rms_norm(h, norm_ffn_g[l]).reshape(B * L, D), w_router_group[l], b_router_group[l],
                       w_router_expert[l], b_router_expert[l], w_exp_gate[l], w_exp_up[l], w_exp_down[l])
        h = h + ffn.reshape(B, L, D)
        convs.append(c_new)
        lrus.append(h_new)
        rets.append(s_new)
    y = rms_norm(h, norm_final_g)
    return y, jnp.stack(convs), jnp.stack(lrus), jnp.stack(rets)

def setup_inputs(seed: int = 0) -> dict:
    key = jax.random.key(seed)
    ks = jax.random.split(key, 32)
    f32 = jnp.float32
    nrm = lambda k, shape, s: jax.random.normal(k, shape, f32) * s
    u = jax.random.uniform(ks[12], (DEPTH, D_LRU), f32, 0.9 ** (1.0 / LRU_C), 0.999 ** (1.0 / LRU_C))
    return {
        'x_prompt': nrm(ks[0], (BATCH, SEQ, D_MODEL), 1.0),
        'x_sample': nrm(ks[1], (DEC_BATCH, DEC_SEQ, D_MODEL), 1.0),
        'cache_conv': nrm(ks[2], (DEPTH, DEC_BATCH, CONV_WIDTH - 1, D_LRU), 1.0),
        'state_lru': nrm(ks[3], (DEPTH, DEC_BATCH, D_LRU), 0.5),
        'state_ret': nrm(ks[4], (DEPTH, DEC_BATCH, N_RET_HEADS, RET_QK_DIM, RET_V_DIM), 0.3),
        'norm_mix_g': 1.0 + nrm(ks[5], (DEPTH, D_MODEL), 0.02),
        'w_in': nrm(ks[6], (DEPTH, D_MODEL, D_IN), D_MODEL ** -0.5),
        'conv_w': nrm(ks[7], (DEPTH, CONV_WIDTH, D_LRU), CONV_WIDTH ** -0.5),
        'conv_b': nrm(ks[8], (DEPTH, D_LRU), 0.02),
        'lru_wa': nrm(ks[9], (DEPTH, N_LRU_BLOCKS, LRU_BLOCK, LRU_BLOCK), LRU_BLOCK ** -0.5),
        'lru_ba': nrm(ks[10], (DEPTH, D_LRU), 0.02),
        'lru_wx': nrm(ks[11], (DEPTH, N_LRU_BLOCKS, LRU_BLOCK, LRU_BLOCK), LRU_BLOCK ** -0.5),
        'lru_bx': nrm(ks[13], (DEPTH, D_LRU), 0.02),
        'lru_lambda': jnp.log(u) - jnp.log1p(-u),
        'ret_gn_g': 1.0 + nrm(ks[14], (DEPTH, D_RET_V), 0.02),
        'w_lru_o': nrm(ks[15], (DEPTH, D_LRU, D_MODEL), D_LRU ** -0.5),
        'w_ret_o': nrm(ks[16], (DEPTH, D_RET_V, D_MODEL), D_RET_V ** -0.5),
        'w_out': nrm(ks[17], (DEPTH, D_MODEL, D_MODEL), D_MODEL ** -0.5),
        'norm_ffn_g': 1.0 + nrm(ks[18], (DEPTH, D_MODEL), 0.02),
        'w_router_group': nrm(ks[19], (DEPTH, D_MODEL, N_GROUPS), D_MODEL ** -0.5),
        'b_router_group': nrm(ks[20], (DEPTH, N_GROUPS), 0.01),
        'w_router_expert': nrm(ks[21], (DEPTH, D_MODEL, N_EXPERTS), D_MODEL ** -0.5),
        'b_router_expert': nrm(ks[22], (DEPTH, N_EXPERTS), 0.01),
        'w_exp_gate': nrm(ks[23], (DEPTH, N_EXPERTS, D_MODEL, D_EXPERT), D_MODEL ** -0.5),
        'w_exp_up': nrm(ks[24], (DEPTH, N_EXPERTS, D_MODEL, D_EXPERT), D_MODEL ** -0.5),
        'w_exp_down': nrm(ks[25], (DEPTH, N_EXPERTS, D_EXPERT, D_MODEL), D_EXPERT ** -0.5),
        'norm_final_g': 1.0 + nrm(ks[26], (D_MODEL,), 0.02),
    }

def reference(x_prompt, x_sample, cache_conv, state_lru, state_ret, norm_mix_g, w_in, conv_w, conv_b,
              lru_wa, lru_ba, lru_wx, lru_bx, lru_lambda, ret_gn_g, w_lru_o, w_ret_o, w_out, norm_ffn_g,
              w_router_group, b_router_group, w_router_expert, b_router_expert,
              w_exp_gate, w_exp_up, w_exp_down, norm_final_g):
    B, L, _ = x_prompt.shape
    DB, DL, _ = x_sample.shape
    pos_p = jnp.arange(L, dtype=jnp.int32)
    conv0 = jnp.zeros((DEPTH, B, CONV_WIDTH - 1, D_LRU), x_prompt.dtype)
    lru0 = jnp.zeros((DEPTH, B, D_LRU), jnp.float32)
    ret0 = jnp.zeros((DEPTH, B, N_RET_HEADS, RET_QK_DIM, RET_V_DIM), jnp.float32)
    y_prompt, conv_prompt, lru_prompt, ret_prompt = run_trunk(
        x_prompt, pos_p, conv0, lru0, ret0, CHUNK, norm_mix_g, w_in, conv_w, conv_b, lru_wa, lru_ba,
        lru_wx, lru_bx, lru_lambda, ret_gn_g, w_lru_o, w_ret_o, w_out, norm_ffn_g,
        w_router_group, b_router_group, w_router_expert, b_router_expert,
        w_exp_gate, w_exp_up, w_exp_down, norm_final_g)
    pos_s = PAST_LEN + jnp.arange(DL, dtype=jnp.int32)
    y_sample, conv_sample, lru_sample, ret_sample = run_trunk(
        x_sample, pos_s, cache_conv, state_lru, state_ret, DL, norm_mix_g, w_in, conv_w, conv_b,
        lru_wa, lru_ba, lru_wx, lru_bx, lru_lambda, ret_gn_g, w_lru_o, w_ret_o, w_out, norm_ffn_g,
        w_router_group, b_router_group, w_router_expert, b_router_expert,
        w_exp_gate, w_exp_up, w_exp_down, norm_final_g)
    return (y_prompt, y_sample, conv_prompt, lru_prompt, ret_prompt, conv_sample, lru_sample, ret_sample)


_drawn_inputs = setup_inputs


def setup_inputs(seed=0):
    import zlib

    import numpy as np

    out = dict(_drawn_inputs(seed))
    spreads = {}
    factors = {'lru_ba': 8.0,
     'lru_bx': 7.033,
     'ret_gn_g': 3.101,
     'b_router_group': 5.128,
     'b_router_expert': 4.013,
     'norm_final_g': 2.79}
    for name, (base, spread) in spreads.items():
        noise = np.random.default_rng([zlib.crc32(name.encode()), seed]).standard_normal(out[name].shape)
        drawn = base * np.exp(spread * noise) if base else spread * noise
        out[name] = __import__('jax').numpy.asarray(drawn.astype(out[name].dtype))
    for name, factor in factors.items():
        out[name] = (out[name] * factor).astype(out[name].dtype)
    return out
```

```python
from contextlib import ExitStack

import numpy as np

import concourse.bass as bass
from concourse import mybir

F32 = mybir.dt.float32
F32R = mybir.dt.float32r
U32 = mybir.dt.uint32
I32 = mybir.dt.int32
ALU = mybir.AluOpType
ACT = mybir.ActivationFunctionType
AX = mybir.AxisListType
ds = bass.ds

P = 128
D = 1024
KD = D // P
SEQ = 1024
DEC = 32
PAST = 512
T = SEQ + DEC
NT = SEQ // P
NTILE = NT + 1
CT = 3
CW = T // CT
CONV = 4
PAD = CONV - 1
XP = PAD + SEQ + PAD + DEC
XC = XP - PAD
S0 = SEQ + PAD
CHUNK = 64
HEADS = 8
GROUPS = 4
PER_GROUP = 8
E = GROUPS * PER_GROUP
FE = 512
KF = FE // P
SLOTS = 128
ROUT = GROUPS + E
EPS = 1e-6
BIG = 3.0e38

PR_GMIX, PR_CONVW, PR_CONVB, PR_BA, PR_BX, PR_LAM, PR_GN, PR_LRU, PR_CACHE = 0, 8, 40, 48, 56, 64, 72, 80, 88
PR_N = 112
ST_CONVP, ST_CONVS, ST_LRUP, ST_LRUS = 0, 24, 48, 56
ST_N = 64
TB_COS = 0
TB_SIN = TB_COS + T
TB_MASK = TB_SIN + T
TB_QDEC = TB_MASK + HEADS * P
TB_KDEC = TB_QDEC + HEADS * P
TB_KDECS = TB_KDEC + HEADS
TB_GT = TB_KDECS + HEADS
TB_GS = TB_GT + HEADS
TB_N = TB_GS + HEADS
CN_ID = 0
CN_TRI = CN_ID + P
CN_ONE = CN_TRI + P
CN_IOTA = CN_ONE + P
CN_TOK = CN_IOTA + P
CN_DST = CN_TOK + NTILE
CN_N = CN_DST + 2 * NTILE
NOWHERE = float(1 << 20)
LOG_TERMS = 9


def shape_tables():
    f32 = np.float32
    half = P // 2
    inv = np.power(f32(10000.0), -np.arange(half, dtype=f32) / f32(half)).astype(f32)
    pos = np.concatenate([np.arange(SEQ), PAST + np.arange(DEC)]).astype(f32)
    ang = (pos[None, :] * inv[:, None]).astype(f32).astype(np.float64)
    tb = np.zeros((P, TB_N), np.float64)
    tb[:, TB_COS:TB_COS + T] = np.concatenate([np.cos(ang), np.cos(ang)], 0)
    tb[:, TB_SIN:TB_SIN + T] = np.concatenate([np.sin(ang), -np.sin(ang)], 0)
    i = np.arange(P)
    scale = float(P) ** -0.5
    for h in range(HEADS):
        lg = np.log1p(-np.power(2.0, -5.0 - h))
        jj, ii = i[:, None], i[None, :]
        same = (ii // CHUNK) == (jj // CHUNK)
        decay = np.where(same, np.exp(lg * np.abs(ii - jj)),
                         np.where(ii > jj, np.exp(lg * np.maximum(ii - jj, 0)), 0.0))
        tb[:, TB_MASK + h * P:TB_MASK + (h + 1) * P] = decay * np.exp(-lg * (ii + 1.0)) * scale
        tb[:, TB_QDEC + h * P:TB_QDEC + (h + 1) * P] = np.exp(lg * (i + 1.0))[None, :]
        tb[:, TB_KDEC + h] = np.exp(lg * (P - 1.0 - i)) * scale
        tb[:DEC, TB_KDECS + h] = np.exp(lg * (DEC - 1.0 - i[:DEC])) * scale
        tb[:, TB_GT + h] = np.exp(lg * P)
        tb[:, TB_GS + h] = np.exp(lg * DEC)
    cn = np.zeros((P, CN_N), f32)
    cn[:, CN_ID:CN_ID + P] = np.eye(P)
    cn[:, CN_TRI:CN_TRI + P] = (i[:, None] < i[None, :])
    cn[:, CN_ONE:CN_ONE + P] = 1.0
    cn[:, CN_IOTA:CN_IOTA + P] = np.arange(P)[None, :]
    for t in range(NTILE):
        cn[:, CN_TOK + t] = t * P + i + 1
        for k in range(2):
            cn[:, CN_DST + k * NTILE + t] = 2 * (t * P + i) + k + 1
    return tb.astype(f32), cn


def wait_alone(eng, sem, value, passed):
    eng.wait_ge(sem, value)
    eng.sem_inc(passed, 1)


class Steps:

    def __init__(self, eng, sem, base=0):
        self.eng, self.sem, self.base, self.n = eng, sem, base, 0

    def did(self, ins):
        ins.then_inc(self.sem, 1)
        self.n += 1

    def wait(self):
        self.eng.wait_ge(self.sem, self.base + self.n)

    def link(self, ins):
        self.did(ins)
        self.wait()


class Mixer:

    def __init__(self, nc, ctx, R):
        self.nc, self.passed, self.spend = nc, R.passed, R.spend
        sb = lambda n, s, d=F32: ctx.enter_context(nc.sbuf_tensor(n, s, d))
        self.xn_hi = sb("xn_hi", [P, KD, T], F32R)
        self.xn_lo = sb("xn_lo", [P, KD, T], F32R)
        self.u = sb("u", [P, KD, T])
        self.w_raw = [sb(f"w_raw{s}", [P, KD, P]) for s in range(2)]
        self.w_hi = [sb(f"w_hi{s}", [P, KD, P], F32R) for s in range(2)]
        self.w_lo = [sb(f"w_lo{s}", [P, KD, P], F32R) for s in range(2)]

    def open(self, ctx, tag):
        nc = self.nc
        sem = lambda n: self.spend(ctx.enter_context(nc.semaphore(f"{tag}_{n}")))
        self.raw_in = [sem(f"raw_in{s}") for s in range(2)]
        self.hi_done = [sem(f"hi_done{s}") for s in range(2)]
        self.split_done = [sem(f"split_done{s}") for s in range(2)]
        self.tile_done = [sem(f"tile_done{s}") for s in range(2)]
        self.tile_free = [sem(f"tile_free{s}") for s in range(2)]


    def load(self, sp, s, turn, src):
        wait_alone(sp, self.split_done[s], turn, self.passed)
        sp.dma_start(self.w_raw[s][:], src.rearrange("(k p) n -> p k n", p=P)).then_inc(self.raw_in[s], 16)

    def split(self, pool, s, turn):
        pool.wait_ge(self.raw_in[s], turn * 16 + 16)
        wait_alone(pool, self.tile_done[s], turn * CT, self.passed)
        pool.tensor_copy(self.w_hi[s][:], self.w_raw[s][:]).then_inc(self.hi_done[s], 1)
        pool.wait_ge(self.hi_done[s], turn + 1)
        pool.tensor_tensor(self.w_lo[s][:], self.w_raw[s][:], self.w_hi[s][:].bitcast(F32),
                           ALU.subtract).then_inc(self.split_done[s], 1)

    def product(self, pe, s, turn, psum, x_hi, x_lo):
        pe.wait_ge(self.split_done[s], turn + 1)
        pe.wait_ge(self.tile_free[s], turn * CT)
        for c in range(CT):
            cols = slice(c * CW, (c + 1) * CW)
            out = psum[s][c][:, 0:CW]
            for k in range(KD):
                pe.matmul(out, self.w_hi[s][:, k, :], x_hi[:, k, cols], start=(k == 0), stop=False)
                pe.matmul(out, self.w_hi[s][:, k, :], x_lo[:, k, cols], start=False, stop=False)
                mm = pe.matmul(out, self.w_lo[s][:, k, :], x_hi[:, k, cols], start=False, stop=(k == KD - 1))
            mm.then_inc(self.tile_done[s], 1)

    def tile_ready(self, eng, s, turn, c):
        eng.wait_ge(self.tile_done[s], turn * CT + c + 1)

    def taken(self, eng, s, turn):
        eng.wait_ge(self.tile_free[s], turn * CT + CT)


def banks(nc, ctx, tag):
    return [[ctx.enter_context(nc.psum_tensor(f"{tag}_ps{s}{c}", [P, 512], F32)) for c in range(CT)]
            for s in range(2)]


def normalise(nc, A, R, M):
    with ExitStack() as ctx:
        sb = lambda n, s, d=F32: ctx.enter_context(nc.sbuf_tensor(n, s, d))
        sem = lambda n: R.spend(ctx.enter_context(nc.semaphore(n)))
        xt = [sb(f"x_tile{b}", [P, D]) for b in range(2)]
        gx = [sb(f"gx{b}", [P, KD, P]) for b in range(2)]
        junk = sb("square", [P, D])
        ss = sb("sum_sq", [P, 2])
        rms = sb("rms", [P, 2])
        rstd = sb("rstd", [P, 2])
        rows = sb("par_rows", [PR_N, P])
        sp_e = sb("sp_e", [P, 8])
        sp_s = sb("sp_s", [P, 8])
        sp_q = sb("sp_q", [P, 8])
        sp_a = sb("sp_a", [P, 8])
        pt = [[ctx.enter_context(nc.psum_tensor(f"pt{b}{n}", [P, 4, P], F32)) for n in range(2)] for b in range(2)]
        pp = ctx.enter_context(nc.psum_tensor("pp", [P, 512], F32))
        par_in = sem("par_in")
        const_in = sem("const_in")
        par_t = sem("par_t")
        par_done = sem("par_done")
        eps_done = sem("eps_done")
        x_in = [sem(f"x_in{b}") for b in range(2)]
        sq_done = sem("sq_done")
        rms_done = sem("rms_done")
        rstd_done = sem("rstd_done")
        scaled = sem("scaled")
        turned = [sem(f"turned{b}") for b in range(2)]
        gx_done = sem("gx_done")
        hi_done = sem("xn_hi_done")
        lo_done = sem("xn_lo_done")
        exp_done = sem("exp_done")
        abs_done = sem("abs_done")
        dve_step = sem("dve_step")

        def tile(t):
            return (P, ds(t * P, P)) if not isinstance(t, int) or t < NT else (DEC, slice(SEQ, T))

        def over_tiles(eng, body):
            with eng.Fori(0, NT // 2) as i:
                for b in range(2):
                    body(i * 2 + b, b, i)
            body(NT, 0, NT // 2)

        with nc.Block() as block:
            @block.sync
            def _(sp):
                sp.dma_start(R.const[:], A["const_small"]).then_inc(const_in, 16)
                vectors = [(PR_GMIX, "norm_mix_g"), (PR_CONVW, "conv_w"), (PR_CONVB, "conv_b"), (PR_BA, "lru_ba"),
                           (PR_BX, "lru_bx"), (PR_LAM, "lru_lambda"), (PR_GN, "ret_gn_g"), (PR_LRU, "state_lru"),
                           (PR_CACHE, "cache_conv")]
                for at, name in vectors:
                    src = A[name]
                    src = src[0, 0] if name == "cache_conv" else src[0]
                    src = (src.rearrange("j (n p) -> (j n) p", p=P) if name in ("conv_w", "cache_conv")
                           else src.rearrange("o (n p) -> (o n) p", p=P) if name == "state_lru"
                           else src.rearrange("(n p) -> n p", p=P))
                    sp.dma_start(rows[at:at + src.shape[0], :], src).then_inc(par_in, 16)

                def load(t, b, i):
                    n, _ = tile(t)
                    src = A["x_prompt"][0, ds(t * P, P), :] if n == P else A["x_sample"][0]
                    sp.wait_ge(turned[b], i)
                    sp.dma_start(xt[b][0:n, :], src).then_inc(x_in[b], 16)

                over_tiles(sp, load)

            @block.scalar
            def _(act):
                act.wait_ge(eps_done, 1)

                def body(t, b, i):
                    n, cols = tile(t)
                    act.wait_ge(x_in[b], 16 * i + 16)
                    act.activation(junk[0:n, :], xt[b][0:n, :], ACT.Square,
                                   accum_out=ss[0:n, b:b + 1]).then_inc(sq_done, 1)
                    act.wait_ge(sq_done, t + 1)
                    act.activation(rms[0:n, b:b + 1], ss[0:n, b:b + 1], ACT.Sqrt, bias=R.eps[0:n, :],
                                   scale=1.0 / D).then_inc(rms_done, 1)
                    act.wait_ge(gx_done, 2 * t + 2)
                    act.activation(M.xn_hi[:, :, cols], gx[b][:, :, 0:n], ACT.Copy).then_inc(hi_done, 1)

                over_tiles(act, body)
                act.wait_ge(abs_done, 1)
                act.activation(sp_e[:], sp_a[:], ACT.Exp, scale=-1.0).then_inc(exp_done, 1)

            @block.vector
            def _(dve):
                dve.memset(R.eps[:], EPS).then_inc(eps_done, 1)
                dve.memset(R.stage[:], 0.0)
                dve.wait_ge(par_t, 1)
                dve.tensor_copy(R.par[:], pp[:, 0:PR_N]).then_inc(par_done, 1)
                dve.wait_ge(par_done, 1)
                g_mix = R.par[:, PR_GMIX:PR_GMIX + KD]

                def body(t, b, i):
                    n, cols = tile(t)
                    dve.wait_ge(rms_done, t + 1)
                    dve.reciprocal(rstd[0:n, b:b + 1], rms[0:n, b:b + 1]).then_inc(rstd_done, 1)
                    dve.wait_ge(rstd_done, t + 1)
                    dve.tensor_scalar(xt[b][0:n, :], xt[b][0:n, :], rstd[0:n, b:b + 1], None,
                                      ALU.mult).then_inc(scaled, 1)
                    dve.wait_ge(turned[b], i + 1)
                    for m in range(2):
                        ins = dve.tensor_tensor(gx[b][:, 4 * m:4 * m + 4, 0:n], pt[b][m][:, :, 0:n],
                                                g_mix[:, 4 * m:4 * m + 4].unsqueeze(2).broadcast_to((P, 4, n)),
                                                ALU.mult)
                        ins.then_inc(gx_done, 1)
                    dve.wait_ge(hi_done, t + 1)
                    dve.tensor_tensor(M.xn_lo[:, :, cols], gx[b][:, :, 0:n], M.xn_hi[:, :, cols].bitcast(F32),
                                      ALU.subtract).then_inc(lo_done, 1)

                over_tiles(dve, body)
                dve.wait_ge(lo_done, NTILE)
                st = Steps(dve, dve_step)
                lam = R.par[:, PR_LAM:PR_LAM + 8]
                st.link(dve.tensor_scalar(sp_s[:], lam, -1.0, None, ALU.mult))
                dve.tensor_tensor(sp_a[:], sp_s[:], lam, ALU.max).then_inc(abs_done, 1)
                dve.wait_ge(exp_done, 1)
                st.link(dve.tensor_scalar(sp_q[:], sp_e[:], 2.0, None, ALU.add))
                st.link(dve.reciprocal(sp_q[:], sp_q[:]))
                st.link(dve.tensor_tensor(sp_e[:], sp_e[:], sp_q[:], ALU.mult))
                st.link(dve.tensor_tensor(sp_q[:], sp_e[:], sp_e[:], ALU.mult))
                st.link(dve.memset(sp_a[:], 1.0 / (2 * LOG_TERMS - 1)))
                for j in range(LOG_TERMS - 2, -1, -1):
                    st.link(dve.tensor_tensor(sp_a[:], sp_a[:], sp_q[:], ALU.mult))
                    st.link(dve.tensor_scalar(sp_a[:], sp_a[:], 1.0 / (2 * j + 1), None, ALU.add))
                st.link(dve.tensor_tensor(sp_a[:], sp_a[:], sp_e[:], ALU.mult))
                st.link(dve.tensor_scalar(sp_s[:], sp_s[:], 0.0, None, ALU.max))
                st.link(dve.scalar_tensor_tensor(out=sp_s[:], in0=sp_a[:], scalar=2.0, in1=sp_s[:],
                                                 op0=ALU.mult, op1=ALU.add))
                dve.tensor_scalar(R.lam_neg[:], sp_s[:], -8.0, None, ALU.mult)
                dve.tensor_scalar(R.lam_pos[:], sp_s[:], 8.0, None, ALU.mult)

            @block.tensor
            def _(pe):
                pe.wait_ge(const_in, 16)
                pe.wait_ge(par_in, 16 * 9)
                pe.transpose(pp[:, 0:PR_N], rows[:], R.ident[0:PR_N, 0:PR_N]).then_inc(par_t, 1)

                def body(t, b, i):
                    n, _ = tile(t)
                    pe.wait_ge(scaled, t + 1)
                    pe.wait_ge(gx_done, 4 * i)
                    for k in range(KD):
                        ins = pe.transpose(pt[b][k // 4][:, k % 4, 0:n], xt[b][0:n, k * P:(k + 1) * P],
                                           R.ident[0:n, 0:n])
                    ins.then_inc(turned[b], 1)

                over_tiles(pe, body)


def lru(nc, A, R, M):
    with ExitStack() as ctx:
        sb = lambda n, s, d=F32: ctx.enter_context(nc.sbuf_tensor(n, s, d))
        sem = lambda n: R.spend(ctx.enter_context(nc.semaphore(f"lru_{n}")))
        M.open(ctx, "lru")
        psum = banks(nc, ctx, "lru")
        pg = [ctx.enter_context(nc.psum_tensor(f"lru_pg{g}", [P, 512], F32)) for g in range(2)]
        xp = sb("conv_in", [P, XP])
        xc = sb("conv_out", [P, XC])
        gl = sb("gelu_gate", [P, T])
        r = sb("r_gate", [P, XC])
        ig = sb("i_gate", [P, XC])
        a = sb("decay_a", [P, XC])
        tl = sb("tanh_la", [P, XC])
        mu = sb("mult", [P, XC])
        hs = sb("hidden", [P, XC])
        wg = sb("w_gates", [P, 2, P])
        wg_in = sem("wg_in")
        conv_step = sem("conv_step")
        xc_done = sem("xc_done")
        gelu_out = sem("gelu_out")
        gate_done = sem("gate_done")
        gate_free = [sem(f"gate_free{g}") for g in range(2)]
        gates_out = sem("gates_out")
        a_out = sem("a_out")
        tl_out = sem("tl_out")
        m2_done = sem("m2_done")
        mult_out = sem("mult_out")
        chain = sem("chain")
        u_done = sem("u_done")
        xp_set = sem("xp_set")
        CG = XC // CT
        CONV_STEPS = 5
        CHAIN_STEPS = 8
        w_in = A["w_in"][0]

        with nc.Block() as block:
            @block.sync
            def _(sp):
                with sp.Fori(0, KD) as n:
                    M.load(sp, 0, n, w_in[:, ds(n * P, P)])
                    M.load(sp, 1, n, w_in[:, ds(n * P + D, P)])
                    wait_alone(sp, gate_done, n * (2 * CT), R.passed)
                    sp.dma_start(wg[:, 0, :], A["lru_wa"][0, ds(n, 1), :, :].rearrange("o c d -> (o c) d")).then_inc(wg_in, 16)
                    sp.dma_start(wg[:, 1, :], A["lru_wx"][0, ds(n, 1), :, :].rearrange("o c d -> (o c) d")).then_inc(wg_in, 16)

            @block.gpsimd
            def _(pool):
                with pool.Fori(0, KD) as n:
                    for s in range(2):
                        M.split(pool, s, n)

            @block.tensor
            def _(pe):
                with pe.Fori(0, KD) as n:
                    for s in range(2):
                        M.product(pe, s, n, psum, M.xn_hi, M.xn_lo)
                    pe.wait_ge(wg_in, n * 32 + 32)
                    pe.wait_ge(xc_done, n + 1)
                    for c in range(CT):
                        for g in range(2):
                            pe.wait_ge(gate_free[g], n * CT + c)
                            pe.matmul(pg[g][:, 0:CG], wg[:, g, :], xc[:, c * CG:(c + 1) * CG],
                                      start=True, stop=True).then_inc(gate_done, 1)

            @block.scalar
            def _(act):
                act.wait_ge(xp_set, 1)
                with act.Fori(0, KD) as n:
                    act.wait_ge(conv_step, n * CONV_STEPS)
                    act.activation(xp[:, PAD + SEQ:PAD + SEQ + PAD],
                                   R.par[:, PR_CACHE:PR_CACHE + 24].rearrange("p (j n) -> p j n", n=KD)[:, :, ds(n, 1)]
                                   .rearrange("p j o -> p (j o)"), ACT.Copy)
                    for c in range(CT):
                        M.tile_ready(act, 0, n, c)
                        lo, hi = c * CW, min((c + 1) * CW, SEQ)
                        ins = act.activation(xp[:, PAD + lo:PAD + hi], psum[0][c][:, 0:hi - lo], ACT.Copy)
                        if hi - lo < CW:
                            ins = act.activation(xp[:, PAD + S0:XP], psum[0][c][:, hi - lo:CW], ACT.Copy)
                        ins.then_inc(M.tile_free[0], 1)
                    act.wait_ge(u_done, n)
                    for c in range(CT):
                        M.tile_ready(act, 1, n, c)
                        act.activation(gl[:, c * CW:(c + 1) * CW], psum[1][c][:, 0:CW],
                                       ACT.Gelu_apprx_tanh).then_inc(M.tile_free[1], 1)
                    for c in range(CT):
                        for g, (dst, bias) in enumerate(((r, PR_BA), (ig, PR_BX))):
                            wait_alone(act, gate_done, n * (2 * CT) + 2 * c + g + 1, R.passed)
                            act.activation(dst[:, c * CG:(c + 1) * CG], pg[g][:, 0:CG], ACT.Sigmoid,
                                           bias=R.par[:, ds(n + bias, 1)]).then_inc(gate_free[g], 1)
                    act.wait_ge(gate_free[0], n * CT + CT)
                    act.activation(a[:], r[:], ACT.Exp, scale=R.lam_neg[:, ds(n, 1)]).then_inc(a_out, 1)
                    act.activation(tl[:], r[:], ACT.Tanh, scale=R.lam_pos[:, ds(n, 1)]).then_inc(tl_out, 1)
                    act.wait_ge(m2_done, n + 1)
                    act.activation(mu[:], mu[:], ACT.Sqrt).then_inc(mult_out, 1)

            @block.vector
            def _(dve):
                dve.memset(xp[:], 0.0).then_inc(xp_set, 1)
                with dve.Fori(0, KD) as n:
                    st = Steps(dve, conv_step, n * CONV_STEPS)
                    M.taken(dve, 0, n)
                    dve.wait_ge(gate_done, n * (2 * CT))
                    w = lambda j: R.par[:, ds(n + (PR_CONVW + KD * j), 1)]
                    st.link(dve.tensor_scalar(xc[:], xp[:, 0:XC], w(0), R.par[:, ds(n + PR_CONVB, 1)],
                                              ALU.mult, ALU.add))
                    for j in range(1, CONV):
                        ins = dve.scalar_tensor_tensor(out=xc[:], in0=xp[:, j:j + XC], scalar=w(j), in1=xc[:],
                                                       op0=ALU.mult, op1=ALU.add)
                        if j < CONV - 1:
                            st.link(ins)
                        else:
                            ins.then_inc(xc_done, 1)
                    stage = R.stage[:].rearrange("p (j n) -> p j n", n=KD)
                    st.did(dve.tensor_copy(stage[:, 0:3, ds(n, 1)], xp[:, SEQ:SEQ + PAD].unsqueeze(2)))
                    st.did(dve.tensor_copy(stage[:, 3:6, ds(n, 1)], xp[:, XP - PAD:XP].unsqueeze(2)))
                    ch = Steps(dve, chain, n * CHAIN_STEPS)
                    dve.wait_ge(a_out, n + 1)
                    dve.wait_ge(xc_done, n + 1)
                    dve.wait_ge(gate_free[1], n * CT + CT)
                    ch.did(dve.tensor_tensor(mu[:], a[:], a[:], ALU.mult))
                    ch.link(dve.tensor_tensor(ig[:], ig[:], xc[:], ALU.mult))
                    dve.wait_ge(tl_out, n + 1)
                    dve.scalar_tensor_tensor(out=mu[:], in0=mu[:], scalar=1.0, in1=tl[:],
                                             op0=ALU.add, op1=ALU.mult).then_inc(m2_done, 1)
                    dve.wait_ge(mult_out, n + 1)
                    ch.link(dve.memset(mu[:, 0:1], 1.0))
                    ch.link(dve.tensor_tensor(ig[:], ig[:], mu[:], ALU.mult))
                    ch.did(dve.tensor_tensor_scan(out=hs[:, 0:SEQ], data0=a[:, 0:SEQ], data1=ig[:, 0:SEQ],
                                                  initial=0.0, op0=ALU.mult, op1=ALU.add))
                    ch.link(dve.tensor_tensor_scan(out=hs[:, S0:XC], data0=a[:, S0:XC], data1=ig[:, S0:XC],
                                                   initial=R.par[:, ds(n + PR_LRU, 1)], op0=ALU.mult, op1=ALU.add))
                    ch.did(dve.tensor_copy(stage[:, 6:7, ds(n, 1)], hs[:, SEQ - 1:SEQ].unsqueeze(2)))
                    ch.did(dve.tensor_copy(stage[:, 7:8, ds(n, 1)], hs[:, XC - 1:XC].unsqueeze(2)))
                    M.taken(dve, 1, n)
                    dve.tensor_tensor(M.u[:, ds(n, 1), 0:SEQ].rearrange("p o t -> p (o t)"), gl[:, 0:SEQ],
                                      hs[:, 0:SEQ], ALU.mult)
                    dve.tensor_tensor(M.u[:, ds(n, 1), SEQ:T].rearrange("p o t -> p (o t)"), gl[:, SEQ:T],
                                      hs[:, S0:XC], ALU.mult).then_inc(u_done, 1)
                    dve.wait_ge(u_done, n + 1)


def merge(nc, A, R, M, tag, gate_col, w_out_name, src, dst):
    with ExitStack() as ctx:
        sb = lambda n, s, d=F32: ctx.enter_context(nc.sbuf_tensor(f"{tag}_{n}", s, d))
        sem = lambda n: ctx.enter_context(nc.semaphore(f"{tag}_{n}"))
        M.open(ctx, tag)
        psum = banks(nc, ctx, tag)
        u_hi = sb("u_hi", [P, KD, T], F32R)
        u_lo = sb("u_lo", [P, KD, T], F32R)
        sg = sb("sig_gate", [P, T])
        m = sb("merged", [P, T])
        old = sb("old", [P, T]) if src is not None else None
        u_hi_done = sem("u_hi_done")
        u_split = sem("u_split")
        m_done = sem("m_done")
        m_stored = sem("m_stored")
        old_in = sem("old_in")
        w_gate = A["w_in"][0][:, gate_col * D:(gate_col + 1) * D]
        w_out = A[w_out_name][0]

        with nc.Block() as block:
            @block.sync
            def _(sp):
                def loads(j):
                    M.load(sp, 0, j, w_gate[:, ds(j * P, P)])
                    M.load(sp, 1, j, w_out[:, ds(j * P, P)])

                def load_old(j):
                    if src is not None:
                        sp.dma_start(old[:], src[ds(j, 1)].rearrange("o p t -> (o p) t")).then_inc(old_in, 16)

                def store(j):
                    sp.wait_ge(m_done, j * CT + CT)
                    sp.dma_start(dst[ds(j, 1)].rearrange("o p t -> (o p) t"), m[:]).then_inc(m_stored, 16)

                loads(0)
                load_old(0)
                with sp.Fori(0, KD - 1) as j:
                    loads(j + 1)
                    store(j)
                    load_old(j + 1)
                store(KD - 1)
                sp.wait_ge(m_stored, 16 * KD)

            @block.gpsimd
            def _(pool):
                with pool.Fori(0, KD) as j:
                    for s in range(2):
                        M.split(pool, s, j)

            @block.tensor
            def _(pe):
                with pe.Fori(0, KD) as j:
                    M.product(pe, 0, j, psum, M.xn_hi, M.xn_lo)
                    pe.wait_ge(u_split, KD)
                    M.product(pe, 1, j, psum, u_hi, u_lo)

            @block.scalar
            def _(act):
                with act.Fori(0, KD) as k:
                    act.activation(u_hi[:, ds(k, 1), :], M.u[:, ds(k, 1), :], ACT.Copy).then_inc(u_hi_done, 1)
                with act.Fori(0, KD) as j:
                    act.wait_ge(m_done, j * CT)
                    for c in range(CT):
                        M.tile_ready(act, 0, j, c)
                        act.activation(sg[:, c * CW:(c + 1) * CW], psum[0][c][:, 0:CW],
                                       ACT.Sigmoid).then_inc(M.tile_free[0], 1)

            @block.vector
            def _(dve):
                with dve.Fori(0, KD) as k:
                    dve.wait_ge(u_hi_done, k + 1)
                    dve.tensor_tensor(u_lo[:, ds(k, 1), :], M.u[:, ds(k, 1), :], u_hi[:, ds(k, 1), :].bitcast(F32),
                                      ALU.subtract).then_inc(u_split, 1)
                with dve.Fori(0, KD) as j:
                    dve.wait_ge(m_stored, j * 16)
                    for c in range(CT):
                        cols = slice(c * CW, (c + 1) * CW)
                        dve.wait_ge(M.tile_free[0], j * CT + c + 1)
                        M.tile_ready(dve, 1, j, c)
                        dve.tensor_tensor(m[:, cols], psum[1][c][:, 0:CW], sg[:, cols],
                                          ALU.mult).then_inc(M.tile_free[1], 1)
                        dve.wait_ge(M.tile_free[1], j * CT + c + 1)
                        if src is None:
                            dve.sem_inc(m_done, 1)
                            continue
                        if c == 0:
                            dve.wait_ge(old_in, j * 16 + 16)
                        dve.tensor_tensor(m[:, cols], m[:, cols], old[:, cols], ALU.add).then_inc(m_done, 1)


class Turns:

    ORDER = ("o", "vt", "ot", "kt", "sc", "kv")

    def __init__(self, nc, ctx, passed):
        self.passed = passed
        self.bank = [ctx.enter_context(nc.psum_tensor(f"ret_turn{b}", [P, 4, P], F32)) for b in range(2)]
        self.free = [ctx.enter_context(nc.semaphore(f"ret_turn_free{b}")) for b in range(2)]
        self.done = {s: ctx.enter_context(nc.semaphore(f"ret_{s}_done")) for s in self.ORDER}

    def at(self, kind, h, stage, c):
        have = {"first": ("vt", "kt", "sc", "kv"), "loop": self.ORDER, "last": ("o", "ot")}
        places = lambda k: [(s, x, (3 * self.ORDER.index(s) + x) % 2) for s in self.ORDER if s in have[k]
                            for x in range(3)]
        mine = places(kind)
        n = next(i for i, (s, x, _) in enumerate(mine) if (s, x) == (stage, c))
        bank = mine[n][2]
        before = sum(b == bank for _, _, b in mine[:n])
        if kind != "first":
            before += sum(b == bank for _, _, b in places("first"))
            before = (h - 1) * sum(b == bank for _, _, b in places("loop")) + before
        return bank, before

    def claim(self, pe, kind, h, stage, c):
        b, before = self.at(kind, h, stage, c)
        wait_alone(pe, self.free[b], before, self.passed)
        return self.bank[b]

    def ready(self, eng, kind, h, head, stage, c):
        wait_alone(eng, self.done[stage], head * 3 + c + 1, self.passed)
        b, _ = self.at(kind, h, stage, c)
        return self.bank[b], self.free[b]

    def taken(self, eng, kind, h, stage):
        for c in (1, 2):
            b, before = self.at(kind, h, stage, c)
            wait_alone(eng, self.free[b], before + 1, self.passed)


def tiles_of(c):
    return range(4 * c, 4 * c + 4) if c < 2 else [NT]


def retention(nc, A, R, M, out_prompt, out_sample):
    with ExitStack() as ctx:
        sb = lambda n, s, d=F32: ctx.enter_context(nc.sbuf_tensor(f"ret_{n}", s, d))
        sem = lambda n: ctx.enter_context(nc.semaphore(f"ret_{n}"))
        M.open(ctx, "ret")
        psum = banks(nc, ctx, "ret")
        turns = Turns(nc, ctx, R.passed)
        tb = sb("tables", [P, TB_N])
        s_in = sb("state_in", [P, HEADS, P])
        v_f = sb("v_features", [P, T])
        k_f = sb("k_features", [P, T])
        q_f = sb("q_features", [P, T])
        half = sb("rotary_half", [P, T])
        srg = sb("silu_gate", [P, T])
        v_t = sb("v_tokens", [P, NTILE, P])
        k_t = sb("k_tokens", [P, NTILE, P])
        pt = sb("scores", [P, NTILE, P])
        on = sb("out_tokens", [P, NTILE, P])
        state = sb("states", [P, NTILE, P])
        bst = sb("bn_parts", [P, NTILE, 6])
        mv = sb("mean_var", [P, NTILE, 2])
        sd = sb("deviation", [P, NTILE])
        table_in = sem("table_in")
        init = sem("init")
        k_rot = sem("k_rotated")
        q_rot = sem("q_rotated")
        rope_step = sem("rope_step")
        stats_step = sem("stats_step")
        state_step = sem("state_step")
        centred = sem("centred")
        sd_out = sem("sd_out")
        on_done = sem("on_done")
        u_done = sem("u_done")
        stored = sem("state_stored")
        w_in = A["w_in"][0]
        STATE_STEPS = NT + 1
        STATS_STEPS = 2 * NTILE + 1
        ROPE_STEPS = 7
        cols = lambda t: slice(t * P, (t + 1) * P) if t < NT else slice(SEQ, T)
        rows = lambda t: P if t < NT else DEC
        one = lambda ap: ap.rearrange("p o t -> p (o t)")

        with nc.Block() as block:
            @block.sync
            def _(sp):
                sp.dma_start(tb[:], A["const_tables"]).then_inc(table_in, 16)
                sp.dma_start(s_in[:], A["state_ret"][0, 0].rearrange("h d e -> d h e")).then_inc(table_in, 16)

                def loads(h):
                    for n, col in enumerate((4, 3, 2, 5)):
                        M.load(sp, n % 2, h * 2 + n // 2, w_in[:, ds(h * P + col * D, P)])

                def store(h):
                    sp.wait_ge(state_step, h * STATE_STEPS + STATE_STEPS)
                    sp.dma_start(out_prompt[ds(h, 1)].rearrange("o d e -> (o d) e"), state[:, NT, :]).then_inc(stored, 16)
                    sp.dma_start(out_sample[ds(h, 1)].rearrange("o d e -> (o d) e"), state[:, 0, :]).then_inc(stored, 16)

                loads(0)
                with sp.Fori(0, HEADS - 1) as h:
                    loads(h + 1)
                    store(h)
                store(HEADS - 1)
                sp.wait_ge(stored, 32 * HEADS)

            @block.gpsimd
            def _(pool):
                with pool.Fori(0, HEADS) as h:
                    for n in range(4):
                        M.split(pool, n % 2, h * 2 + n // 2)

            @block.tensor
            def _(pe):
                def turn_to(kind, step, stage, src, out_free):
                    for c in range(3):
                        bank = turns.claim(pe, kind, step, stage, c)
                        for t in tiles_of(c):
                            n = rows(t)
                            if out_free:
                                ins = pe.transpose(bank[0:n, t % 4, :], src[:, cols(t)], R.ident[:])
                            else:
                                ins = pe.transpose(bank[:, t % 4, 0:n], src[0:n, t, :], R.ident[0:n, 0:n])
                        ins.then_inc(turns.done[stage], 1)

                def outputs(kind, step, head):
                    for c in range(3):
                        bank = turns.claim(pe, kind, step, "o", c)
                        for t in tiles_of(c):
                            n = rows(t)
                            out = bank[0:n, t % 4, :]
                            ins = pe.matmul(out, pt[0:n, t, 0:n], v_t[0:n, t, :], start=True, stop=(t == 0))
                            if 0 < t < NT:
                                ins = pe.matmul(out, q_f[:, cols(t)], state[:, t, :], start=False, stop=True)
                            if t == NT:
                                ins = pe.matmul(out, q_f[:, cols(t)], one(s_in[:, ds(head, 1), :]),
                                                start=False, stop=True)
                        ins.then_inc(turns.done["o"], 1)

                def out_turned(kind, step, head):
                    pe.wait_ge(on_done, head + 1)
                    turn_to(kind, step, "ot", on, False)

                def step_of(kind, h):
                    M.product(pe, 0, h * 2, psum, M.xn_hi, M.xn_lo)
                    if kind == "loop":
                        pe.wait_ge(state_step, h * STATE_STEPS)
                        outputs(kind, h, h - 1)
                    M.product(pe, 1, h * 2, psum, M.xn_hi, M.xn_lo)
                    M.taken(pe, 0, h * 2)
                    turn_to(kind, h, "vt", v_f, True)
                    if kind == "loop":
                        out_turned(kind, h, h - 1)
                    M.product(pe, 0, h * 2 + 1, psum, M.xn_hi, M.xn_lo)
                    pe.wait_ge(k_rot, h + 1)
                    turn_to(kind, h, "kt", k_f, True)
                    M.product(pe, 1, h * 2 + 1, psum, M.xn_hi, M.xn_lo)
                    pe.wait_ge(q_rot, h + 1)
                    for c in range(3):
                        bank = turns.claim(pe, kind, h, "sc", c)
                        for t in tiles_of(c):
                            n = rows(t)
                            ins = pe.matmul(bank[0:n, t % 4, 0:n], k_f[:, cols(t)], q_f[:, cols(t)],
                                            start=True, stop=True)
                        ins.then_inc(turns.done["sc"], 1)
                    turns.taken(pe, kind, h, "vt")
                    turns.taken(pe, kind, h, "kt")
                    for c in range(3):
                        bank = turns.claim(pe, kind, h, "kv", c)
                        for t in tiles_of(c):
                            n = rows(t)
                            ins = pe.matmul(bank[:, t % 4, :], k_t[0:n, t, :], v_t[0:n, t, :], start=True, stop=True)
                        ins.then_inc(turns.done["kv"], 1)

                pe.wait_ge(table_in, 32)
                step_of("first", 0)
                with pe.Fori(1, HEADS) as h:
                    step_of("loop", h)
                pe.wait_ge(state_step, HEADS * STATE_STEPS)
                outputs("last", HEADS, HEADS - 1)
                out_turned("last", HEADS, HEADS - 1)

            @block.scalar
            def _(act):
                def take(s, turn, dst, func):
                    for c in range(CT):
                        M.tile_ready(act, s, turn, c)
                        act.activation(dst[:, c * CW:(c + 1) * CW], psum[s][c][:, 0:CW], func).then_inc(M.tile_free[s], 1)

                def deviation(head):
                    act.wait_ge(centred, (head + 1) * NTILE)
                    act.activation(sd[:], mv[:, :, 1:2].rearrange("p t o -> p (t o)"), ACT.Sqrt,
                                   bias=R.eps[:]).then_inc(sd_out, 1)

                def step_of(kind, h):
                    act.wait_ge(turns.done["vt"], h * 3)
                    take(0, h * 2, v_f, ACT.Copy)
                    if kind == "loop":
                        deviation(h - 1)
                    act.wait_ge(turns.done["sc"], h * 3)
                    take(1, h * 2, k_f, ACT.Copy)
                    act.wait_ge(turns.done["o"], h * 3)
                    for c in range(3):
                        bank, free = turns.ready(act, kind, h, h, "vt", c)
                        ts = tiles_of(c)
                        n = rows(ts[0])
                        act.activation(v_t[0:n, ts[0]:ts[-1] + 1, :], bank[0:n, 0:len(ts), :], ACT.Copy).then_inc(free, 1)
                    take(0, h * 2 + 1, q_f, ACT.Copy)
                    act.wait_ge(turns.done["kv"], h * 3)
                    for c in range(3):
                        bank, free = turns.ready(act, kind, h, h, "kt", c)
                        ts = tiles_of(c)
                        n = rows(ts[0])
                        dec = tb[0:n, ds(h + (TB_KDEC if c < 2 else TB_KDECS), 1)]
                        act.activation(k_t[0:n, ts[0]:ts[-1] + 1, :], bank[0:n, 0:len(ts), :], ACT.Copy,
                                       scale=dec).then_inc(free, 1)
                    act.wait_ge(u_done, h * 3)
                    take(1, h * 2 + 1, srg, ACT.Silu)

                act.wait_ge(init, 1)
                act.wait_ge(table_in, 32)
                step_of("first", 0)
                with act.Fori(1, HEADS) as h:
                    step_of("loop", h)
                deviation(HEADS - 1)

            @block.vector
            def _(dve):
                def centre(kind, step, head):
                    st = Steps(dve, stats_step, head * STATS_STEPS)
                    dve.wait_ge(turns.done["ot"], head * 3)
                    for c in range(3):
                        bank, free = turns.ready(dve, kind, step, head, "o", c)
                        for t in tiles_of(c):
                            n = rows(t)
                            st.did(dve.bn_stats(bst[0:n, t, :], bank[0:n, t % 4, :]))
                        wait_alone(dve, stats_step, st.base + st.n, R.passed)
                        for t in tiles_of(c):
                            n = rows(t)
                            st.did(dve.bn_aggr(mv[0:n, t, :], bst[0:n, t, :]))
                        st.wait()
                        for t in tiles_of(c):
                            n = rows(t)
                            dve.tensor_scalar(on[0:n, t, :], bank[0:n, t % 4, :], mv[0:n, t, 0:1], None,
                                              ALU.subtract).then_inc(centred, 1)
                        dve.wait_ge(centred, head * NTILE + tiles_of(c)[-1] + 1)
                        dve.sem_inc(free, 1)
                    dve.wait_ge(sd_out, head + 1)
                    st.link(dve.reciprocal(sd[:], sd[:]))
                    dve.tensor_tensor(on[:], on[:], sd[:].unsqueeze(2).broadcast_to((P, NTILE, P)),
                                      ALU.mult).then_inc(on_done, 1)

                def gated(kind, step, head):
                    M.taken(dve, 1, head * 2 + 1)
                    for c in range(3):
                        bank, free = turns.ready(dve, kind, step, head, "ot", c)
                        lo, hi = cols(tiles_of(c)[0]).start, cols(tiles_of(c)[-1]).stop
                        dve.scalar_tensor_tensor(
                            out=one(M.u[:, ds(head, 1), lo:hi]),
                            in0=bank[:].rearrange("p a b -> p (a b)")[:, 0:hi - lo],
                            scalar=R.par[:, ds(head + PR_GN, 1)], in1=srg[:, lo:hi],
                            op0=ALU.mult, op1=ALU.mult).then_inc(u_done, 1)
                        dve.wait_ge(u_done, head * 3 + c + 1)
                        dve.sem_inc(free, 1)

                def rotate(st, x, s, turn, done):
                    M.taken(dve, s, turn)
                    st.did(dve.tensor_tensor(half[64:128, :], x[0:64, :], tb[0:64, TB_SIN:TB_SIN + T], ALU.mult))
                    st.link(dve.tensor_tensor(half[0:64, :], x[64:128, :], tb[64:128, TB_SIN:TB_SIN + T], ALU.mult))
                    st.link(dve.tensor_tensor(x[:], x[:], tb[:, TB_COS:TB_COS + T], ALU.mult))
                    ins = dve.tensor_tensor(x[:], x[:], half[:], ALU.add)
                    ins.then_inc(done, 1)

                def step_of(kind, h):
                    st = Steps(dve, rope_step, h * ROPE_STEPS)
                    if kind == "loop":
                        centre(kind, h, h - 1)
                    rotate(st, k_f, 1, h * 2, k_rot)
                    if kind == "loop":
                        gated(kind, h, h - 1)
                    dve.wait_ge(k_rot, h + 1)
                    M.taken(dve, 0, h * 2 + 1)
                    st.did(dve.tensor_tensor(half[64:128, :], q_f[0:64, :], tb[0:64, TB_SIN:TB_SIN + T], ALU.mult))
                    st.link(dve.tensor_tensor(half[0:64, :], q_f[64:128, :], tb[64:128, TB_SIN:TB_SIN + T], ALU.mult))
                    st.link(dve.tensor_tensor(q_f[:], q_f[:], tb[:, TB_COS:TB_COS + T], ALU.mult))
                    st.link(dve.tensor_tensor(q_f[:], q_f[:], half[:], ALU.add))
                    qd = tb[:, ds(h * P + TB_QDEC, P)]
                    dve.tensor_tensor(q_f[:, 0:SEQ].rearrange("p (a b) -> p a b", b=P),
                                      q_f[:, 0:SEQ].rearrange("p (a b) -> p a b", b=P),
                                      qd.unsqueeze(1).broadcast_to((P, NT, P)), ALU.mult)
                    dve.tensor_tensor(q_f[:, SEQ:T], q_f[:, SEQ:T], tb[:, ds(h * P + TB_QDEC, DEC)],
                                      ALU.mult).then_inc(q_rot, 1)
                    dve.wait_ge(turns.done["o"], h * 3)
                    for c in range(3):
                        bank, free = turns.ready(dve, kind, h, h, "sc", c)
                        ts = tiles_of(c)
                        n = rows(ts[0])
                        mask = tb[0:n, ds(h * P + TB_MASK, n)]
                        dve.tensor_tensor(pt[0:n, ts[0]:ts[-1] + 1, 0:n], bank[0:n, 0:len(ts), 0:n],
                                          mask.unsqueeze(1).broadcast_to((n, len(ts), n)), ALU.mult).then_inc(free, 1)
                    dve.wait_ge(stored, h * 32)
                    ss = Steps(dve, state_step, h * STATE_STEPS)
                    for c in range(3):
                        bank, free = turns.ready(dve, kind, h, h, "kv", c)
                        for t in tiles_of(c):
                            if t == 0:
                                ss.link(dve.tensor_copy(state[:, 1, :], bank[:, 0, :]))
                            elif t < NT:
                                ss.link(dve.scalar_tensor_tensor(
                                    out=state[:, t + 1, :], in0=state[:, t, :], scalar=tb[:, ds(h + TB_GT, 1)],
                                    in1=bank[:, t % 4, :], op0=ALU.mult, op1=ALU.add))
                            else:
                                ss.link(dve.scalar_tensor_tensor(
                                    out=state[:, 0, :], in0=one(s_in[:, ds(h, 1), :]), scalar=tb[:, ds(h + TB_GS, 1)],
                                    in1=bank[:, 0, :], op0=ALU.mult, op1=ALU.add))
                        dve.sem_inc(free, 1)

                dve.memset(mv[:], 1.0)
                dve.memset(on[:], 0.0).then_inc(init, 1)
                dve.wait_ge(init, 1)
                dve.wait_ge(table_in, 32)
                step_of("first", 0)
                with dve.Fori(1, HEADS) as h:
                    step_of("loop", h)
                centre("last", HEADS, HEADS - 1)
                gated("last", HEADS, HEADS - 1)


def tile_at(x, t, n):
    return x[0:n, ds(t, 1), :].rearrange("p o d -> p (o d)")


def out_proj(nc, A, R, H, merged, xf_rows):
    with ExitStack() as ctx:
        sb = lambda n, s, d=F32: ctx.enter_context(nc.sbuf_tensor(f"op_{n}", s, d))
        sem = lambda n: ctx.enter_context(nc.semaphore(f"op_{n}"))
        ps = lambda n, s: ctx.enter_context(nc.psum_tensor(f"op_{n}", s, F32))
        RAW = 3
        w_raw = [sb(f"w_raw{b}", [P, D]) for b in range(RAW)]
        w_hi = sb("w_hi", [P, KD, D], F32R)
        w_lo = sb("w_lo", [P, KD, D], F32R)
        m_raw = [sb(f"m_raw{b}", [P, KD, P]) for b in range(2)]
        m_hi = [sb(f"m_hi{b}", [P, KD, P], F32R) for b in range(2)]
        m_lo = [sb(f"m_lo{b}", [P, KD, P], F32R) for b in range(2)]
        xt = [sb(f"x_tile{b}", [P, D]) for b in range(2)]
        xf_t = sb("xf_turned", [P, KD, P])
        xf = [sb(f"xf{b}", [P, D]) for b in range(2)]
        w_rt = sb("w_router", [P, KD, ROUT])
        ss = sb("sum_sq", [P, 1])
        po = [ps(f"out{n}", [P, 512]) for n in range(2)]
        pt = [ps(f"turned{n}", [P, 4, P]) for n in range(2)]
        pl = ps("logits", [P, ROUT])
        w_in = [sem(f"w_in{b}") for b in range(RAW)]
        w_hi_done, w_lo_done = sem("w_hi_done"), sem("w_lo_done")
        m_in = [sem(f"m_in{b}") for b in range(2)]
        m_hi_done, m_lo_done = sem("m_hi_done"), sem("m_lo_done")
        x_in = [sem(f"x_in{b}") for b in range(2)]
        rt_in = sem("rt_in")
        out_done = [sem(f"out_done{n}") for n in range(2)]
        h_done = [sem(f"h_done{n}") for n in range(2)]
        sq_done, rms_done = sem("sq_done"), sem("rms_done")
        rstd_done = sem("rstd_done")
        xf_done = sem("xf_done")
        xf_stored = [sem(f"xf_stored{b}") for b in range(2)]
        turned = sem("turned")
        xf_t_done = sem("xf_t_done")
        logit_done = sem("logit_done")
        logit_out = sem("logit_out")
        init = sem("init")
        N2 = D // 512

        def over_tiles(eng, body):
            for b in range(2):
                body(b, b, 0, P)
            with eng.Fori(1, NT // 2) as i:
                for b in range(2):
                    body(i * 2 + b, b, i, P)
            body(NT, 0, NT // 2, DEC)

        def two_ahead(eng, split, norm, weights):
            split(0, 0, 0, P)
            weights()
            split(1, 1, 0, P)
            for b in range(2):
                norm(b, b, 0, P, lambda: split(b + 2, b, 1, P))
            with eng.Fori(1, NT // 2 - 1) as i:
                for b in range(2):
                    norm(i * 2 + b, b, i, P, lambda: split(i * 2 + b + 2, b, i + 1, P))
            norm(NT - 2, 0, NT // 2 - 1, P, lambda: split(NT, 0, NT // 2, DEC))
            norm(NT - 1, 1, NT // 2 - 1, P, lambda: None)
            norm(NT, 0, NT // 2, DEC, lambda: None)

        def first(t):
            return isinstance(t, int) and t < 2

        with nc.Block() as block:
            @block.sync
            def _(sp):
                m_view = merged.rearrange("k p t -> p k t")

                def load(t, b, i, n):
                    at = ds(t * P, P) if n == P else slice(SEQ, T)
                    if not first(t):
                        sp.wait_ge(m_lo_done, t - 1)
                        sp.dma_start(m_raw[b][:, :, 0:n], m_view[:, :, at]).then_inc(m_in[b], 16)
                        sp.wait_ge(h_done[1], t - 1)
                    src = A["x_prompt"][0, at, :] if n == P else A["x_sample"][0]
                    sp.dma_start(xt[b][0:n, :], src).then_inc(x_in[b], 16)

                for s in R.spent:
                    sp.sem_clear(s)
                sp.dma_start(m_raw[0][:], m_view[:, :, 0:P]).then_inc(m_in[0], 16)
                for k in range(KD):
                    if k >= RAW:
                        sp.wait_ge(w_lo_done, k - RAW + 1)
                    sp.dma_start(w_raw[k % RAW][:], A["w_out"][0][k * P:(k + 1) * P, :]).then_inc(w_in[k % RAW], 16)
                sp.dma_start(m_raw[1][:], m_view[:, :, P:2 * P]).then_inc(m_in[1], 16)
                over_tiles(sp, load)
                for b in range(2):
                    sp.wait_ge(xf_stored[b], 16 * len(range(b, NTILE, 2)))

            @block.gpsimd
            def _(pool):
                for name, at, n in (("w_router_group", 0, GROUPS), ("w_router_expert", GROUPS, E)):
                    pool.dma_start(w_rt[:, :, at:at + n], A[name][0].rearrange("(k p) n -> p k n", p=P)).then_inc(rt_in, 16)
                pool.dma_start(H.bias[:, 0:GROUPS], A["b_router_group"][0].partition_broadcast(P)).then_inc(rt_in, 16)
                pool.dma_start(H.bias[:, GROUPS:ROUT], A["b_router_expert"][0].partition_broadcast(P)).then_inc(rt_in, 16)
                pool.dma_start(H.g_ffn[:], A["norm_ffn_g"][0].partition_broadcast(P)).then_inc(rt_in, 16)
                pool.wait_ge(rt_in, 80)

                def keep(t, b, i, n):
                    pool.wait_ge(xf_done, t + 1)
                    pool.dma_start(xf_rows[ds(t * P, n), :], xf[b][0:n, :]).then_inc(xf_stored[b], 16)

                over_tiles(pool, keep)

            @block.tensor
            def _(pe):
                def project(t, b, i, n):
                    pe.wait_ge(m_lo_done, t + 1)
                    for half in range(N2):
                        if not isinstance(t, int) or t > 0:
                            pe.wait_ge(h_done[half], t)
                        out = po[half][0:n, :]
                        at = slice(half * 512, half * 512 + 512)
                        for k in range(KD):
                            if isinstance(t, int) and t == 0:
                                pe.wait_ge(w_lo_done, k + 1)
                            pe.matmul(out, m_hi[b][:, k, 0:n], w_hi[:, k, at], start=(k == 0), stop=False)
                            pe.matmul(out, m_hi[b][:, k, 0:n], w_lo[:, k, at], start=False, stop=False)
                            mm = pe.matmul(out, m_lo[b][:, k, 0:n], w_hi[:, k, at], start=False, stop=(k == KD - 1))
                        mm.then_inc(out_done[half], 1)

                def route(t, b, i, n):
                    pe.wait_ge(xf_done, t + 1)
                    pe.wait_ge(xf_t_done, t * 2)
                    for k in range(KD):
                        ins = pe.transpose(pt[k // 4][:, k % 4, 0:n], xf[b][0:n, k * P:(k + 1) * P],
                                           R.ident[0:n, 0:n])
                        if k % 4 == 3:
                            ins.then_inc(turned, 1)
                    pe.wait_ge(xf_t_done, t * 2 + 2)
                    pe.wait_ge(logit_out, t)
                    for k in range(KD):
                        mm = pe.matmul(pl[0:n, :], xf_t[:, k, 0:n], w_rt[:, k, :], start=(k == 0), stop=(k == KD - 1))
                    mm.then_inc(logit_done, 1)

                project(0, 0, 0, P)
                pe.wait_ge(rt_in, 80)
                with pe.Fori(0, NT // 2 - 1) as i:
                    project(i * 2 + 1, 1, i, P)
                    route(i * 2, 0, i, P)
                    project(i * 2 + 2, 0, i + 1, P)
                    route(i * 2 + 1, 1, i, P)
                project(NT - 1, 1, NT // 2 - 1, P)
                route(NT - 2, 0, NT // 2 - 1, P)
                project(NT, 0, NT // 2, DEC)
                route(NT - 1, 1, NT // 2 - 1, P)
                route(NT, 0, NT // 2, DEC)

            @block.scalar
            def _(act):
                def split(t, b, i, n):
                    act.wait_ge(m_in[b], i * 16 + 16)
                    if not first(t):
                        act.wait_ge(out_done[1], t - 1)
                    act.activation(m_hi[b][:, :, 0:n], m_raw[b][:, :, 0:n], ACT.Copy).then_inc(m_hi_done, 1)

                def norm(t, b, i, n, next_split):
                    act.wait_ge(h_done[1], t + 1)
                    if not first(t):
                        act.wait_ge(turned, t * 2 - 2)
                        act.wait_ge(xf_stored[b], i * 16)
                    act.activation(xf[b][0:n, :], tile_at(H.h, t, n), ACT.Square,
                                   accum_out=ss[0:n, :]).then_inc(sq_done, 1)
                    act.wait_ge(sq_done, t + 1)
                    act.activation(H.rms[0:n, ds(t, 1)], ss[0:n, :], ACT.Sqrt, bias=R.eps[0:n, :],
                                   scale=1.0 / D).then_inc(rms_done, 1)
                    next_split()
                    act.wait_ge(logit_done, t)
                    for m in range(2):
                        act.wait_ge(turned, t * 2 + m + 1)
                        act.activation(xf_t[:, 4 * m:4 * m + 4, 0:n], pt[m][:, :, 0:n], ACT.Copy).then_inc(xf_t_done, 1)
                    act.wait_ge(logit_done, t + 1)
                    act.activation(tile_at(H.logits, t, n), pl[0:n, :], ACT.Copy).then_inc(logit_out, 1)

                def weights():
                    for k in range(KD):
                        act.wait_ge(w_in[k % RAW], 16 * (k // RAW) + 16)
                        act.activation(w_hi[:, k, :], w_raw[k % RAW][:], ACT.Copy).then_inc(w_hi_done, 1)
                    act.wait_ge(init, 1)

                two_ahead(act, split, norm, weights)

            @block.vector
            def _(dve):
                def split(t, b, i, n):
                    dve.wait_ge(m_hi_done, t + 1)
                    dve.tensor_tensor(m_lo[b][:, :, 0:n], m_raw[b][:, :, 0:n], m_hi[b][:, :, 0:n].bitcast(F32),
                                      ALU.subtract).then_inc(m_lo_done, 1)

                def norm(t, b, i, n, next_split):
                    dve.wait_ge(x_in[b], i * 16 + 16)
                    for half in range(N2):
                        at = slice(half * 512, half * 512 + 512)
                        dve.wait_ge(out_done[half], t + 1)
                        dve.tensor_tensor(tile_at(H.h, t, n)[:, at], po[half][0:n, :], xt[b][0:n, at],
                                          ALU.add).then_inc(h_done[half], 1)
                    next_split()
                    dve.wait_ge(rms_done, t + 1)
                    dve.reciprocal(H.rstd[0:n, ds(t, 1)], H.rms[0:n, ds(t, 1)]).then_inc(rstd_done, 1)
                    dve.wait_ge(rstd_done, t + 1)
                    dve.scalar_tensor_tensor(out=xf[b][0:n, :], in0=tile_at(H.h, t, n),
                                             scalar=H.rstd[0:n, ds(t, 1)], in1=H.g_ffn[0:n, :],
                                             op0=ALU.mult, op1=ALU.mult).then_inc(xf_done, 1)

                def weights():
                    for k in range(KD):
                        dve.wait_ge(w_hi_done, k + 1)
                        dve.tensor_tensor(w_lo[:, k, :], w_raw[k % RAW][:], w_hi[:, k, :].bitcast(F32),
                                          ALU.subtract).then_inc(w_lo_done, 1)
                    dve.wait_ge(rt_in, 80)

                dve.memset(H.logits[:], 0.0).then_inc(init, 1)
                two_ahead(dve, split, norm, weights)


class Router:

    def __init__(self, nc, ctx, R, H):
        sb = lambda n, s, d=F32: ctx.enter_context(nc.sbuf_tensor(f"rt_{n}", s, d))
        sem = lambda n: ctx.enter_context(nc.semaphore(f"rt_{n}"))
        self.slots_done = sem("slots_done")
        g_max, g_sum, g_idx, g_top = (sb(n, [P, NTILE]) for n in ("g_max", "g_sum", "g_idx", "g_top"))
        g_key = sb("g_key", [P, NTILE, GROUPS])
        g_exp = sb("g_exp", [P, NTILE, GROUPS])
        g_hot = sb("g_hot", [P, NTILE, GROUPS])
        picked = sb("picked", [P, NTILE, GROUPS, PER_GROUP])
        sel = sb("sel", [P, NTILE, PER_GROUP])
        key = sb("key", [P, NTILE, PER_GROUP])
        hot8 = sb("hot8", [P, NTILE, PER_GROUP])
        v = [sb(f"v{k}", [P, NTILE]) for k in range(2)]
        eid = [sb(f"eid{k}", [P, NTILE]) for k in range(2)]
        ratio, den = sb("ratio", [P, NTILE]), sb("den", [P, NTILE])
        w = [sb(f"w{k}", [P, NTILE]) for k in range(2)]
        hot = [sb(f"hot{k}", [P, NTILE, E]) for k in range(2)]
        took = sb("took", [P, NTILE, E])
        before = sb("before", [P, NTILE + 1, E])
        tmp = sb("tmp", [P, NTILE, E])
        rank = [sb(f"rank{k}", [P, NTILE]) for k in range(2)]
        fits = [sb(f"fits{k}", [P, NTILE]) for k in range(2)]
        in_slot = [sb(f"in_slot{k}", [P, NTILE, SLOTS]) for k in range(2)]
        ids = [sb(f"ids{k}", [P, NTILE, 2, E]) for k in range(2)]
        slot_f, slot_none = sb("slot_f", [P, 2, E]), sb("slot_none", [P, 2, E])
        over = sb("over", [1, E])
        over_n = sb("over_n", [1, E])
        over_x = sb("over_x", [1, E, E])
        ones = sb("ones", [1, E])
        over_f = sb("over_f", [1, E + 1])
        bank = ctx.enter_context(nc.psum_tensor("rt_bank", [P, (NTILE + 3) * E], F32))
        pr = bank[:, 0:(NTILE + 1) * E]
        pm = bank[:, (NTILE + 1) * E:].rearrange("p (a e) -> p a e", a=2)
        step = sem("step")
        g_in = sem("g_in")
        d_in = sem("d_in")
        exp_out = sem("exp_out")
        took_done = sem("took_done")
        rank_done = sem("rank_done")
        in_slot_done = sem("in_slot_done")
        slots_turned = sem("slots_turned")
        wide = lambda ap, n: ap[:].unsqueeze(2).broadcast_to((P, NTILE, n))
        iota = lambda n: R.const[:, CN_IOTA:CN_IOTA + n].unsqueeze(1).broadcast_to((P, NTILE, n))

        def vector(dve):
            st = Steps(dve, step)

            def first_index(x, top, k_buf, out, n):
                st.link(dve.tensor_tensor(k_buf[:], x, wide(top, n), ALU.is_lt))
                st.link(dve.scalar_tensor_tensor(out=k_buf[:], in0=k_buf[:], scalar=64.0, in1=iota(n),
                                                 op0=ALU.mult, op1=ALU.add))
                st.link(dve.tensor_reduce(out[:], k_buf[:], AX.X, ALU.min))

            st.link(dve.tensor_tensor(H.logits[:], H.logits[:],
                                      H.bias[:].unsqueeze(1).broadcast_to((P, NTILE, ROUT)), ALU.add))
            g = H.logits[:, :, 0:GROUPS]
            st.link(dve.tensor_reduce(g_max[:], g, AX.X, ALU.max))
            dve.tensor_tensor(g_exp[:], g, wide(g_max, GROUPS), ALU.subtract).then_inc(g_in, 1)
            first_index(g, g_max, g_key, g_idx, GROUPS)
            st.link(dve.tensor_tensor(g_hot[:], iota(GROUPS), wide(g_idx, GROUPS), ALU.is_equal))
            e4 = H.logits[:, :, GROUPS:ROUT].rearrange("p t (g j) -> p t g j", g=GROUPS)
            st.link(dve.tensor_tensor(picked[:], e4,
                                      g_hot[:].unsqueeze(3).broadcast_to((P, NTILE, GROUPS, PER_GROUP)), ALU.mult))
            st.link(dve.tensor_reduce(sel[:], picked[:].rearrange("p t g j -> p t j g"), AX.X, ALU.add))
            for k in range(2):
                st.link(dve.tensor_reduce(v[k][:], sel[:], AX.X, ALU.max))
                first_index(sel[:], v[k], key, eid[k], PER_GROUP)
                if k == 0:
                    st.link(dve.tensor_tensor(hot8[:], iota(PER_GROUP), wide(eid[0], PER_GROUP), ALU.is_equal))
                    st.link(dve.scalar_tensor_tensor(out=sel[:], in0=hot8[:], scalar=-BIG, in1=sel[:],
                                                     op0=ALU.mult, op1=ALU.add))
                st.link(dve.scalar_tensor_tensor(out=eid[k][:], in0=g_idx[:], scalar=float(PER_GROUP), in1=eid[k][:],
                                                 op0=ALU.mult, op1=ALU.add))
                st.link(dve.tensor_tensor(hot[k][:], iota(E), wide(eid[k], E), ALU.is_equal))
            dve.tensor_tensor(ratio[:], v[1][:], v[0][:], ALU.subtract).then_inc(d_in, 1)
            st.link(dve.tensor_tensor(took[:], hot[0][:], hot[1][:], ALU.add))
            for q in range(DEC, P, 32):
                st.did(dve.memset(took[q:q + 32, NT, :], 0.0))
            st.link(dve.memset(before[:, 0, :], 0.0))
            for t in range(NTILE):
                st.link(dve.tensor_tensor(before[:, t + 1, :], before[:, t, :], took[:, t, :], ALU.add))
            dve.sem_inc(took_done, 1)
            dve.wait_ge(exp_out, 1)
            st.link(dve.tensor_reduce(g_sum[:], g_exp[:], AX.X, ALU.add))
            st.link(dve.reciprocal(g_top[:], g_sum[:]))
            dve.wait_ge(exp_out, 2)
            st.link(dve.tensor_scalar(den[:], ratio[:], 1.0, None, ALU.add))
            st.link(dve.reciprocal(den[:], den[:]))
            st.link(dve.tensor_tensor(w[0][:], g_top[:], den[:], ALU.mult))
            st.link(dve.tensor_tensor(w[1][:], w[0][:], ratio[:], ALU.mult))
            for k in range(2):
                st.did(dve.tensor_tensor(ids[k][:, :, 0, :], hot[k][:], R.const[:, CN_TOK:CN_TOK + NTILE]
                                         .unsqueeze(2).broadcast_to((P, NTILE, E)), ALU.mult))
                st.link(dve.tensor_tensor(ids[k][:, :, 1, :], hot[k][:],
                                          R.const[:, CN_DST + k * NTILE:CN_DST + (k + 1) * NTILE]
                                          .unsqueeze(2).broadcast_to((P, NTILE, E)), ALU.mult))
            dve.wait_ge(rank_done, 1)
            st.did(dve.tensor_scalar(over[:], pr[0:1, NTILE * E:], float(SLOTS), None, ALU.is_gt))
            ranks = pr[:, 0:NTILE * E].rearrange("p (t e) -> p t e", e=E)
            for k in range(2):
                st.link(dve.tensor_tensor(tmp[:], ranks, hot[k][:], ALU.mult))
                st.link(dve.tensor_reduce(rank[k][:], tmp[:], AX.X, ALU.add))
            for k in range(2):
                dve.tensor_tensor(in_slot[k][:], R.const[:, CN_IOTA:CN_IOTA + SLOTS].unsqueeze(1)
                                  .broadcast_to((P, NTILE, SLOTS)), wide(rank[k], SLOTS),
                                  ALU.is_equal).then_inc(in_slot_done, 1)
            dve.wait_ge(slots_turned, 1)
            st.did(dve.tensor_scalar(slot_none[:], pm[:], 0.5, NOWHERE, ALU.is_lt, ALU.mult))
            st.link(dve.tensor_copy(slot_f[:], pm[:]))
            st.link(dve.scalar_tensor_tensor(out=slot_f[:], in0=slot_f[:], scalar=-1.0, in1=slot_none[:],
                                             op0=ALU.add, op1=ALU.add))
            dve.tensor_copy(H.slots[:], slot_f[:]).then_inc(self.slots_done, 1)
            for k in range(2):
                st.link(dve.tensor_scalar(fits[k][:], rank[k][:], float(SLOTS), None, ALU.is_lt))
                st.link(dve.tensor_tensor(H.w[k][:], w[k][:], fits[k][:], ALU.mult))
                st.link(dve.tensor_tensor(w[k][:], w[k][:], H.w[k][:], ALU.subtract))
                st.link(dve.tensor_tensor(hot[k][:], hot[k][:], wide(w[k], E), ALU.mult))
                st.link(dve.scalar_tensor_tensor(out=fits[k][:], in0=fits[k][:], scalar=NOWHERE,
                                                 in1=R.const[:, CN_DST + k * NTILE:CN_DST + (k + 1) * NTILE],
                                                 op0=ALU.mult, op1=ALU.add))
                st.link(dve.tensor_scalar(fits[k][:], fits[k][:], -1.0, None, ALU.add))
                st.link(dve.tensor_copy(H.unfilled[k][:], fits[k][:]))
            st.link(dve.tensor_tensor(H.w_over[:], hot[0][:], hot[1][:], ALU.add))
            st.link(dve.memset(ones[:], 1.0))
            st.link(dve.tensor_tensor_scan(out=over_n[:], data0=ones[:], data1=over[:], initial=0.0,
                                           op0=ALU.mult, op1=ALU.add))
            st.link(dve.tensor_copy(over_f[:, E:E + 1], over_n[:, E - 1:E]))
            st.link(dve.tensor_tensor(over_n[:], over_n[:], over[:], ALU.mult))
            st.link(dve.tensor_scalar(ones[:], R.const[0:1, CN_IOTA:CN_IOTA + E], 1.0, None, ALU.add))
            st.link(dve.tensor_tensor(over_x[:], over_n[:].unsqueeze(1).broadcast_to((1, E, E)),
                                      ones[:].unsqueeze(2).broadcast_to((1, E, E)), ALU.is_equal))
            st.link(dve.tensor_tensor(over_x[:], over_x[:],
                                      R.const[0:1, CN_IOTA:CN_IOTA + E].unsqueeze(1).broadcast_to((1, E, E)),
                                      ALU.mult))
            st.link(dve.tensor_reduce(over_f[:, 0:E], over_x[:], AX.X, ALU.add))
            st.link(dve.tensor_copy(H.over[:], over_f[:]))

        def scalar(act):
            act.wait_ge(g_in, 1)
            act.activation(g_exp[:], g_exp[:], ACT.Exp).then_inc(exp_out, 1)
            act.wait_ge(d_in, 1)
            act.activation(ratio[:], ratio[:], ACT.Exp).then_inc(exp_out, 1)

        def tensor(pe):
            pe.wait_ge(took_done, 1)
            pe.matmul(pr[:, :], R.const[:, CN_ONE:CN_ONE + P], before[:].rearrange("p t e -> p (t e)"),
                      start=True, stop=False)
            pe.matmul(pr[:, 0:NTILE * E], R.const[:, CN_TRI:CN_TRI + P], took[:].rearrange("p t e -> p (t e)"),
                      start=False, stop=True).then_inc(rank_done, 1)
            for k in range(2):
                pe.wait_ge(in_slot_done, k + 1)
                for t in range(NTILE):
                    n = P if t < NT else DEC
                    mm = pe.matmul(pm[:].rearrange("p a e -> p (a e)"), in_slot[k][0:n, t, :],
                                   ids[k][0:n, t, :, :].rearrange("p a e -> p (a e)"),
                                   start=(k == 0 and t == 0), stop=(k == 1 and t == NT))
            mm.then_inc(slots_turned, 1)

        self.vector, self.scalar, self.tensor = vector, scalar, tensor


class Chunks:

    def __init__(self, kind, step):
        self.kind, self.step = kind, step

    def order(self, c):
        return {"first": lambda: c, "last": lambda: 6 * E - 6 + c}.get(self.kind, lambda: self.step * 6 + (c - 2))()

    def slot(self, c):
        return c % 3 if self.kind in ("loop", "end") else (c + 2) % 3

    def turn(self, c):
        return self.step if c < 4 else self.step - 1


def experts(nc, A, R, H, xf_rows, y_rows):
    with ExitStack() as ctx:
        sb = lambda n, s, d=F32: ctx.enter_context(nc.sbuf_tensor(f"ex_{n}", s, d))
        sem = lambda n: ctx.enter_context(nc.semaphore(f"ex_{n}"))
        ps = lambda n, s: ctx.enter_context(nc.psum_tensor(f"ex_{n}", s, F32))
        CHUNK_W = 4 * FE
        raw = [sb(f"raw{c}", [P, CHUNK_W]) for c in range(6)]
        w_hi = [sb(f"w_hi{c}", [P, CHUNK_W], F32R) for c in range(3)]
        w_lo = [sb(f"w_lo{c}", [P, CHUNK_W], F32R) for c in range(3)]
        xe = sb("rows", [P, D])
        row_in, row_out = sb("row_in", [P, 1], U32), sb("row_out", [P, 1], U32)
        x_hi, x_lo = sb("x_hi", [P, KD, P], F32R), sb("x_lo", [P, KD, P], F32R)
        sil, hid = sb("silu", [P, FE]), sb("hidden", [P, FE])
        h_hi, h_lo = sb("h_hi", [P, KF, P], F32R), sb("h_lo", [P, KF, P], F32R)
        y = sb("y", [P, D])
        pg, pu, ph = ps("gate", [P, FE]), ps("up", [P, FE]), ps("h_turned", [P, KF, P])
        px = [ps(f"x_turned{m}", [P, 4, P]) for m in range(2)]
        py = [ps(f"y{m}", [P, 512]) for m in range(2)]
        raw_in = [sem(f"raw_in{c}") for c in range(6)]
        raw_free = [sem(f"raw_free{c}") for c in range(6)]
        hi_done, lo_done = sem("hi_done"), sem("lo_done")
        used = sem("used")
        xe_in = sem("xe_in")
        x_turned, x_hi_done, x_lo_done = sem("x_turned"), sem("x_hi_done"), sem("x_lo_done")
        silu_done, hid_done = sem("silu_done"), sem("hid_done")
        h_turned, h_hi_done, h_lo_done = sem("h_turned"), sem("h_hi_done"), sem("h_lo_done")
        y_done, y_stored = sem("y_done"), sem("y_stored")
        xe_set, rows_set = sem("xe_set"), sem("rows_set")
        N2 = D // 512
        router = Router(nc, ctx, R, H)

        def source(c, e):
            name = ("w_exp_gate", "w_exp_up", "w_exp_down")[c // 2]
            rows_ = (KD if c < 4 else KF) // 2 * P
            m = A[name][0, ds(e, 1)].rearrange("o r n -> (o r) n")
            return m[(c % 2) * rows_:(c % 2 + 1) * rows_, :].rearrange("(k p) n -> p k n", p=P)

        def in_steps(eng, body):
            body("first", 0)
            with eng.Fori(1, E - 1) as s:
                body("loop", s)
            body("end", E - 1)
            body("last", E)

        with nc.Block() as block:
            @block.sync
            def _(sp):
                def body(kind, s):
                    ch = Chunks(kind, s)
                    for c in {"first": range(4), "last": range(4, 6)}.get(kind, range(6)):
                        e = s if c < 4 else s - 1
                        sp.wait_ge(raw_free[c], ch.turn(c))
                        k = 4 if c < 4 else 2
                        sp.dma_start(raw[c][:].rearrange("p (k n) -> p k n", k=k), source(c, e)).then_inc(raw_in[c], 16)

                in_steps(sp, body)

            @block.gpsimd
            def _(pool):
                def load(e, moved):
                    if not (isinstance(e, int) and e == 0):
                        wait_alone(pool, x_turned, e * 2, R.passed)
                    pool.tensor_copy(row_in[:], H.slots[:, 0, ds(e, 1)]).then_inc(rows_set, 1)
                    wait_alone(pool, rows_set, moved + 1, R.passed)
                    pool.indirect_dma_start(
                        out=xe[:], out_offset=None, in_=xf_rows, in_offset=bass.IndirectOffsetOnAxis(ap=row_in[:], axis=0),
                        bounds_check=T - 1, oob_is_err=False).then_inc(xe_in, 16)

                def store(e, moved):
                    if not (isinstance(e, int) and e == 0):
                        wait_alone(pool, y_stored, e * 16, R.passed)
                    pool.tensor_copy(row_out[:], H.slots[:, 1, ds(e, 1)]).then_inc(rows_set, 1)
                    wait_alone(pool, y_done, e * N2 + N2, R.passed)
                    wait_alone(pool, rows_set, moved + 1, R.passed)
                    pool.indirect_dma_start(
                        out=y_rows, out_offset=bass.IndirectOffsetOnAxis(ap=row_out[:], axis=0), in_=y[:], in_offset=None,
                        bounds_check=2 * T - 1, oob_is_err=False).then_inc(y_stored, 16)

                def body(kind, s):
                    if kind in ("first", "loop"):
                        load(s + 1, 2 * s + 1 - (kind != "first"))
                    if kind != "first":
                        store(s - 1, 2 * s + (kind == "loop") - (kind == "last"))

                pool.memset(xe[:], 0.0).then_inc(xe_set, 1)
                pool.wait_ge(xe_set, 1)
                pool.wait_ge(router.slots_done, 1)
                load(0, 0)
                in_steps(pool, body)
                pool.wait_ge(y_stored, 16 * E)

            @block.tensor
            def _(pe):
                def three(out, a_hi, a_lo, b_hi, b_lo, first, last):
                    pe.matmul(out, a_hi, b_hi, start=first, stop=False)
                    pe.matmul(out, a_hi, b_lo, start=False, stop=False)
                    return pe.matmul(out, a_lo, b_hi, start=False, stop=last)

                def turn_x(e):
                    pe.wait_ge(xe_in, e * 16 + 16)
                    pe.wait_ge(x_lo_done, e * 2)
                    for k in range(KD):
                        ins = pe.transpose(px[k // 4][:, k % 4, :], xe[:, k * P:(k + 1) * P], R.ident[:])
                        if k % 4 == 3:
                            ins.then_inc(x_turned, 1)

                def up_or_gate(ch, out, cs):
                    for i, c in enumerate(cs):
                        pe.wait_ge(lo_done, ch.order(c) + 1)
                        hi = w_hi[ch.slot(c)][:].rearrange("p (k n) -> p k n", k=4)
                        lo = w_lo[ch.slot(c)][:].rearrange("p (k n) -> p k n", k=4)
                        for k in range(4):
                            kk = 4 * i + k
                            ins = three(out[:], x_hi[:, kk, :], x_lo[:, kk, :], hi[:, k, :], lo[:, k, :],
                                        kk == 0, kk == KD - 1)
                        ins.then_inc(used, 1)

                def body(kind, s):
                    ch = Chunks(kind, s)
                    if kind != "last":
                        pe.wait_ge(x_lo_done, s * 2 + 2)
                        pe.wait_ge(silu_done, s)
                        up_or_gate(ch, pg, (0, 1))
                    if kind != "first":
                        pe.wait_ge(hid_done, s)
                        pe.wait_ge(h_lo_done, s - 1)
                        for k in range(KF):
                            ins = pe.transpose(ph[:, k, :], hid[:, k * P:(k + 1) * P], R.ident[:])
                        ins.then_inc(h_turned, 1)
                    if kind != "last":
                        pe.wait_ge(hid_done, s)
                        up_or_gate(ch, pu, (2, 3))
                    if kind in ("first", "loop"):
                        turn_x(s + 1)
                    if kind != "first":
                        pe.wait_ge(h_lo_done, s)
                        pe.wait_ge(y_done, s * N2 - N2)
                        for i, c in enumerate((4, 5)):
                            pe.wait_ge(lo_done, ch.order(c) + 1)
                            hi = w_hi[ch.slot(c)][:].rearrange("p (k n) -> p k n", k=2)
                            lo = w_lo[ch.slot(c)][:].rearrange("p (k n) -> p k n", k=2)
                            for k in range(2):
                                kk = 2 * i + k
                                for m in range(N2):
                                    at = slice(m * 512, m * 512 + 512)
                                    ins = three(py[m][:], h_hi[:, kk, :], h_lo[:, kk, :], hi[:, k, at], lo[:, k, at],
                                                kk == 0, kk == KF - 1)
                            ins.then_inc(used, 1)

                router.tensor(pe)
                turn_x(0)
                in_steps(pe, body)

            def splitting(eng, part, x_part, h_part, mid, end):
                def ahead(kind, s):
                    for c in (0, 1, 2):
                        part(Chunks(kind, s), c)
                        if c == 0:
                            x_part(s)

                def body(kind, s):
                    ch = Chunks(kind, s)
                    if kind != "last":
                        part(ch, 3)
                    if kind != "first":
                        h_part(s - 1)
                        part(ch, 4)
                        if kind == "last":
                            part(ch, 5)
                    if kind != "last":
                        mid(ch, s)
                        if kind != "first":
                            part(ch, 5)
                    if kind in ("first", "loop"):
                        ahead("loop" if kind == "first" else kind, s + 1)
                    if kind != "first":
                        end(ch, s - 1)

                ahead("first", 0)
                in_steps(eng, body)

            @block.scalar
            def _(act):
                def part(ch, c):
                    act.wait_ge(raw_in[c], ch.turn(c) * 16 + 16)
                    if not (ch.kind == "first" and c < 3):
                        act.wait_ge(used, ch.order(c) - 2)
                    act.activation(w_hi[ch.slot(c)][:], raw[c][:], ACT.Copy).then_inc(hi_done, 1)

                def x_part(e):
                    for m in range(2):
                        act.wait_ge(x_turned, e * 2 + m + 1)
                        act.activation(x_hi[:, 4 * m:4 * m + 4, :], px[m][:], ACT.Copy).then_inc(x_hi_done, 1)

                def h_part(e):
                    act.wait_ge(h_turned, e + 1)
                    act.activation(h_hi[:], ph[:], ACT.Copy).then_inc(h_hi_done, 1)

                def silu(ch, e):
                    act.wait_ge(used, ch.order(1) + 1)
                    act.wait_ge(hid_done, e)
                    act.activation(sil[:], pg[:], ACT.Silu).then_inc(silu_done, 1)

                router.scalar(act)
                splitting(act, part, x_part, h_part, silu, lambda ch, e: None)

            @block.vector
            def _(dve):
                def part(ch, c):
                    dve.wait_ge(hi_done, ch.order(c) + 1)
                    s = ch.slot(c)
                    dve.tensor_tensor(w_lo[s][:], raw[c][:], w_hi[s][:].bitcast(F32), ALU.subtract).then_inc(lo_done, 1)
                    dve.wait_ge(lo_done, ch.order(c) + 1)
                    dve.sem_inc(raw_free[c], 1)

                def x_part(e):
                    for m in range(2):
                        dve.wait_ge(x_hi_done, e * 2 + m + 1)
                        dve.tensor_tensor(x_lo[:, 4 * m:4 * m + 4, :], px[m][:],
                                          x_hi[:, 4 * m:4 * m + 4, :].bitcast(F32), ALU.subtract).then_inc(x_lo_done, 1)

                def h_part(e):
                    dve.wait_ge(h_hi_done, e + 1)
                    dve.tensor_tensor(h_lo[:], ph[:], h_hi[:].bitcast(F32), ALU.subtract).then_inc(h_lo_done, 1)

                def hidden(ch, e):
                    dve.wait_ge(silu_done, e + 1)
                    dve.wait_ge(used, ch.order(3) + 1)
                    dve.wait_ge(h_turned, e)
                    dve.tensor_tensor(hid[:], sil[:], pu[:], ALU.mult).then_inc(hid_done, 1)

                def out(ch, e):
                    dve.wait_ge(used, ch.order(5) + 1)
                    dve.wait_ge(y_stored, e * 16)
                    for m in range(N2):
                        dve.tensor_copy(y[:, m * 512:m * 512 + 512], py[m][:]).then_inc(y_done, 1)

                router.vector(dve)
                splitting(dve, part, x_part, h_part, hidden, out)


def overflow(nc, A, R, H, xf_rows, y_rows):
    with ExitStack() as ctx:
        sb = lambda n, s, d=F32: ctx.enter_context(nc.sbuf_tensor(f"ov_{n}", s, d))
        sem = lambda n: ctx.enter_context(nc.semaphore(f"ov_{n}"))
        ps = lambda n, s: ctx.enter_context(nc.psum_tensor(f"ov_{n}", s, F32))
        wg, wu, wd = sb("w_gate", [P, KD, FE]), sb("w_up", [P, KD, FE]), sb("w_down", [P, KF, D])
        xt, x_t = sb("rows", [P, D]), sb("rows_t", [P, KD, P])
        sil, hid, hid_t = sb("silu", [P, FE]), sb("hidden", [P, FE]), sb("hidden_t", [P, KF, P])
        px = [ps(f"x_turned{m}", [P, 4, P]) for m in range(2)]
        pg, pu, ph = ps("gate", [P, FE]), ps("up", [P, FE]), ps("h_turned", [P, KF, P])
        py = [ps(f"y{m}", [P, 512]) for m in range(2)]
        w_in, x_in = sem("w_in"), sem("x_in")
        x_turned, x_out = sem("x_turned"), sem("x_out")
        gu_done, silu_done, hid_done = sem("gu_done"), sem("silu_done"), sem("hid_done")
        h_turned, h_out, y_done, added = sem("h_turned"), sem("h_out"), sem("y_done"), sem("added")
        none, none_set, none_out = sb("none", [P, D]), sem("none_set"), sem("none_out")
        w_now, w_copied = sb("w_now", [P, 1]), sem("w_copied")

        def listed(eng, i):
            return eng.value_load(H.over[0:1, ds(i, 1)], min_val=0, max_val=E - 1)

        def over_experts(eng, each):
            n_over = eng.value_load(H.over[0:1, E:E + 1], min_val=0, max_val=E)
            with eng.If(n_over > 0):
                with eng.Fori(0, n_over) as i:
                    each(i)
            eng.nop()

        def over_tiles(eng, i, body):
            with eng.Fori(0, NT) as t:
                body(t, i * NTILE + t, P)
            body(NT, i * NTILE + NT, DEC)

        with nc.Block() as block:
            @block.sync
            def _(sp):
                def each(i):
                    e = listed(sp, i)
                    sp.wait_ge(added, i * (2 * NTILE))
                    for dst, name in ((wg, "w_exp_gate"), (wu, "w_exp_up"), (wd, "w_exp_down")):
                        src = A[name][0, ds(e, 1)].rearrange("o (k p) n -> p (o k) n", p=P)
                        sp.dma_start(dst[:], src).then_inc(w_in, 16)

                    def body(t, g, n):
                        sp.wait_ge(x_turned, g * 2)
                        sp.dma_start(xt[0:n, :], xf_rows[ds(t * P, n), :]).then_inc(x_in, 16)

                    over_tiles(sp, i, body)

                over_experts(sp, each)

            @block.gpsimd
            def _(pool):
                n_over = pool.value_load(H.over[0:1, E:E + 1], min_val=0, max_val=E)
                with pool.If(n_over > 0):
                    pool.memset(none[:], 0.0).then_inc(none_set, 1)
                    pool.wait_ge(none_set, 1)
                    for t in range(NTILE):
                        n = P if t < NT else DEC
                        for k in range(2):
                            pool.indirect_dma_start(
                                out=y_rows, in_=none[0:n, :], in_offset=None, bounds_check=2 * T - 1, oob_is_err=False,
                                out_offset=bass.IndirectOffsetOnAxis(ap=H.unfilled[k][0:n, t:t + 1], axis=0),
                                ).then_inc(none_out, 16)
                    pool.wait_ge(none_out, 2 * NTILE * 16)
                pool.nop()

            @block.tensor
            def _(pe):
                def each(i):
                    wait_alone(pe, w_in, i * 48 + 48, R.passed)

                    def body(t, g, n):
                        pe.wait_ge(x_in, g * 16 + 16)
                        wait_alone(pe, x_out, g * 2, R.passed)
                        for k in range(KD):
                            ins = pe.transpose(px[k // 4][:, k % 4, 0:n], xt[0:n, k * P:(k + 1) * P], R.ident[0:n, 0:n])
                            if k % 4 == 3:
                                ins.then_inc(x_turned, 1)
                        pe.wait_ge(x_out, g * 2 + 2)
                        pe.wait_ge(hid_done, g)
                        for out, w in ((pg, wg), (pu, wu)):
                            for k in range(KD):
                                ins = pe.matmul(out[0:n, :], x_t[:, k, 0:n], w[:, k, :], start=(k == 0), stop=(k == KD - 1))
                            ins.then_inc(gu_done, 1)
                        pe.wait_ge(h_out, g)
                        wait_alone(pe, hid_done, g + 1, R.passed)
                        for k in range(KF):
                            ins = pe.transpose(ph[:, k, 0:n], hid[0:n, k * P:(k + 1) * P], R.ident[0:n, 0:n])
                        ins.then_inc(h_turned, 1)
                        pe.wait_ge(h_out, g + 1)
                        pe.wait_ge(added, g * 2)
                        for m in range(2):
                            for k in range(KF):
                                ins = pe.matmul(py[m][0:n, :], hid_t[:, k, 0:n], wd[:, k, m * 512:m * 512 + 512],
                                                start=(k == 0), stop=(k == KF - 1))
                            ins.then_inc(y_done, 1)

                    over_tiles(pe, i, body)

                over_experts(pe, each)

            @block.scalar
            def _(act):
                def each(i):
                    def body(t, g, n):
                        act.wait_ge(gu_done, g * 2)
                        for m in range(2):
                            act.wait_ge(x_turned, g * 2 + m + 1)
                            act.activation(x_t[:, 4 * m:4 * m + 4, 0:n], px[m][:, :, 0:n], ACT.Copy).then_inc(x_out, 1)
                        act.wait_ge(gu_done, g * 2 + 1)
                        act.wait_ge(hid_done, g)
                        act.activation(sil[0:n, :], pg[0:n, :], ACT.Silu).then_inc(silu_done, 1)
                        act.wait_ge(h_turned, g + 1)
                        act.wait_ge(y_done, g * 2)
                        act.activation(hid_t[:, :, 0:n], ph[:, :, 0:n], ACT.Copy).then_inc(h_out, 1)

                    over_tiles(act, i, body)

                over_experts(act, each)

            @block.vector
            def _(dve):
                def each(i):
                    e = listed(dve, i)

                    def body(t, g, n):
                        dve.wait_ge(silu_done, g + 1)
                        dve.wait_ge(gu_done, g * 2 + 2)
                        dve.wait_ge(h_turned, g)
                        dve.tensor_tensor(hid[0:n, :], sil[0:n, :], pu[0:n, :], ALU.mult).then_inc(hid_done, 1)
                        wait_alone(dve, added, g * 2, R.passed)
                        dve.tensor_copy(w_now[0:n, :], H.w_over[0:n, ds(t, 1), ds(e, 1)].rearrange("p a b -> p (a b)")
                                        ).then_inc(w_copied, 1)
                        dve.wait_ge(w_copied, g + 1)
                        h_t = tile_at(H.h, t, n)
                        for m in range(2):
                            at = slice(m * 512, m * 512 + 512)
                            dve.wait_ge(y_done, g * 2 + m + 1)
                            dve.scalar_tensor_tensor(out=h_t[:, at], in0=py[m][0:n, :], scalar=w_now[0:n, :],
                                                     in1=h_t[:, at], op0=ALU.mult, op1=ALU.add).then_inc(added, 1)

                    over_tiles(dve, i, body)

                over_experts(dve, each)


def combine(nc, A, R, H, y_rows, outs):
    with ExitStack() as ctx:
        sb = lambda n, s, d=F32: ctx.enter_context(nc.sbuf_tensor(f"co_{n}", s, d))
        sem = lambda n: ctx.enter_context(nc.semaphore(f"co_{n}"))
        RING = 3
        yb = [sb(f"y{b}", [P, 2, D]) for b in range(RING)]
        out = [sb(f"out{b}", [P, D]) for b in range(2)]
        g_fin = sb("g_final", [P, D])
        ss, rms, rstd = (sb(n, [P, NTILE]) for n in ("sum_sq", "rms", "rstd"))
        small = sb("small", [ST_N, P])
        pst = ctx.enter_context(nc.psum_tensor("co_stage", [P, 512], F32))
        g_in = sem("g_in")
        y_in = [sem(f"y_in{b}") for b in range(RING)]
        mixed, sq_done, rms_done = sem("mixed"), sem("sq_done"), sem("rms_done")
        rstd_done, out_done = sem("rstd_done"), sem("out_done")
        stored = [sem(f"stored{b}") for b in range(2)]
        st_turned, st_out, st_stored = sem("st_turned"), sem("st_out"), sem("st_stored")
        n_rows = lambda t: P if t < NT else DEC
        y_prompt, y_sample, conv_p, lru_p, conv_s, lru_s = outs

        with nc.Block() as block:
            @block.gpsimd
            def _(pool):
                for t in range(NTILE):
                    b, n = t % RING, n_rows(t)
                    if t >= RING:
                        pool.wait_ge(mixed, 2 * (t - RING + 1))
                    src = y_rows[2 * t * P:2 * (t * P + n), :].rearrange("(n k) d -> n (k d)", k=2)
                    pool.dma_start(yb[b][0:n].rearrange("n k d -> n (k d)"), src).then_inc(y_in[b], 16)

            @block.vector
            def _(dve):
                def finish(t):
                    b, n = t % 2, n_rows(t)
                    dve.wait_ge(rms_done, t + 1)
                    dve.reciprocal(rstd[0:n, t:t + 1], rms[0:n, t:t + 1]).then_inc(rstd_done, 1)
                    dve.wait_ge(rstd_done, t + 1)
                    if t >= 2:
                        dve.wait_ge(stored[b], 16 * (t // 2))
                    dve.scalar_tensor_tensor(out=out[b][0:n, :], in0=H.h[0:n, t, :], scalar=rstd[0:n, t:t + 1],
                                             in1=g_fin[0:n, :], op0=ALU.mult, op1=ALU.mult).then_inc(out_done, 1)

                dve.wait_ge(g_in, 16)
                for t in range(NTILE):
                    b, n = t % RING, n_rows(t)
                    dve.wait_ge(y_in[b], 16 * (t // RING) + 16)
                    for k in range(2):
                        if k:
                            dve.wait_ge(mixed, 2 * t + 1)
                        dve.scalar_tensor_tensor(out=H.h[0:n, t, :], in0=yb[b][0:n, k, :], scalar=H.w[k][0:n, t:t + 1],
                                                 in1=H.h[0:n, t, :], op0=ALU.mult, op1=ALU.add).then_inc(mixed, 1)
                    if t:
                        finish(t - 1)
                finish(NT)

            @block.scalar
            def _(act):
                act.wait_ge(st_turned, 1)
                act.activation(small[:], pst[0:ST_N, 0:P], ACT.Copy).then_inc(st_out, 1)
                for t in range(NTILE):
                    b, n = t % 2, n_rows(t)
                    act.wait_ge(mixed, 2 * t + 2)
                    if t >= 2:
                        act.wait_ge(stored[b], 16 * (t // 2))
                    act.activation(out[b][0:n, :], H.h[0:n, t, :], ACT.Square,
                                   accum_out=ss[0:n, t:t + 1]).then_inc(sq_done, 1)
                    act.wait_ge(sq_done, t + 1)
                    act.activation(rms[0:n, t:t + 1], ss[0:n, t:t + 1], ACT.Sqrt, bias=R.eps[0:n, :],
                                   scale=1.0 / D).then_inc(rms_done, 1)

            @block.tensor
            def _(pe):
                pe.transpose(pst[0:ST_N, 0:P], R.stage[:], R.ident[:]).then_inc(st_turned, 1)

            @block.sync
            def _(sp):
                sp.dma_start(g_fin[:], A["norm_final_g"].partition_broadcast(P)).then_inc(g_in, 16)
                sp.wait_ge(st_out, 1)
                for at, n, dst in ((ST_CONVP, 24, conv_p), (ST_CONVS, 24, conv_s)):
                    sp.dma_start(dst[0, 0].rearrange("j (n p) -> (j n) p", p=P), small[at:at + n, :]).then_inc(st_stored, 16)
                for at, n, dst in ((ST_LRUP, 8, lru_p), (ST_LRUS, 8, lru_s)):
                    sp.dma_start(dst[0, 0].rearrange("(n p) -> n p", p=P), small[at:at + n, :]).then_inc(st_stored, 16)
                for t in range(NTILE):
                    b, n = t % 2, n_rows(t)
                    sp.wait_ge(out_done, t + 1)
                    dst = y_prompt[0, t * P:(t + 1) * P, :] if t < NT else y_sample[0]
                    sp.dma_start(dst, out[b][0:n, :]).then_inc(stored[b], 16)
                for b in range(2):
                    sp.wait_ge(stored[b], 16 * len(range(b, NTILE, 2)))
                sp.wait_ge(st_stored, 64)


class Resident:

    def __init__(self, nc, ctx):
        sb = lambda n, s, d=F32: ctx.enter_context(nc.sbuf_tensor(n, s, d))
        self.passed = ctx.enter_context(nc.semaphore("passed"))
        self.spent = []
        self.const = sb("const", [P, CN_N])
        self.ident = self.const[:, CN_ID:CN_ID + P]
        self.par = sb("par", [P, PR_N])
        self.stage = sb("stage", [P, ST_N])
        self.eps = sb("eps", [P, 1])
        self.lam_neg = sb("lam_neg", [P, 8])
        self.lam_pos = sb("lam_pos", [P, 8])

    def spend(self, sem):
        self.spent.append(sem)
        return sem


class Routed:

    def __init__(self, nc, ctx):
        sb = lambda n, s, d=F32: ctx.enter_context(nc.sbuf_tensor(f"h_{n}", s, d))
        self.h = sb("residual", [P, NTILE, D])
        self.logits = sb("logits", [P, NTILE, ROUT])
        self.bias = sb("bias", [P, ROUT])
        self.g_ffn = sb("g_ffn", [P, D])
        self.rms, self.rstd = sb("rms", [P, NTILE]), sb("rstd", [P, NTILE])
        self.slots = sb("slots", [P, 2, E], U32)
        self.unfilled = [sb(f"unfilled{k}", [P, NTILE], U32) for k in range(2)]
        self.w = [sb(f"w{k}", [P, NTILE]) for k in range(2)]
        self.w_over = sb("w_over", [P, NTILE, E])
        self.over = sb("over", [1, E + 1], I32)


def trunk_kernel(nc, A, outs):
    y_prompt, y_sample, conv_p, lru_p, ret_p, conv_s, lru_s, ret_s = outs
    merged_lru = nc.dram_tensor("merged_lru", (KD, P, T), F32).ap()
    merged = nc.dram_tensor("merged", (KD, P, T), F32).ap()
    y_rows = nc.dram_tensor("y_rows", (2 * T, D), F32).ap()
    xf_rows = nc.dram_tensor("xf_rows", (T, D), F32).ap()
    with ExitStack() as ctx:
        R = Resident(nc, ctx)
        with ExitStack() as mixer:
            M = Mixer(nc, mixer, R)
            normalise(nc, A, R, M)
            lru(nc, A, R, M)
            merge(nc, A, R, M, "ml", 6, "w_lru_o", None, merged_lru)
            retention(nc, A, R, M, ret_p[0, 0], ret_s[0, 0])
            merge(nc, A, R, M, "mr", 7, "w_ret_o", merged_lru, merged)
        H = Routed(nc, ctx)
        out_proj(nc, A, R, H, merged, xf_rows)
        experts(nc, A, R, H, xf_rows, y_rows)
        overflow(nc, A, R, H, xf_rows, y_rows)
        combine(nc, A, R, H, y_rows, (y_prompt, y_sample, conv_p, lru_p, conv_s, lru_s))


_INS = ["x_prompt", "x_sample", "cache_conv", "state_lru", "state_ret", "norm_mix_g", "w_in", "conv_w", "conv_b",
        "lru_wa", "lru_ba", "lru_wx", "lru_bx", "lru_lambda", "ret_gn_g", "w_lru_o", "w_ret_o", "w_out", "norm_ffn_g",
        "w_router_group", "b_router_group", "w_router_expert", "b_router_expert", "w_exp_gate", "w_exp_up",
        "w_exp_down", "norm_final_g"]
_OUTS = [(1, SEQ, D), (1, DEC, D), (1, 1, PAD, D), (1, 1, D), (1, 1, HEADS, P, P),
         (1, 1, PAD, D), (1, 1, D), (1, 1, HEADS, P, P)]


def kernel(**inputs):
    import numpy as _np
    import concourse.bacc as _bacc
    from concourse.bass_utils import run_bass_kernel_spmd as _run

    nc = _bacc.Bacc("TRN2", target_bir_lowering=False, num_devices=1)
    arrays, A = {}, {}
    tables, small = shape_tables()
    for name, a in [(n, inputs[n]) for n in _INS] + [("const_tables", tables), ("const_small", small)]:
        a = _np.ascontiguousarray(a)
        arrays[f"in_{name}"] = a
        A[name] = nc.dram_tensor(f"in_{name}", a.shape, mybir.dt.from_np(a.dtype), kind="ExternalInput").ap()
    outs = [nc.dram_tensor(f"out_{i}", shape, F32, kind="ExternalOutput").ap() for i, shape in enumerate(_OUTS)]
    trunk_kernel(nc, A, outs)
    r = _run(nc, [arrays], core_ids=[0])
    return tuple(r.results[0][f"out_{i}"] for i in range(len(_OUTS)))
```

```python
from contextlib import ExitStack

import numpy as np

import concourse.bass as bass
from concourse import mybir

F32 = mybir.dt.float32
F32R = mybir.dt.float32r
U32 = mybir.dt.uint32
I32 = mybir.dt.int32
ALU = mybir.AluOpType
ACT = mybir.ActivationFunctionType
AX = mybir.AxisListType
ds = bass.ds

P = 128
D = 1024
KD = D // P
SEQ = 1024
DEC = 32
PAST = 512
T = SEQ + DEC
NT = SEQ // P
NTILE = NT + 1
CT = 3
CW = T // CT
CONV = 4
PAD = CONV - 1
XP = PAD + SEQ + PAD + DEC
XC = XP - PAD
S0 = SEQ + PAD
CHUNK = 64
HEADS = 8
GROUPS = 4
PER_GROUP = 8
E = GROUPS * PER_GROUP
FE = 512
KF = FE // P
CHUNK_W = 4 * FE
SLOTS = 96
ROUT = GROUPS + E
EPS = 1e-6
BIG = 3.0e38

PR_GMIX, PR_CONVW, PR_CONVB, PR_BA, PR_BX, PR_LAM, PR_GN, PR_LRU, PR_CACHE = 0, 8, 40, 48, 56, 64, 72, 80, 88
PR_N = 112
ST_CONVP, ST_CONVS, ST_LRUP, ST_LRUS = 0, 24, 48, 56
ST_N = 64
TB_COS = 0
TB_SIN = TB_COS + T
TB_MASK = TB_SIN + T
TB_QDEC = TB_MASK + HEADS * P
TB_KDEC = TB_QDEC + HEADS * P
TB_KDECS = TB_KDEC + HEADS
TB_GT = TB_KDECS + HEADS
TB_GS = TB_GT + HEADS
TB_N = TB_GS + HEADS
CN_ID = 0
CN_TRI = CN_ID + P
CN_ONE = CN_TRI + P
CN_IOTA = CN_ONE + P
CN_TOK = CN_IOTA + P
CN_DST = CN_TOK + NTILE
CN_N = CN_DST + 2 * NTILE
NOWHERE = float(1 << 20)
LOG_TERMS = 9


def shape_tables():
    f32 = np.float32
    half = P // 2
    inv = np.power(f32(10000.0), -np.arange(half, dtype=f32) / f32(half)).astype(f32)
    pos = np.concatenate([np.arange(SEQ), PAST + np.arange(DEC)]).astype(f32)
    ang = (pos[None, :] * inv[:, None]).astype(f32).astype(np.float64)
    tb = np.zeros((P, TB_N), np.float64)
    tb[:, TB_COS:TB_COS + T] = np.concatenate([np.cos(ang), np.cos(ang)], 0)
    tb[:, TB_SIN:TB_SIN + T] = np.concatenate([np.sin(ang), -np.sin(ang)], 0)
    i = np.arange(P)
    scale = float(P) ** -0.5
    for h in range(HEADS):
        lg = np.log1p(-np.power(2.0, -5.0 - h))
        jj, ii = i[:, None], i[None, :]
        same = (ii // CHUNK) == (jj // CHUNK)
        decay = np.where(same, np.exp(lg * np.abs(ii - jj)),
                         np.where(ii > jj, np.exp(lg * np.maximum(ii - jj, 0)), 0.0))
        tb[:, TB_MASK + h * P:TB_MASK + (h + 1) * P] = decay * np.exp(-lg * (ii + 1.0)) * scale
        tb[:, TB_QDEC + h * P:TB_QDEC + (h + 1) * P] = np.exp(lg * (i + 1.0))[None, :]
        tb[:, TB_KDEC + h] = np.exp(lg * (P - 1.0 - i)) * scale
        tb[:DEC, TB_KDECS + h] = np.exp(lg * (DEC - 1.0 - i[:DEC])) * scale
        tb[:, TB_GT + h] = np.exp(lg * P)
        tb[:, TB_GS + h] = np.exp(lg * DEC)
    cn = np.zeros((P, CN_N), f32)
    cn[:, CN_ID:CN_ID + P] = np.eye(P)
    cn[:, CN_TRI:CN_TRI + P] = (i[:, None] < i[None, :])
    cn[:, CN_ONE:CN_ONE + P] = 1.0
    cn[:, CN_IOTA:CN_IOTA + P] = np.arange(P)[None, :]
    for t in range(NTILE):
        cn[:, CN_TOK + t] = t * P + i + 1
        for k in range(2):
            cn[:, CN_DST + k * NTILE + t] = 2 * (t * P + i) + k + 1
    return tb.astype(f32), cn


def first(n):
    return isinstance(n, int) and n == 0


def wait_alone(eng, sem, value, passed):
    eng.wait_ge(sem, value)
    eng.sem_inc(passed, 1)


class Steps:

    def __init__(self, eng, sem, base=0):
        self.eng, self.sem, self.base, self.n = eng, sem, base, 0

    def did(self, ins):
        ins.then_inc(self.sem, 1)
        self.n += 1

    def wait(self):
        self.eng.wait_ge(self.sem, self.base + self.n)

    def link(self, ins):
        self.did(ins)
        self.wait()


class Mixer:

    def __init__(self, nc, ctx, R):
        self.nc, self.passed = nc, R.passed
        sb = lambda n, s, d=F32: ctx.enter_context(nc.sbuf_tensor(n, s, d))
        sem = lambda n: R.spend(ctx.enter_context(nc.semaphore(f"job_{n}")))
        self.xn_hi = sb("xn_hi", [P, KD, T], F32R)
        self.xn_lo = sb("xn_lo", [P, KD, T], F32R)
        self.u = R.u[:].rearrange("p (k t) -> p k t", k=KD)
        self.w_raw = [sb(f"w_raw{s}", [P, KD, P]) for s in range(2)]
        self.w_hi = [sb(f"w_hi{s}", [P, KD, P], F32R) for s in range(2)]
        self.w_lo = [sb(f"w_lo{s}", [P, KD, P], F32R) for s in range(2)]
        self.psum = [self.bank_set(ctx, 0)]
        self.raw_in = [sem(f"raw_in{s}") for s in range(2)]
        self.hi_done = [sem(f"hi_done{s}") for s in range(2)]
        self.split_done = [sem(f"split_done{s}") for s in range(2)]
        self.tile_done = [sem(f"tile_done{s}") for s in range(2)]
        self.tile_free = [sem(f"tile_free{s}") for s in range(2)]
        self.before = 0

    def bank_set(self, ctx, s):
        return [ctx.enter_context(self.nc.psum_tensor(f"job_ps{s}{c}", [P, 512], F32)) for c in range(CT)]

    def next_stage(self, jobs):
        self.before += jobs


    def load(self, sp, s, turn, src):
        turn = turn + self.before
        if not (isinstance(turn, int) and turn == 0):
            wait_alone(sp, self.split_done[s], turn, self.passed)
        sp.dma_start(self.w_raw[s][:], src.rearrange("(k p) n -> p k n", p=P)).then_inc(self.raw_in[s], 16)

    def split(self, pool, s, turn):
        turn = turn + self.before
        pool.wait_ge(self.raw_in[s], turn * 16 + 16)
        if not (isinstance(turn, int) and turn == 0):
            wait_alone(pool, self.tile_done[s], turn * CT, self.passed)
        pool.tensor_copy(self.w_hi[s][:], self.w_raw[s][:]).then_inc(self.hi_done[s], 1)
        pool.wait_ge(self.hi_done[s], turn + 1)
        pool.tensor_tensor(self.w_lo[s][:], self.w_raw[s][:], self.w_hi[s][:].bitcast(F32),
                           ALU.subtract).then_inc(self.split_done[s], 1)

    def column(self, pe, s, turn, c, x_hi, x_lo, before_k=lambda k: None):
        turn = turn + self.before
        pe.wait_ge(self.split_done[s], turn + 1)
        if not (isinstance(turn, int) and turn == 0):
            pe.wait_ge(self.tile_free[s], turn * CT + (c + 1 - CT))
        cols = slice(c * CW, (c + 1) * CW)
        out = self.psum[s][c][:, 0:CW]
        for k in range(KD):
            before_k(k)
            pe.matmul(out, self.w_hi[s][:, k, :], x_hi[:, k, cols], start=(k == 0), stop=False)
            pe.matmul(out, self.w_hi[s][:, k, :], x_lo[:, k, cols], start=False, stop=False)
            mm = pe.matmul(out, self.w_lo[s][:, k, :], x_hi[:, k, cols], start=False, stop=(k == KD - 1))
        mm.then_inc(self.tile_done[s], 1)

    def product(self, pe, s, turn, x_hi, x_lo, after=lambda c: None):
        for c in range(CT):
            self.column(pe, s, turn, c, x_hi, x_lo)
            after(c)

    def tile_ready(self, eng, s, turn, c):
        eng.wait_ge(self.tile_done[s], (turn + self.before) * CT + c + 1)

    def tile_taken(self, eng, s, turn, c):
        eng.wait_ge(self.tile_free[s], (turn + self.before) * CT + c + 1)

    def taken(self, eng, s, turn):
        eng.wait_ge(self.tile_free[s], (turn + self.before) * CT + CT)


def normalise(nc, A, R, M, following):
    RING = 4
    with ExitStack() as ctx:
        sb = lambda n, s, d=F32: ctx.enter_context(nc.sbuf_tensor(n, s, d))
        sem = lambda n: R.spend(ctx.enter_context(nc.semaphore(n)))
        xt = [sb(f"x_tile{b}", [P, D]) for b in range(RING)]
        g_mix = sb("g_mix", [P, D])
        junk = sb("square", [P, D])
        ss, rms, rstd = (sb(n, [P, NTILE]) for n in ("sum_sq", "rms", "rstd"))
        rows = sb("par_rows", [PR_N, P])
        sp_e = sb("sp_e", [P, 8])
        sp_s = sb("sp_s", [P, 8])
        sp_q = sb("sp_q", [P, 8])
        sp_a = sb("sp_a", [P, 8])
        pt = [[ctx.enter_context(nc.psum_tensor(f"pt{b}{n}", [P, 4, P], F32)) for n in range(2)] for b in range(2)]
        pp = ctx.enter_context(nc.psum_tensor("pp", [P, 512], F32))
        par_in = sem("par_in")
        const_in = sem("const_in")
        par_t = sem("par_t")
        par_done = sem("par_done")
        eps_done = sem("eps_done")
        g_in = sem("g_in")
        x_in = [sem(f"x_in{b}") for b in range(RING)]
        sq_done, rms_done, rstd_done = sem("sq_done"), sem("rms_done"), sem("rstd_done")
        scaled = sem("scaled")
        turned = sem("turned")
        hi_done, lo_done = sem("xn_hi_done"), sem("xn_lo_done")
        exp_done = sem("exp_done")
        abs_done = sem("abs_done")
        dve_step = sem("dve_step")

        n_rows = lambda t: P if t < NT else DEC
        cols = lambda t: slice(t * P, t * P + n_rows(t))

        with nc.Block() as block:
            @block.sync
            def _(sp):
                def load(t):
                    b = t % RING
                    if t >= RING:
                        sp.wait_ge(turned, 2 * (t - RING + 1))
                    src = A["x_prompt"][0, cols(t), :] if t < NT else A["x_sample"][0]
                    sp.dma_start(xt[b][0:n_rows(t), :], src).then_inc(x_in[b], 16)

                load(0)
                sp.dma_start(R.const[:], A["const_small"]).then_inc(const_in, 16)
                load(1)
                sp.dma_start(g_mix[:], A["norm_mix_g"][0].partition_broadcast(P)).then_inc(g_in, 16)
                for t in range(2, RING):
                    load(t)
                vectors = [(PR_GMIX, "norm_mix_g"), (PR_CONVW, "conv_w"), (PR_CONVB, "conv_b"), (PR_BA, "lru_ba"),
                           (PR_BX, "lru_bx"), (PR_LAM, "lru_lambda"), (PR_GN, "ret_gn_g"), (PR_LRU, "state_lru"),
                           (PR_CACHE, "cache_conv")]
                for at, name in vectors:
                    src = A[name]
                    src = src[0, 0] if name == "cache_conv" else src[0]
                    src = (src.rearrange("j (n p) -> (j n) p", p=P) if name in ("conv_w", "cache_conv")
                           else src.rearrange("o (n p) -> (o n) p", p=P) if name == "state_lru"
                           else src.rearrange("(n p) -> n p", p=P))
                    sp.dma_start(rows[at:at + src.shape[0], :], src).then_inc(par_in, 16)

                for s_ in range(2):
                    M.load(sp, s_, 0, following[s_])
                for t in range(NTILE):
                    if t >= RING:
                        load(t)

            @block.scalar
            def _(act):
                act.wait_ge(eps_done, 1)

                def hi(t):
                    for m in range(2):
                        act.wait_ge(turned, 2 * t + m + 1)
                        act.activation(M.xn_hi[:, 4 * m:4 * m + 4, cols(t)], pt[t % 2][m][:, :, 0:n_rows(t)],
                                       ACT.Copy).then_inc(hi_done, 1)

                for t in range(NTILE):
                    b, n = t % RING, n_rows(t)
                    act.wait_ge(x_in[b], 16 * (t // RING) + 16)
                    act.activation(junk[0:n, :], xt[b][0:n, :], ACT.Square,
                                   accum_out=ss[0:n, t:t + 1]).then_inc(sq_done, 1)
                    act.wait_ge(sq_done, t + 1)
                    act.activation(rms[0:n, t:t + 1], ss[0:n, t:t + 1], ACT.Sqrt, bias=R.eps[0:n, :],
                                   scale=1.0 / D).then_inc(rms_done, 1)
                    if t:
                        hi(t - 1)
                hi(NT)
                act.wait_ge(abs_done, 1)
                act.activation(sp_e[:], sp_a[:], ACT.Exp, scale=-1.0).then_inc(exp_done, 1)

            @block.vector
            def _(dve):
                dve.memset(R.eps[:], EPS).then_inc(eps_done, 1)
                dve.memset(R.stage[:], 0.0)
                dve.wait_ge(g_in, 16)

                def lo(t):
                    for m in range(2):
                        dve.wait_ge(hi_done, 2 * t + m + 1)
                        at = M.xn_hi[:, 4 * m:4 * m + 4, cols(t)]
                        dve.tensor_tensor(M.xn_lo[:, 4 * m:4 * m + 4, cols(t)], pt[t % 2][m][:, :, 0:n_rows(t)],
                                          at.bitcast(F32), ALU.subtract).then_inc(lo_done, 1)

                for t in range(NTILE):
                    b, n = t % RING, n_rows(t)
                    dve.wait_ge(rms_done, t + 1)
                    dve.reciprocal(rstd[0:n, t:t + 1], rms[0:n, t:t + 1]).then_inc(rstd_done, 1)
                    dve.wait_ge(rstd_done, t + 1)
                    dve.scalar_tensor_tensor(out=xt[b][0:n, :], in0=xt[b][0:n, :], scalar=rstd[0:n, t:t + 1],
                                             in1=g_mix[0:n, :], op0=ALU.mult, op1=ALU.mult).then_inc(scaled, 1)
                    if t:
                        lo(t - 1)
                lo(NT)
                dve.wait_ge(par_t, 1)
                dve.tensor_copy(R.par[:], pp[:, 0:PR_N]).then_inc(par_done, 1)
                dve.wait_ge(par_done, 1)
                st = Steps(dve, dve_step)
                lam = R.par[:, PR_LAM:PR_LAM + 8]
                st.link(dve.tensor_scalar(sp_s[:], lam, -1.0, None, ALU.mult))
                dve.tensor_tensor(sp_a[:], sp_s[:], lam, ALU.max).then_inc(abs_done, 1)
                dve.wait_ge(exp_done, 1)
                st.link(dve.tensor_scalar(sp_q[:], sp_e[:], 2.0, None, ALU.add))
                st.link(dve.reciprocal(sp_q[:], sp_q[:]))
                st.link(dve.tensor_tensor(sp_e[:], sp_e[:], sp_q[:], ALU.mult))
                st.link(dve.tensor_tensor(sp_q[:], sp_e[:], sp_e[:], ALU.mult))
                st.link(dve.memset(sp_a[:], 1.0 / (2 * LOG_TERMS - 1)))
                for j in range(LOG_TERMS - 2, -1, -1):
                    st.link(dve.tensor_tensor(sp_a[:], sp_a[:], sp_q[:], ALU.mult))
                    st.link(dve.tensor_scalar(sp_a[:], sp_a[:], 1.0 / (2 * j + 1), None, ALU.add))
                st.link(dve.tensor_tensor(sp_a[:], sp_a[:], sp_e[:], ALU.mult))
                st.link(dve.tensor_scalar(sp_s[:], sp_s[:], 0.0, None, ALU.max))
                st.link(dve.scalar_tensor_tensor(out=sp_s[:], in0=sp_a[:], scalar=2.0, in1=sp_s[:],
                                                 op0=ALU.mult, op1=ALU.add))
                dve.tensor_scalar(R.lam_neg[:], sp_s[:], -8.0, None, ALU.mult)
                dve.tensor_scalar(R.lam_pos[:], sp_s[:], 8.0, None, ALU.mult)

            @block.tensor
            def _(pe):
                pe.wait_ge(const_in, 16)

                for t in range(NTILE):
                    b, n = t % RING, n_rows(t)
                    pe.wait_ge(scaled, t + 1)
                    for m in range(2):
                        if t >= 2:
                            pe.wait_ge(lo_done, 2 * (t - 2) + m + 1)
                        for k in range(4):
                            ins = pe.transpose(pt[t % 2][m][:, k, 0:n], xt[b][0:n, (4 * m + k) * P:(4 * m + k + 1) * P],
                                               R.ident[0:n, 0:n])
                        ins.then_inc(turned, 1)
                    for c in range(CT):
                        last = ((c + 1) * CW - 1) // P
                        if t == min(last + 2, NT):
                            pe.wait_ge(lo_done, 2 * last + 2)
                            M.column(pe, 0, 0, c, M.xn_hi, M.xn_lo)
                    if t == RING:
                        pe.wait_ge(par_in, 16 * 9)
                        pe.transpose(pp[:, 0:PR_N], rows[:], R.ident[0:PR_N, 0:PR_N]).then_inc(par_t, 1)

            @block.gpsimd
            def _(pool):
                for s_ in range(2):
                    M.split(pool, s_, 0)


def lru(nc, A, R, M, following):
    with ExitStack() as ctx:
        sb = lambda n, s, d=F32: ctx.enter_context(nc.sbuf_tensor(n, s, d))
        sem = lambda n: R.spend(ctx.enter_context(nc.semaphore(f"lru_{n}")))
        psum = M.psum
        pg = [ctx.enter_context(nc.psum_tensor(f"lru_pg{g}", [P, 512], F32)) for g in range(2)]
        xp = sb("conv_in", [P, XP])
        xc = sb("conv_out", [P, XC])
        gl = sb("gelu_gate", [P, T])
        r = sb("r_gate", [P, XC])
        ig = sb("i_gate", [P, XC])
        a = sb("decay_a", [P, XC])
        tl = sb("tanh_la", [P, XC])
        mu = sb("mult", [P, XC])
        hs = sb("hidden", [P, XC])
        wg = sb("w_gates", [P, 2, P])
        wg_in = sem("wg_in")
        conv_step = sem("conv_step")
        xc_done = sem("xc_done")
        gelu_out = sem("gelu_out")
        gate_done = sem("gate_done")
        gate_free = [sem(f"gate_free{g}") for g in range(2)]
        gates_out = sem("gates_out")
        a_out = sem("a_out")
        tl_out = sem("tl_out")
        m2_done = sem("m2_done")
        mult_out = sem("mult_out")
        chain = sem("chain")
        u_done = sem("u_done")
        xp_set = sem("xp_set")
        CG = XC // CT
        CONV_STEPS = 5
        CHAIN_STEPS = 8
        w_in = A["w_in"][0]

        with nc.Block() as block:
            @block.sync
            def _(sp):
                def gates(n):
                    for g, name in enumerate(("lru_wa", "lru_wx")):
                        sp.dma_start(wg[:, g, :], A[name][0, ds(n, 1), :, :].rearrange("o c d -> (o c) d")).then_inc(wg_in, 16)

                gates(0)
                with sp.Fori(1, KD) as n:
                    M.load(sp, 0, n, w_in[:, ds(n * P, P)])
                    M.load(sp, 1, n, w_in[:, ds(n * P + D, P)])
                    wait_alone(sp, gate_done, n * (2 * CT), R.passed)
                    gates(n)
                for s in range(2):
                    M.load(sp, s, KD, following[s])

            @block.gpsimd
            def _(pool):
                with pool.Fori(1, KD + 1) as n:
                    for s in range(2):
                        M.split(pool, s, n)

            @block.tensor
            def _(pe):
                def body(n):
                    M.product(pe, 1, n, M.xn_hi, M.xn_lo)
                    pe.wait_ge(wg_in, n * 32 + 32)
                    pe.wait_ge(xc_done, n + 1)
                    for c in range(CT):
                        for g in range(2):
                            if not (isinstance(n, int) and n == 0 and c == 0):
                                pe.wait_ge(gate_free[g], n * CT + c)
                            pe.matmul(pg[g][:, 0:CG], wg[:, g, :], xc[:, c * CG:(c + 1) * CG],
                                      start=True, stop=True).then_inc(gate_done, 1)
                    M.product(pe, 0, n + 1, M.xn_hi, M.xn_lo)

                body(0)
                with pe.Fori(1, KD) as n:
                    body(n)

            @block.scalar
            def _(act):
                act.wait_ge(xp_set, 1)

                def body(n):
                    if not first(n):
                        act.wait_ge(conv_step, n * CONV_STEPS)
                    act.activation(xp[:, PAD + SEQ:PAD + SEQ + PAD],
                                   R.par[:, PR_CACHE:PR_CACHE + 24].rearrange("p (j n) -> p j n", n=KD)[:, :, ds(n, 1)]
                                   .rearrange("p j o -> p (j o)"), ACT.Copy)
                    for c in range(CT):
                        M.tile_ready(act, 0, n, c)
                        lo, hi = c * CW, min((c + 1) * CW, SEQ)
                        ins = act.activation(xp[:, PAD + lo:PAD + hi], psum[0][c][:, 0:hi - lo], ACT.Copy)
                        if hi - lo < CW:
                            ins = act.activation(xp[:, PAD + S0:XP], psum[0][c][:, hi - lo:CW], ACT.Copy)
                        ins.then_inc(M.tile_free[0], 1)
                    if not first(n):
                        act.wait_ge(u_done, n)
                    for c in range(CT):
                        M.tile_ready(act, 1, n, c)
                        act.activation(gl[:, c * CW:(c + 1) * CW], psum[1][c][:, 0:CW],
                                       ACT.Gelu_apprx_tanh).then_inc(M.tile_free[1], 1)
                    for c in range(CT):
                        for g, (dst, bias) in enumerate(((r, PR_BA), (ig, PR_BX))):
                            wait_alone(act, gate_done, n * (2 * CT) + 2 * c + g + 1, R.passed)
                            act.activation(dst[:, c * CG:(c + 1) * CG], pg[g][:, 0:CG], ACT.Sigmoid,
                                           bias=R.par[:, ds(n + bias, 1)]).then_inc(gate_free[g], 1)
                    act.wait_ge(gate_free[0], n * CT + CT)
                    act.activation(a[:], r[:], ACT.Exp, scale=R.lam_neg[:, ds(n, 1)]).then_inc(a_out, 1)
                    act.activation(tl[:], r[:], ACT.Tanh, scale=R.lam_pos[:, ds(n, 1)]).then_inc(tl_out, 1)
                    act.wait_ge(m2_done, n + 1)
                    act.activation(mu[:], mu[:], ACT.Sqrt).then_inc(mult_out, 1)

                body(0)
                with act.Fori(1, KD) as n:
                    body(n)

            @block.vector
            def _(dve):
                dve.memset(xp[:], 0.0).then_inc(xp_set, 1)

                def body(n):
                    st = Steps(dve, conv_step, n * CONV_STEPS)
                    M.taken(dve, 0, n)
                    if not first(n):
                        dve.wait_ge(gate_done, n * (2 * CT))
                    w = lambda j: R.par[:, ds(n + (PR_CONVW + KD * j), 1)]
                    st.link(dve.tensor_scalar(xc[:], xp[:, 0:XC], w(0), R.par[:, ds(n + PR_CONVB, 1)],
                                              ALU.mult, ALU.add))
                    for j in range(1, CONV):
                        ins = dve.scalar_tensor_tensor(out=xc[:], in0=xp[:, j:j + XC], scalar=w(j), in1=xc[:],
                                                       op0=ALU.mult, op1=ALU.add)
                        if j < CONV - 1:
                            st.link(ins)
                        else:
                            ins.then_inc(xc_done, 1)
                    stage = R.stage[:].rearrange("p (j n) -> p j n", n=KD)
                    st.did(dve.tensor_copy(stage[:, 0:3, ds(n, 1)], xp[:, SEQ:SEQ + PAD].unsqueeze(2)))
                    st.did(dve.tensor_copy(stage[:, 3:6, ds(n, 1)], xp[:, XP - PAD:XP].unsqueeze(2)))
                    ch = Steps(dve, chain, n * CHAIN_STEPS)
                    dve.wait_ge(a_out, n + 1)
                    dve.wait_ge(xc_done, n + 1)
                    dve.wait_ge(gate_free[1], n * CT + CT)
                    ch.did(dve.tensor_tensor(mu[:], a[:], a[:], ALU.mult))
                    ch.link(dve.tensor_tensor(ig[:], ig[:], xc[:], ALU.mult))
                    dve.wait_ge(tl_out, n + 1)
                    dve.scalar_tensor_tensor(out=mu[:], in0=mu[:], scalar=1.0, in1=tl[:],
                                             op0=ALU.add, op1=ALU.mult).then_inc(m2_done, 1)
                    dve.wait_ge(mult_out, n + 1)
                    ch.link(dve.memset(mu[:, 0:1], 1.0))
                    ch.link(dve.tensor_tensor(ig[:], ig[:], mu[:], ALU.mult))
                    ch.did(dve.tensor_tensor_scan(out=hs[:, 0:SEQ], data0=a[:, 0:SEQ], data1=ig[:, 0:SEQ],
                                                  initial=0.0, op0=ALU.mult, op1=ALU.add))
                    ch.link(dve.tensor_tensor_scan(out=hs[:, S0:XC], data0=a[:, S0:XC], data1=ig[:, S0:XC],
                                                   initial=R.par[:, ds(n + PR_LRU, 1)], op0=ALU.mult, op1=ALU.add))
                    ch.did(dve.tensor_copy(stage[:, 6:7, ds(n, 1)], hs[:, SEQ - 1:SEQ].unsqueeze(2)))
                    ch.did(dve.tensor_copy(stage[:, 7:8, ds(n, 1)], hs[:, XC - 1:XC].unsqueeze(2)))
                    M.taken(dve, 1, n)
                    dve.tensor_tensor(M.u[:, ds(n, 1), 0:SEQ].rearrange("p o t -> p (o t)"), gl[:, 0:SEQ],
                                      hs[:, 0:SEQ], ALU.mult)
                    dve.tensor_tensor(M.u[:, ds(n, 1), SEQ:T].rearrange("p o t -> p (o t)"), gl[:, SEQ:T],
                                      hs[:, S0:XC], ALU.mult).then_inc(u_done, 1)
                    dve.wait_ge(u_done, n + 1)

                body(0)
                with dve.Fori(1, KD) as n:
                    body(n)


def merge(nc, A, R, M, tag, gate_col, w_out_name, src, dst, following):
    with ExitStack() as ctx:
        sb = lambda n, s, d=F32: ctx.enter_context(nc.sbuf_tensor(f"{tag}_{n}", s, d))
        sem = lambda n: ctx.enter_context(nc.semaphore(f"{tag}_{n}"))
        psum = M.psum
        u_hi = sb("u_hi", [P, KD, T], F32R)
        u_lo = sb("u_lo", [P, KD, T], F32R)
        sg = sb("sig_gate", [P, T])
        m = sb("merged", [P, T])
        old = sb("old", [P, T]) if src is not None else None
        u_hi_done = sem("u_hi_done")
        u_split = sem("u_split")
        m_done = sem("m_done")
        m_stored = sem("m_stored")
        old_in = sem("old_in")
        w_gate = A["w_in"][0][:, gate_col * D:(gate_col + 1) * D]
        w_out = A[w_out_name][0]

        with nc.Block() as block:
            @block.sync
            def _(sp):
                def loads(j):
                    M.load(sp, 0, j, w_gate[:, ds(j * P, P)])
                    M.load(sp, 1, j, w_out[:, ds(j * P, P)])

                def load_old(j):
                    if src is not None:
                        sp.dma_start(old[:], src[ds(j, 1)].rearrange("o p t -> (o p) t")).then_inc(old_in, 16)

                def store(j):
                    sp.wait_ge(m_done, j * CT + CT)
                    sp.dma_start(dst[ds(j, 1)].rearrange("o p t -> (o p) t"), m[:]).then_inc(m_stored, 16)

                load_old(0)
                with sp.Fori(0, KD - 1) as j:
                    loads(j + 1)
                    store(j)
                    load_old(j + 1)
                if following:
                    for s in range(2):
                        M.load(sp, s, KD, following[s])
                else:
                    sp.wait_ge(u_split, KD)
                    for k in range(KD):
                        sp.dma_start(R.u[:, k * D:(k + 1) * D], A["w_out"][0][k * P:(k + 1) * P, :]).then_inc(R.w_out_in, 16)
                store(KD - 1)
                sp.wait_ge(m_stored, 16 * KD)

            @block.gpsimd
            def _(pool):
                with pool.Fori(1, KD + 1 if following else KD) as j:
                    for s in range(2):
                        M.split(pool, s, j)

            @block.tensor
            def _(pe):
                M.column(pe, 1, 0, 0, u_hi, u_lo, before_k=lambda k: pe.wait_ge(u_split, k + 1))
                for c in range(1, CT):
                    M.column(pe, 1, 0, c, u_hi, u_lo)
                with pe.Fori(1, KD) as j:
                    M.product(pe, 0, j, M.xn_hi, M.xn_lo)
                    M.product(pe, 1, j, u_hi, u_lo)
                if following:
                    M.product(pe, 0, KD, M.xn_hi, M.xn_lo)

            @block.scalar
            def _(act):
                with act.Fori(0, KD) as k:
                    act.activation(u_hi[:, ds(k, 1), :], M.u[:, ds(k, 1), :], ACT.Copy).then_inc(u_hi_done, 1)

                def body(j):
                    if not first(j):
                        act.wait_ge(m_done, j * CT)
                    for c in range(CT):
                        M.tile_ready(act, 0, j, c)
                        act.activation(sg[:, c * CW:(c + 1) * CW], psum[0][c][:, 0:CW],
                                       ACT.Sigmoid).then_inc(M.tile_free[0], 1)

                body(0)
                with act.Fori(1, KD) as j:
                    body(j)

            @block.vector
            def _(dve):
                with dve.Fori(0, KD) as k:
                    dve.wait_ge(u_hi_done, k + 1)
                    dve.tensor_tensor(u_lo[:, ds(k, 1), :], M.u[:, ds(k, 1), :], u_hi[:, ds(k, 1), :].bitcast(F32),
                                      ALU.subtract).then_inc(u_split, 1)

                def body(j):
                    if not first(j):
                        dve.wait_ge(m_stored, j * 16)
                    for c in range(CT):
                        cols = slice(c * CW, (c + 1) * CW)
                        M.tile_taken(dve, 0, j, c)
                        M.tile_ready(dve, 1, j, c)
                        dve.tensor_tensor(m[:, cols], psum[1][c][:, 0:CW], sg[:, cols],
                                          ALU.mult).then_inc(M.tile_free[1], 1)
                        M.tile_taken(dve, 1, j, c)
                        if src is None:
                            dve.sem_inc(m_done, 1)
                            continue
                        if c == 0:
                            dve.wait_ge(old_in, j * 16 + 16)
                        dve.tensor_tensor(m[:, cols], m[:, cols], old[:, cols], ALU.add).then_inc(m_done, 1)

                body(0)
                with dve.Fori(1, KD) as j:
                    body(j)


class Turns:

    ORDER = (("o", 0), ("o", 1), ("o", 2), ("vt", 0), ("vt", 1), ("vt", 2), ("ot", 0), ("ot", 1), ("kt", 0),
             ("ot", 2), ("kt", 1), ("kt", 2), ("kv", 0), ("kv", 1), ("kv", 2), ("sc", 0), ("sc", 1), ("sc", 2))

    def __init__(self, nc, ctx, passed):
        self.passed = passed
        self.bank = [ctx.enter_context(nc.psum_tensor(f"ret_turn{b}", [P, 4, P], F32)) for b in range(2)]
        self.free = [ctx.enter_context(nc.semaphore(f"ret_turn_free{b}")) for b in range(2)]
        self.done = {s: ctx.enter_context(nc.semaphore(f"ret_{s}_done")) for s, c in self.ORDER if c == 0}

    def at(self, kind, h, stage, c):
        have = {"first": ("vt", "kt", "sc", "kv"), "loop": self.done, "last": ("o", "ot")}
        places = lambda k: [(s, x, i % 2) for i, (s, x) in enumerate(self.ORDER) if s in have[k]]
        mine = places(kind)
        n = next(i for i, (s, x, _) in enumerate(mine) if (s, x) == (stage, c))
        bank = mine[n][2]
        before = sum(b == bank for _, _, b in mine[:n])
        if kind != "first":
            before += sum(b == bank for _, _, b in places("first"))
            before = (h - 1) * sum(b == bank for _, _, b in places("loop")) + before
        return bank, before

    def claim(self, pe, kind, h, stage, c):
        b, before = self.at(kind, h, stage, c)
        if not (isinstance(before, int) and before == 0):
            wait_alone(pe, self.free[b], before, self.passed)
        return self.bank[b]

    def ready(self, eng, kind, h, head, stage, c):
        wait_alone(eng, self.done[stage], head * 3 + c + 1, self.passed)
        b, _ = self.at(kind, h, stage, c)
        return self.bank[b], self.free[b]

    def taken(self, eng, kind, h, stage):
        for c in (1, 2):
            b, before = self.at(kind, h, stage, c)
            wait_alone(eng, self.free[b], before + 1, self.passed)


def tiles_of(c):
    return range(4 * c, 4 * c + 4) if c < 2 else [NT]


def retention(nc, A, R, M, out_prompt, out_sample, following):
    with ExitStack() as ctx:
        sb = lambda n, s, d=F32: ctx.enter_context(nc.sbuf_tensor(f"ret_{n}", s, d))
        sem = lambda n: ctx.enter_context(nc.semaphore(f"ret_{n}"))
        psum = M.psum
        turns = Turns(nc, ctx, R.passed)
        tb = sb("tables", [P, TB_N])
        s_in = sb("state_in", [P, HEADS, P])
        v_f = sb("v_features", [P, T])
        k_f = sb("k_features", [P, T])
        q_f = sb("q_features", [P, T])
        half = sb("rotary_half", [P, T])
        srg = sb("silu_gate", [P, T])
        v_t = sb("v_tokens", [P, NTILE, P])
        k_t = sb("k_tokens", [P, NTILE, P])
        pt = sb("scores", [P, NTILE, P])
        on = sb("out_tokens", [P, NTILE, P])
        state = sb("states", [P, NTILE, P])
        bst = sb("bn_parts", [P, NTILE, 6])
        mv = sb("mean_var", [P, NTILE, 2])
        sd = sb("deviation", [P, NTILE])
        table_in = sem("table_in")
        init = sem("init")
        k_rot = sem("k_rotated")
        q_rot = sem("q_rotated")
        rope_step = sem("rope_step")
        stats_step = sem("stats_step")
        state_step = sem("state_step")
        scored = sem("scored")
        centred = sem("centred")
        sd_out = sem("sd_out")
        on_done = sem("on_done")
        u_done = sem("u_done")
        stored = sem("state_stored")
        w_in = A["w_in"][0]
        STATE_STEPS = NT + 1
        STATS_STEPS = 2 * NTILE + 1
        ROPE_STEPS = 7
        cols = lambda t: slice(t * P, (t + 1) * P) if t < NT else slice(SEQ, T)
        rows = lambda t: P if t < NT else DEC
        one = lambda ap: ap.rearrange("p o t -> p (o t)")

        with nc.Block() as block:
            @block.sync
            def _(sp):
                sp.dma_start(tb[:], A["const_tables"]).then_inc(table_in, 16)
                sp.dma_start(s_in[:], A["state_ret"][0, 0].rearrange("h d e -> d h e")).then_inc(table_in, 16)

                def loads(h):
                    for n, col in enumerate((4, 3, 2, 5)):
                        M.load(sp, n % 2, h * 2 + n // 2, w_in[:, ds(h * P + col * D, P)])

                def store(h):
                    sp.wait_ge(state_step, h * STATE_STEPS + STATE_STEPS)
                    sp.dma_start(out_prompt[ds(h, 1)].rearrange("o d e -> (o d) e"), state[:, NT, :]).then_inc(stored, 16)
                    sp.dma_start(out_sample[ds(h, 1)].rearrange("o d e -> (o d) e"), state[:, 0, :]).then_inc(stored, 16)

                def rest(h):
                    for n, col in ((2, 2), (3, 5)):
                        M.load(sp, n % 2, h * 2 + n // 2, w_in[:, ds(h * P + col * D, P)])

                rest(0)
                with sp.Fori(0, HEADS - 1) as h:
                    loads(h + 1)
                    store(h)
                for s in range(2):
                    M.load(sp, s, HEADS * 2, following[s])
                store(HEADS - 1)
                sp.wait_ge(stored, 32 * HEADS)

            @block.gpsimd
            def _(pool):
                with pool.Fori(0, HEADS) as h:
                    for n in range(2, 6):
                        M.split(pool, n % 2, h * 2 + n // 2)

            @block.tensor
            def _(pe):
                def turn_to(kind, step, stage, c, src, out_free):
                    bank = turns.claim(pe, kind, step, stage, c)
                    for t in tiles_of(c):
                        n = rows(t)
                        if out_free:
                            ins = pe.transpose(bank[0:n, t % 4, :], src[:, cols(t)], R.ident[:])
                        else:
                            ins = pe.transpose(bank[:, t % 4, 0:n], src[0:n, t, :], R.ident[0:n, 0:n])
                    ins.then_inc(turns.done[stage], 1)

                def output(kind, step, head, c):
                    if c == 0:
                        pe.wait_ge(state_step, (head + 1) * STATE_STEPS)
                        pe.wait_ge(scored, (head + 1) * 3)
                    bank = turns.claim(pe, kind, step, "o", c)
                    for t in tiles_of(c):
                        n = rows(t)
                        out = bank[0:n, t % 4, :]
                        ins = pe.matmul(out, pt[0:n, t, 0:n], v_t[0:n, t, :], start=True, stop=(t == 0))
                        if 0 < t < NT:
                            ins = pe.matmul(out, q_f[:, cols(t)], state[:, t, :], start=False, stop=True)
                        if t == NT:
                            ins = pe.matmul(out, q_f[:, cols(t)], one(s_in[:, ds(head, 1), :]),
                                            start=False, stop=True)
                    ins.then_inc(turns.done["o"], 1)

                def out_turned(kind, step, head, c):
                    if c == 0:
                        pe.wait_ge(on_done, head + 1)
                    turn_to(kind, step, "ot", c, on, False)

                def v_turned(kind, h, c):
                    if c == 0:
                        M.taken(pe, 0, h * 2)
                    turn_to(kind, h, "vt", c, v_f, True)

                def k_turned(kind, h, c):
                    if c == 0:
                        pe.wait_ge(k_rot, h + 1)
                    turn_to(kind, h, "kt", c, k_f, True)

                def score(kind, h, c):
                    if c == 0:
                        pe.wait_ge(q_rot, h + 1)
                    bank = turns.claim(pe, kind, h, "sc", c)
                    for t in tiles_of(c):
                        n = rows(t)
                        ins = pe.matmul(bank[0:n, t % 4, 0:n], k_f[:, cols(t)], q_f[:, cols(t)],
                                        start=True, stop=True)
                    ins.then_inc(turns.done["sc"], 1)

                def state_share(kind, h, c):
                    if c == 0:
                        turns.taken(pe, kind, h, "vt")
                        turns.taken(pe, kind, h, "kt")
                    bank = turns.claim(pe, kind, h, "kv", c)
                    for t in tiles_of(c):
                        n = rows(t)
                        ins = pe.matmul(bank[:, t % 4, :], k_t[0:n, t, :], v_t[0:n, t, :], start=True, stop=True)
                    ins.then_inc(turns.done["kv"], 1)

                def step_of(kind, h):
                    def behind_q(c):
                        if kind == "loop":
                            if c == 1:
                                out_turned(kind, h, h - 1, 1)
                            else:
                                out_turned(kind, h, h - 1, c)
                        if c == 1:
                            k_turned(kind, h, 0)
                        if c == 2:
                            k_turned(kind, h, 1)
                            k_turned(kind, h, 2)

                    def behind_gate(c):
                        state_share(kind, h, c)
                        if c == 2:
                            for x in range(3):
                                score(kind, h, x)

                    if kind == "loop":
                        M.product(pe, 0, h * 2, M.xn_hi, M.xn_lo, lambda c: output(kind, h, h - 1, c))
                    M.product(pe, 1, h * 2, M.xn_hi, M.xn_lo, lambda c: v_turned(kind, h, c))
                    M.product(pe, 0, h * 2 + 1, M.xn_hi, M.xn_lo, behind_q)
                    M.product(pe, 1, h * 2 + 1, M.xn_hi, M.xn_lo, behind_gate)

                step_of("first", 0)
                pe.wait_ge(table_in, 32)
                with pe.Fori(1, HEADS) as h:
                    step_of("loop", h)
                M.product(pe, 0, HEADS * 2, M.xn_hi, M.xn_lo, lambda c: output("last", HEADS, HEADS - 1, c))
                for c in range(3):
                    out_turned("last", HEADS, HEADS - 1, c)

            @block.scalar
            def _(act):
                def take(s, turn, dst, func, after=lambda c: None):
                    for c in range(CT):
                        M.tile_ready(act, s, turn, c)
                        act.activation(dst[:, c * CW:(c + 1) * CW], psum[s][c][:, 0:CW], func).then_inc(M.tile_free[s], 1)
                        after(c)

                def deviation(head):
                    act.wait_ge(centred, (head + 1) * NTILE)
                    act.activation(sd[:], mv[:, :, 1:2].rearrange("p t o -> p (t o)"), ACT.Sqrt,
                                   bias=R.eps[:]).then_inc(sd_out, 1)

                def step_of(kind, h):
                    def take_v_t(c):
                        bank, free = turns.ready(act, kind, h, h, "vt", c)
                        ts = tiles_of(c)
                        n = rows(ts[0])
                        act.activation(v_t[0:n, ts[0]:ts[-1] + 1, :], bank[0:n, 0:len(ts), :], ACT.Copy).then_inc(free, 1)
                        if kind == "loop" and c == 1:
                            deviation(h - 1)

                    def earlier(stage, steps=3):
                        if kind == "loop":
                            act.wait_ge(turns.done[stage], h * 3)

                    earlier("vt")
                    take(0, h * 2, v_f, ACT.Copy)
                    earlier("sc")
                    earlier("o")
                    take(1, h * 2, k_f, ACT.Copy, take_v_t)
                    take(0, h * 2 + 1, q_f, ACT.Copy)
                    earlier("kv")
                    if kind == "first":
                        act.wait_ge(table_in, 32)
                    for c in range(3):
                        bank, free = turns.ready(act, kind, h, h, "kt", c)
                        ts = tiles_of(c)
                        n = rows(ts[0])
                        dec = tb[0:n, ds(h + (TB_KDEC if c < 2 else TB_KDECS), 1)]
                        act.activation(k_t[0:n, ts[0]:ts[-1] + 1, :], bank[0:n, 0:len(ts), :], ACT.Copy,
                                       scale=dec).then_inc(free, 1)
                    if kind == "loop":
                        act.wait_ge(u_done, h * 3)
                    take(1, h * 2 + 1, srg, ACT.Silu)

                act.wait_ge(init, 1)
                step_of("first", 0)
                with act.Fori(1, HEADS) as h:
                    step_of("loop", h)
                deviation(HEADS - 1)

            @block.vector
            def _(dve):
                def centre(kind, step, head):
                    st = Steps(dve, stats_step, head * STATS_STEPS)
                    for c in range(3):
                        bank, free = turns.ready(dve, kind, step, head, "o", c)
                        for t in tiles_of(c):
                            n = rows(t)
                            st.did(dve.bn_stats(bst[0:n, t, :], bank[0:n, t % 4, :]))
                        wait_alone(dve, stats_step, st.base + st.n, R.passed)
                        for t in tiles_of(c):
                            n = rows(t)
                            st.did(dve.bn_aggr(mv[0:n, t, :], bst[0:n, t, :]))
                        st.wait()
                        for t in tiles_of(c):
                            n = rows(t)
                            dve.tensor_scalar(on[0:n, t, :], bank[0:n, t % 4, :], mv[0:n, t, 0:1], None,
                                              ALU.subtract).then_inc(centred, 1)
                        dve.wait_ge(centred, head * NTILE + tiles_of(c)[-1] + 1)
                        dve.sem_inc(free, 1)
                    dve.wait_ge(sd_out, head + 1)
                    st.link(dve.reciprocal(sd[:], sd[:]))
                    dve.tensor_tensor(on[:], on[:], sd[:].unsqueeze(2).broadcast_to((P, NTILE, P)),
                                      ALU.mult).then_inc(on_done, 1)

                def gated(kind, step, head):
                    M.taken(dve, 1, head * 2 + 1)
                    for c in range(3):
                        bank, free = turns.ready(dve, kind, step, head, "ot", c)
                        lo, hi = cols(tiles_of(c)[0]).start, cols(tiles_of(c)[-1]).stop
                        dve.scalar_tensor_tensor(
                            out=one(M.u[:, ds(head, 1), lo:hi]),
                            in0=bank[:].rearrange("p a b -> p (a b)")[:, 0:hi - lo],
                            scalar=R.par[:, ds(head + PR_GN, 1)], in1=srg[:, lo:hi],
                            op0=ALU.mult, op1=ALU.mult).then_inc(u_done, 1)
                        dve.wait_ge(u_done, head * 3 + c + 1)
                        dve.sem_inc(free, 1)

                def rotate(st, x, s, turn, done):
                    M.taken(dve, s, turn)
                    st.did(dve.tensor_tensor(half[64:128, :], x[0:64, :], tb[0:64, TB_SIN:TB_SIN + T], ALU.mult))
                    st.link(dve.tensor_tensor(half[0:64, :], x[64:128, :], tb[64:128, TB_SIN:TB_SIN + T], ALU.mult))
                    st.link(dve.tensor_tensor(x[:], x[:], tb[:, TB_COS:TB_COS + T], ALU.mult))
                    ins = dve.tensor_tensor(x[:], x[:], half[:], ALU.add)
                    ins.then_inc(done, 1)

                def step_of(kind, h):
                    st = Steps(dve, rope_step, h * ROPE_STEPS)
                    if kind == "loop":
                        centre(kind, h, h - 1)
                    rotate(st, k_f, 1, h * 2, k_rot)
                    if kind == "loop":
                        gated(kind, h, h - 1)
                    dve.wait_ge(k_rot, h + 1)
                    M.taken(dve, 0, h * 2 + 1)
                    st.did(dve.tensor_tensor(half[64:128, :], q_f[0:64, :], tb[0:64, TB_SIN:TB_SIN + T], ALU.mult))
                    st.link(dve.tensor_tensor(half[0:64, :], q_f[64:128, :], tb[64:128, TB_SIN:TB_SIN + T], ALU.mult))
                    st.link(dve.tensor_tensor(q_f[:], q_f[:], tb[:, TB_COS:TB_COS + T], ALU.mult))
                    st.link(dve.tensor_tensor(q_f[:], q_f[:], half[:], ALU.add))
                    qd = tb[:, ds(h * P + TB_QDEC, P)]
                    dve.tensor_tensor(q_f[:, 0:SEQ].rearrange("p (a b) -> p a b", b=P),
                                      q_f[:, 0:SEQ].rearrange("p (a b) -> p a b", b=P),
                                      qd.unsqueeze(1).broadcast_to((P, NT, P)), ALU.mult)
                    dve.tensor_tensor(q_f[:, SEQ:T], q_f[:, SEQ:T], tb[:, ds(h * P + TB_QDEC, DEC)],
                                      ALU.mult).then_inc(q_rot, 1)
                    if kind == "loop":
                        dve.wait_ge(turns.done["o"], h * 3)
                        dve.wait_ge(stored, h * 32)
                    ss = Steps(dve, state_step, h * STATE_STEPS)
                    for c in range(3):
                        bank, free = turns.ready(dve, kind, h, h, "kv", c)
                        for t in tiles_of(c):
                            if t == 0:
                                ss.link(dve.tensor_copy(state[:, 1, :], bank[:, 0, :]))
                            elif t < NT:
                                ss.link(dve.scalar_tensor_tensor(
                                    out=state[:, t + 1, :], in0=state[:, t, :], scalar=tb[:, ds(h + TB_GT, 1)],
                                    in1=bank[:, t % 4, :], op0=ALU.mult, op1=ALU.add))
                            else:
                                ss.link(dve.scalar_tensor_tensor(
                                    out=state[:, 0, :], in0=one(s_in[:, ds(h, 1), :]), scalar=tb[:, ds(h + TB_GS, 1)],
                                    in1=bank[:, 0, :], op0=ALU.mult, op1=ALU.add))
                        dve.sem_inc(free, 1)
                    for c in range(3):
                        bank, free = turns.ready(dve, kind, h, h, "sc", c)
                        ts = tiles_of(c)
                        n = rows(ts[0])
                        mask = tb[0:n, ds(h * P + TB_MASK, n)]
                        dve.tensor_tensor(pt[0:n, ts[0]:ts[-1] + 1, 0:n], bank[0:n, 0:len(ts), 0:n],
                                          mask.unsqueeze(1).broadcast_to((n, len(ts), n)), ALU.mult).then_inc(scored, 1)
                        dve.wait_ge(scored, h * 3 + c + 1)
                        dve.sem_inc(free, 1)

                dve.memset(mv[:], 1.0)
                dve.memset(on[:], 0.0).then_inc(init, 1)
                dve.wait_ge(init, 1)
                dve.wait_ge(table_in, 32)
                step_of("first", 0)
                with dve.Fori(1, HEADS) as h:
                    step_of("loop", h)
                centre("last", HEADS, HEADS - 1)
                gated("last", HEADS, HEADS - 1)


def tile_at(x, t, n):
    return x[0:n, ds(t, 1), :].rearrange("p o d -> p (o d)")


def out_proj(nc, A, R, H, merged, xf_rows):
    with ExitStack() as ctx:
        sb = lambda n, s, d=F32: ctx.enter_context(nc.sbuf_tensor(f"op_{n}", s, d))
        sem = lambda n: ctx.enter_context(nc.semaphore(f"op_{n}"))
        ps = lambda n, s: ctx.enter_context(nc.psum_tensor(f"op_{n}", s, F32))
        w_raw = [R.u[:, k * D:(k + 1) * D] for k in range(KD)]
        w_hi = sb("w_hi", [P, KD, D], F32R)
        w_lo = sb("w_lo", [P, KD, D], F32R)
        m_raw = [sb(f"m_raw{b}", [P, KD, P]) for b in range(2)]
        m_hi = [sb(f"m_hi{b}", [P, KD, P], F32R) for b in range(2)]
        m_lo = [sb(f"m_lo{b}", [P, KD, P], F32R) for b in range(2)]
        xt = [sb(f"x_tile{b}", [P, D]) for b in range(2)]
        xf_t = sb("xf_turned", [P, KD, P])
        xf = [sb(f"xf{b}", [P, D]) for b in range(2)]
        w_rt = sb("w_router", [P, KD, ROUT])
        ss = sb("sum_sq", [P, 1])
        po = [ps(f"out{n}", [P, 512]) for n in range(2)]
        pt = [ps(f"turned{n}", [P, 4, P]) for n in range(2)]
        pl = ps("logits", [P, ROUT])
        w_hi_done, w_lo_done = sem("w_hi_done"), sem("w_lo_done")
        m_in = [sem(f"m_in{b}") for b in range(2)]
        m_hi_done, m_lo_done = sem("m_hi_done"), sem("m_lo_done")
        x_in = [sem(f"x_in{b}") for b in range(2)]
        rt_in = sem("rt_in")
        out_done = [sem(f"out_done{n}") for n in range(2)]
        h_done = [sem(f"h_done{n}") for n in range(2)]
        sq_done, rms_done = sem("sq_done"), sem("rms_done")
        rstd_done = sem("rstd_done")
        xf_done = sem("xf_done")
        xf_stored = [sem(f"xf_stored{b}") for b in range(2)]
        turned = sem("turned")
        xf_t_done = sem("xf_t_done")
        logit_done = sem("logit_done")
        logit_out = sem("logit_out")
        init = sem("init")
        N2 = D // 512

        def over_tiles(eng, body, started=False):
            for b in range(0 if started else 2):
                body(b, b, 0, P)
            with eng.Fori(1, NT // 2) as i:
                for b in range(2):
                    body(i * 2 + b, b, i, P)
            body(NT, 0, NT // 2, DEC)

        def two_ahead(eng, split, norm, weights):
            weights(range(0, 3))
            split(0, 0, 0, P)
            weights(range(3, KD))
            split(1, 1, 0, P)
            for b in range(2):
                norm(b, b, 0, P, lambda: split(b + 2, b, 1, P))
            with eng.Fori(1, NT // 2 - 1) as i:
                for b in range(2):
                    norm(i * 2 + b, b, i, P, lambda: split(i * 2 + b + 2, b, i + 1, P))
            norm(NT - 2, 0, NT // 2 - 1, P, lambda: split(NT, 0, NT // 2, DEC))
            norm(NT - 1, 1, NT // 2 - 1, P, lambda: None)
            norm(NT, 0, NT // 2, DEC, lambda: None)

        def first(t):
            return isinstance(t, int) and t < 2

        with nc.Block() as block:
            @block.sync
            def _(sp):
                m_view = merged.rearrange("k p t -> p k t")

                def load(t, b, i, n):
                    at = ds(t * P, P) if n == P else slice(SEQ, T)
                    if not first(t):
                        sp.wait_ge(m_lo_done, t - 1)
                        sp.dma_start(m_raw[b][:, :, 0:n], m_view[:, :, at]).then_inc(m_in[b], 16)
                        sp.wait_ge(h_done[1], t - 1)
                    src = A["x_prompt"][0, at, :] if n == P else A["x_sample"][0]
                    sp.dma_start(xt[b][0:n, :], src).then_inc(x_in[b], 16)

                sp.dma_start(m_raw[0][:], m_view[:, :, 0:P]).then_inc(m_in[0], 16)
                sp.dma_start(m_raw[1][:], m_view[:, :, P:2 * P]).then_inc(m_in[1], 16)
                for b in range(2):
                    load(b, b, 0, P)
                sp.wait_ge(w_lo_done, KD)
                for c in range(4):
                    load_chunk(sp, A, H, c, 0)
                over_tiles(sp, load, started=True)
                for s in R.spent:
                    sp.sem_clear(s)
                for b in range(2):
                    sp.wait_ge(xf_stored[b], 16 * len(range(b, NTILE, 2)))

            @block.gpsimd
            def _(pool):
                for name, at, n in (("w_router_group", 0, GROUPS), ("w_router_expert", GROUPS, E)):
                    pool.dma_start(w_rt[:, :, at:at + n], A[name][0].rearrange("(k p) n -> p k n", p=P)).then_inc(rt_in, 16)
                pool.dma_start(H.bias[:, 0:GROUPS], A["b_router_group"][0].partition_broadcast(P)).then_inc(rt_in, 16)
                pool.dma_start(H.bias[:, GROUPS:ROUT], A["b_router_expert"][0].partition_broadcast(P)).then_inc(rt_in, 16)
                pool.dma_start(H.g_ffn[:], A["norm_ffn_g"][0].partition_broadcast(P)).then_inc(rt_in, 16)
                pool.wait_ge(rt_in, 80)

                def keep(t, b, i, n):
                    pool.wait_ge(xf_done, t + 1)
                    pool.dma_start(xf_rows[ds(t * P, n), :], xf[b][0:n, :]).then_inc(xf_stored[b], 16)

                over_tiles(pool, keep)

            @block.tensor
            def _(pe):
                def project(t, b, n, half):
                    pe.wait_ge(m_lo_done, t + 1)
                    if not isinstance(t, int) or t > 0:
                        pe.wait_ge(h_done[half], t)
                    out = po[half][0:n, :]
                    at = slice(half * 512, half * 512 + 512)
                    for k in range(KD):
                        if isinstance(t, int) and t == 0:
                            pe.wait_ge(w_lo_done, k + 1)
                        pe.matmul(out, m_hi[b][:, k, 0:n], w_hi[:, k, at], start=(k == 0), stop=False)
                        pe.matmul(out, m_hi[b][:, k, 0:n], w_lo[:, k, at], start=False, stop=False)
                        mm = pe.matmul(out, m_lo[b][:, k, 0:n], w_hi[:, k, at], start=False, stop=(k == KD - 1))
                    mm.then_inc(out_done[half], 1)

                def turn(t, b, n):
                    pe.wait_ge(xf_done, t + 1)
                    if not isinstance(t, int) or t > 0:
                        pe.wait_ge(xf_t_done, t * 2)
                    for k in range(KD):
                        ins = pe.transpose(pt[k // 4][:, k % 4, 0:n], xf[b][0:n, k * P:(k + 1) * P],
                                           R.ident[0:n, 0:n])
                        if k % 4 == 3:
                            ins.then_inc(turned, 1)

                def logits(t, n):
                    pe.wait_ge(xf_t_done, t * 2 + 2)
                    if not isinstance(t, int) or t > 0:
                        pe.wait_ge(logit_out, t)
                    for k in range(KD):
                        mm = pe.matmul(pl[0:n, :], xf_t[:, k, 0:n], w_rt[:, k, :], start=(k == 0), stop=(k == KD - 1))
                    mm.then_inc(logit_done, 1)

                def both(t, b, n):
                    project(t, b, n, 0)
                    turn(t - 1, 1 - b, P)
                    project(t, b, n, 1)
                    logits(t - 1, P)

                for half in range(N2):
                    project(0, 0, P, half)
                pe.wait_ge(rt_in, 80)
                both(1, 1, P)
                with pe.Fori(1, NT // 2) as i:
                    both(i * 2, 0, P)
                    both(i * 2 + 1, 1, P)
                both(NT, 0, DEC)
                turn(NT, 0, DEC)
                logits(NT, DEC)

            @block.scalar
            def _(act):
                def split(t, b, i, n):
                    act.wait_ge(m_in[b], i * 16 + 16)
                    if not first(t):
                        act.wait_ge(out_done[1], t - 1)
                    act.activation(m_hi[b][:, :, 0:n], m_raw[b][:, :, 0:n], ACT.Copy).then_inc(m_hi_done, 1)

                def norm(t, b, i, n, next_split):
                    act.wait_ge(h_done[1], t + 1)
                    if not first(t):
                        act.wait_ge(turned, t * 2 - 2)
                        act.wait_ge(xf_stored[b], i * 16)
                    act.activation(xf[b][0:n, :], tile_at(H.h, t, n), ACT.Square,
                                   accum_out=ss[0:n, :]).then_inc(sq_done, 1)
                    act.wait_ge(sq_done, t + 1)
                    act.activation(H.rms[0:n, ds(t, 1)], ss[0:n, :], ACT.Sqrt, bias=R.eps[0:n, :],
                                   scale=1.0 / D).then_inc(rms_done, 1)
                    next_split()
                    act.wait_ge(logit_done, t)
                    for m in range(2):
                        act.wait_ge(turned, t * 2 + m + 1)
                        act.activation(xf_t[:, 4 * m:4 * m + 4, 0:n], pt[m][:, :, 0:n], ACT.Copy).then_inc(xf_t_done, 1)
                    act.wait_ge(logit_done, t + 1)
                    act.activation(tile_at(H.logits, t, n), pl[0:n, :], ACT.Copy).then_inc(logit_out, 1)

                def weights(ks):
                    act.wait_ge(R.w_out_in, 16 * KD)
                    for k in ks:
                        act.activation(w_hi[:, k, :], w_raw[k], ACT.Copy).then_inc(w_hi_done, 1)

                act.wait_ge(init, 1)
                two_ahead(act, split, norm, weights)

            @block.vector
            def _(dve):
                def split(t, b, i, n):
                    dve.wait_ge(m_hi_done, t + 1)
                    dve.tensor_tensor(m_lo[b][:, :, 0:n], m_raw[b][:, :, 0:n], m_hi[b][:, :, 0:n].bitcast(F32),
                                      ALU.subtract).then_inc(m_lo_done, 1)

                def norm(t, b, i, n, next_split):
                    dve.wait_ge(x_in[b], i * 16 + 16)
                    for half in range(N2):
                        at = slice(half * 512, half * 512 + 512)
                        dve.wait_ge(out_done[half], t + 1)
                        dve.tensor_tensor(tile_at(H.h, t, n)[:, at], po[half][0:n, :], xt[b][0:n, at],
                                          ALU.add).then_inc(h_done[half], 1)
                    dve.wait_ge(rms_done, t + 1)
                    dve.reciprocal(H.rstd[0:n, ds(t, 1)], H.rms[0:n, ds(t, 1)]).then_inc(rstd_done, 1)
                    dve.wait_ge(rstd_done, t + 1)
                    dve.scalar_tensor_tensor(out=xf[b][0:n, :], in0=tile_at(H.h, t, n),
                                             scalar=H.rstd[0:n, ds(t, 1)], in1=H.g_ffn[0:n, :],
                                             op0=ALU.mult, op1=ALU.mult).then_inc(xf_done, 1)
                    next_split()

                def weights(ks):
                    for k in ks:
                        dve.wait_ge(w_hi_done, k + 1)
                        dve.tensor_tensor(w_lo[:, k, :], w_raw[k], w_hi[:, k, :].bitcast(F32),
                                          ALU.subtract).then_inc(w_lo_done, 1)
                    if KD - 1 in ks:
                        dve.wait_ge(rt_in, 80)

                dve.memset(H.logits[:], 0.0).then_inc(init, 1)
                two_ahead(dve, split, norm, weights)


class Router:

    def __init__(self, nc, ctx, R, H):
        sb = lambda n, s, d=F32: ctx.enter_context(nc.sbuf_tensor(f"rt_{n}", s, d))
        sem = lambda n: ctx.enter_context(nc.semaphore(f"rt_{n}"))
        self.slots_done = sem("slots_done")
        g_max, g_sum, g_idx, g_top = (sb(n, [P, NTILE]) for n in ("g_max", "g_sum", "g_idx", "g_top"))
        g_key = sb("g_key", [P, NTILE, GROUPS])
        g_exp = sb("g_exp", [P, NTILE, GROUPS])
        g_hot = sb("g_hot", [P, NTILE, GROUPS])
        picked = sb("picked", [P, NTILE, GROUPS, PER_GROUP])
        sel = sb("sel", [P, NTILE, PER_GROUP])
        key = sb("key", [P, NTILE, PER_GROUP])
        hot8 = sb("hot8", [P, NTILE, PER_GROUP])
        v = [sb(f"v{k}", [P, NTILE]) for k in range(2)]
        eid = [sb(f"eid{k}", [P, NTILE]) for k in range(2)]
        ratio, den = sb("ratio", [P, NTILE]), sb("den", [P, NTILE])
        w = [sb(f"w{k}", [P, NTILE]) for k in range(2)]
        hot = [sb(f"hot{k}", [P, NTILE, E]) for k in range(2)]
        took = sb("took", [P, NTILE, E])
        before = sb("before", [P, NTILE + 1, E])
        tmp = sb("tmp", [P, NTILE, E])
        rank = [sb(f"rank{k}", [P, NTILE]) for k in range(2)]
        fits = [sb(f"fits{k}", [P, NTILE]) for k in range(2)]
        in_slot = [sb(f"in_slot{k}", [P, NTILE, SLOTS], F32R) for k in range(2)]
        ids = [sb(f"ids{k}", [P, NTILE, 2, E], F32R) for k in range(2)]
        slot_f, slot_none = sb("slot_f", [SLOTS, 2, E]), sb("slot_none", [SLOTS, 2, E])
        over = sb("over", [1, E])
        over_n = sb("over_n", [1, E])
        over_x = sb("over_x", [1, E, E])
        ones = sb("ones", [1, E])
        over_f = sb("over_f", [1, E + 1])
        bank = ctx.enter_context(nc.psum_tensor("rt_bank", [P, (NTILE + 3) * E], F32))
        pr = bank[:, 0:(NTILE + 1) * E]
        pm = bank[0:SLOTS, (NTILE + 1) * E:].rearrange("p (a e) -> p a e", a=2)
        step = sem("step")
        g_in = sem("g_in")
        d_in = sem("d_in")
        exp_out = sem("exp_out")
        took_done = sem("took_done")
        rank_done = sem("rank_done")
        in_slot_done = sem("in_slot_done")
        slots_turned = sem("slots_turned")
        wide = lambda ap, n: ap[:].unsqueeze(2).broadcast_to((P, NTILE, n))
        iota = lambda n: R.const[:, CN_IOTA:CN_IOTA + n].unsqueeze(1).broadcast_to((P, NTILE, n))

        def vector(dve):
            st = Steps(dve, step)

            def first_index(x, top, k_buf, out, n):
                st.link(dve.tensor_tensor(k_buf[:], x, wide(top, n), ALU.is_lt))
                st.link(dve.scalar_tensor_tensor(out=k_buf[:], in0=k_buf[:], scalar=64.0, in1=iota(n),
                                                 op0=ALU.mult, op1=ALU.add))
                st.link(dve.tensor_reduce(out[:], k_buf[:], AX.X, ALU.min))

            st.link(dve.tensor_tensor(H.logits[:], H.logits[:],
                                      H.bias[:].unsqueeze(1).broadcast_to((P, NTILE, ROUT)), ALU.add))
            g = H.logits[:, :, 0:GROUPS]
            st.link(dve.tensor_reduce(g_max[:], g, AX.X, ALU.max))
            dve.tensor_tensor(g_exp[:], g, wide(g_max, GROUPS), ALU.subtract).then_inc(g_in, 1)
            first_index(g, g_max, g_key, g_idx, GROUPS)
            st.link(dve.tensor_tensor(g_hot[:], iota(GROUPS), wide(g_idx, GROUPS), ALU.is_equal))
            e4 = H.logits[:, :, GROUPS:ROUT].rearrange("p t (g j) -> p t g j", g=GROUPS)
            st.link(dve.tensor_tensor(picked[:], e4,
                                      g_hot[:].unsqueeze(3).broadcast_to((P, NTILE, GROUPS, PER_GROUP)), ALU.mult))
            st.link(dve.tensor_reduce(sel[:], picked[:].rearrange("p t g j -> p t j g"), AX.X, ALU.add))
            for k in range(2):
                st.link(dve.tensor_reduce(v[k][:], sel[:], AX.X, ALU.max))
                first_index(sel[:], v[k], key, eid[k], PER_GROUP)
                if k == 0:
                    st.link(dve.tensor_tensor(hot8[:], iota(PER_GROUP), wide(eid[0], PER_GROUP), ALU.is_equal))
                    st.link(dve.scalar_tensor_tensor(out=sel[:], in0=hot8[:], scalar=-BIG, in1=sel[:],
                                                     op0=ALU.mult, op1=ALU.add))
                st.link(dve.scalar_tensor_tensor(out=eid[k][:], in0=g_idx[:], scalar=float(PER_GROUP), in1=eid[k][:],
                                                 op0=ALU.mult, op1=ALU.add))
                st.link(dve.tensor_tensor(hot[k][:], iota(E), wide(eid[k], E), ALU.is_equal))
            dve.tensor_tensor(ratio[:], v[1][:], v[0][:], ALU.subtract).then_inc(d_in, 1)
            st.link(dve.tensor_tensor(took[:], hot[0][:], hot[1][:], ALU.add))
            for q in range(DEC, P, 32):
                st.did(dve.memset(took[q:q + 32, NT, :], 0.0))
            st.link(dve.memset(before[:, 0, :], 0.0))
            for t in range(NTILE):
                st.link(dve.tensor_tensor(before[:, t + 1, :], before[:, t, :], took[:, t, :], ALU.add))
            dve.sem_inc(took_done, 1)
            for k in range(2):
                st.did(dve.tensor_tensor(ids[k][:, :, 0, :], hot[k][:], R.const[:, CN_TOK:CN_TOK + NTILE]
                                         .unsqueeze(2).broadcast_to((P, NTILE, E)), ALU.mult))
                st.link(dve.tensor_tensor(ids[k][:, :, 1, :], hot[k][:],
                                          R.const[:, CN_DST + k * NTILE:CN_DST + (k + 1) * NTILE]
                                          .unsqueeze(2).broadcast_to((P, NTILE, E)), ALU.mult))
            dve.wait_ge(rank_done, 1)
            st.did(dve.tensor_scalar(over[:], pr[0:1, NTILE * E:], float(SLOTS), None, ALU.is_gt))
            ranks = pr[:, 0:NTILE * E].rearrange("p (t e) -> p t e", e=E)
            for k in range(2):
                st.link(dve.tensor_tensor(tmp[:], ranks, hot[k][:], ALU.mult))
                st.link(dve.tensor_reduce(rank[k][:], tmp[:], AX.X, ALU.add))
            for k in range(2):
                dve.tensor_tensor(in_slot[k][:], R.const[:, CN_IOTA:CN_IOTA + SLOTS].unsqueeze(1)
                                  .broadcast_to((P, NTILE, SLOTS)), wide(rank[k], SLOTS),
                                  ALU.is_equal).then_inc(in_slot_done, 1)
            dve.wait_ge(slots_turned, 1)
            st.did(dve.tensor_scalar(slot_none[:], pm[:], 0.5, NOWHERE, ALU.is_lt, ALU.mult))
            st.link(dve.tensor_copy(slot_f[:], pm[:]))
            st.link(dve.scalar_tensor_tensor(out=slot_f[:], in0=slot_f[:], scalar=-1.0, in1=slot_none[:],
                                             op0=ALU.add, op1=ALU.add))
            dve.tensor_copy(H.slots[:], slot_f[:]).then_inc(self.slots_done, 1)
            self.steps = st

        def weigh(dve):
            st = self.steps
            dve.wait_ge(exp_out, 2)
            st.link(dve.tensor_reduce(g_sum[:], g_exp[:], AX.X, ALU.add))
            st.link(dve.reciprocal(g_top[:], g_sum[:]))
            st.link(dve.tensor_scalar(den[:], ratio[:], 1.0, None, ALU.add))
            st.link(dve.reciprocal(den[:], den[:]))
            st.link(dve.tensor_tensor(w[0][:], g_top[:], den[:], ALU.mult))
            st.link(dve.tensor_tensor(w[1][:], w[0][:], ratio[:], ALU.mult))
            for k in range(2):
                st.link(dve.tensor_scalar(fits[k][:], rank[k][:], float(SLOTS), None, ALU.is_lt))
                st.link(dve.tensor_tensor(H.w[k][:], w[k][:], fits[k][:], ALU.mult))
                st.link(dve.tensor_tensor(w[k][:], w[k][:], H.w[k][:], ALU.subtract))
                st.link(dve.tensor_tensor(hot[k][:], hot[k][:], wide(w[k], E), ALU.mult))
                st.link(dve.scalar_tensor_tensor(out=fits[k][:], in0=fits[k][:], scalar=NOWHERE,
                                                 in1=R.const[:, CN_DST + k * NTILE:CN_DST + (k + 1) * NTILE],
                                                 op0=ALU.mult, op1=ALU.add))
                st.link(dve.tensor_scalar(fits[k][:], fits[k][:], -1.0, None, ALU.add))
                st.link(dve.tensor_copy(H.unfilled[k][:], fits[k][:]))
            st.link(dve.tensor_tensor(H.w_over[:], hot[0][:], hot[1][:], ALU.add))
            st.link(dve.memset(ones[:], 1.0))
            st.link(dve.tensor_tensor_scan(out=over_n[:], data0=ones[:], data1=over[:], initial=0.0,
                                           op0=ALU.mult, op1=ALU.add))
            st.link(dve.tensor_copy(over_f[:, E:E + 1], over_n[:, E - 1:E]))
            st.link(dve.tensor_tensor(over_n[:], over_n[:], over[:], ALU.mult))
            st.link(dve.tensor_scalar(ones[:], R.const[0:1, CN_IOTA:CN_IOTA + E], 1.0, None, ALU.add))
            st.link(dve.tensor_tensor(over_x[:], over_n[:].unsqueeze(1).broadcast_to((1, E, E)),
                                      ones[:].unsqueeze(2).broadcast_to((1, E, E)), ALU.is_equal))
            st.link(dve.tensor_tensor(over_x[:], over_x[:],
                                      R.const[0:1, CN_IOTA:CN_IOTA + E].unsqueeze(1).broadcast_to((1, E, E)),
                                      ALU.mult))
            st.link(dve.tensor_reduce(over_f[:, 0:E], over_x[:], AX.X, ALU.add))
            st.link(dve.tensor_copy(H.over[:], over_f[:]))

        def scalar(act):
            act.wait_ge(g_in, 1)
            act.activation(g_exp[:], g_exp[:], ACT.Exp).then_inc(exp_out, 1)
            act.wait_ge(d_in, 1)
            act.activation(ratio[:], ratio[:], ACT.Exp).then_inc(exp_out, 1)

        def tensor(pe):
            pe.wait_ge(took_done, 1)
            pe.matmul(pr[:, :], R.const[:, CN_ONE:CN_ONE + P], before[:].rearrange("p t e -> p (t e)"),
                      start=True, stop=False)
            pe.matmul(pr[:, 0:NTILE * E], R.const[:, CN_TRI:CN_TRI + P], took[:].rearrange("p t e -> p (t e)"),
                      start=False, stop=True).then_inc(rank_done, 1)
            for k in range(2):
                pe.wait_ge(in_slot_done, k + 1)
                for t in range(NTILE):
                    n = P if t < NT else DEC
                    mm = pe.matmul(pm[:].rearrange("p a e -> p (a e)"), in_slot[k][0:n, t, :],
                                   ids[k][0:n, t, :, :].rearrange("p a e -> p (a e)"),
                                   start=(k == 0 and t == 0), stop=(k == 1 and t == NT))
            mm.then_inc(slots_turned, 1)

        self.vector, self.weigh, self.scalar, self.tensor = vector, weigh, scalar, tensor


class Chunks:

    def __init__(self, kind, step):
        self.kind, self.step = kind, step

    def order(self, c):
        return {"first": lambda: c, "last": lambda: 6 * E - 6 + c}.get(self.kind, lambda: self.step * 6 + (c - 2))()

    def slot(self, c):
        return c % 3 if self.kind in ("loop", "end") else (c + 2) % 3

    def place(self, c):
        return c - 4 if self.kind == "last" else c

    def turn(self, c):
        return self.step if c < 4 or self.kind == "last" else self.step - 1


def load_chunk(sp, A, H, c, e, place=None):
    place = c if place is None else place
    name = ("w_exp_gate", "w_exp_up", "w_exp_down")[c // 2]
    k = (KD if c < 4 else KF) // 2
    m = A[name][0, ds(e, 1)].rearrange("o r n -> (o r) n")
    src = m[(c % 2) * k * P:(c % 2 + 1) * k * P, :].rearrange("(k p) n -> p k n", p=P)
    sp.dma_start(H.raw[place].rearrange("p (k n) -> p k n", k=k), src).then_inc(H.raw_in[place], 16)


def experts(nc, A, R, H, xf_rows, y_rows):
    with ExitStack() as ctx:
        sb = lambda n, s, d=F32: ctx.enter_context(nc.sbuf_tensor(f"ex_{n}", s, d))
        sem = lambda n: ctx.enter_context(nc.semaphore(f"ex_{n}"))
        ps = lambda n, s: ctx.enter_context(nc.psum_tensor(f"ex_{n}", s, F32))
        H.raw += [sb(f"raw{c}", [P, CHUNK_W])[:] for c in (4, 5)]
        raw, raw_in = H.raw, H.raw_in
        w_hi = [sb(f"w_hi{c}", [P, CHUNK_W], F32R) for c in range(3)]
        w_lo = [sb(f"w_lo{c}", [P, CHUNK_W], F32R) for c in range(3)]
        xe = sb("rows", [SLOTS, D])
        row_in, row_out = sb("row_in", [SLOTS, 1], U32), sb("row_out", [SLOTS, 1], U32)
        x_hi, x_lo = sb("x_hi", [P, KD, SLOTS], F32R), sb("x_lo", [P, KD, SLOTS], F32R)
        sil, hid = sb("silu", [SLOTS, FE]), sb("hidden", [SLOTS, FE])
        h_hi, h_lo = sb("h_hi", [P, KF, SLOTS], F32R), sb("h_lo", [P, KF, SLOTS], F32R)
        y = sb("y", [SLOTS, D])
        pg, pu, ph = ps("gate", [SLOTS, FE]), ps("up", [SLOTS, FE]), ps("h_turned", [P, KF, SLOTS])
        px = [ps(f"x_turned{m}", [P, 4, SLOTS]) for m in range(2)]
        py = [ps(f"y{m}", [SLOTS, 512]) for m in range(2)]
        slot_ident = R.ident[0:SLOTS, 0:SLOTS]
        raw_free = [sem(f"raw_free{c}") for c in range(6)]
        hi_done, lo_done = sem("hi_done"), sem("lo_done")
        used = sem("used")
        xe_in = sem("xe_in")
        x_turned, x_hi_done, x_lo_done = sem("x_turned"), sem("x_hi_done"), sem("x_lo_done")
        silu_done, hid_done = sem("silu_done"), sem("hid_done")
        h_turned, h_hi_done, h_lo_done = sem("h_turned"), sem("h_hi_done"), sem("h_lo_done")
        y_done, y_stored = sem("y_done"), sem("y_stored")
        xe_set, rows_set = sem("xe_set"), sem("rows_set")
        N2 = D // 512
        router = Router(nc, ctx, R, H)

        def in_steps(eng, body, halfway=None):
            body("first", 0)
            body("loop", 1)
            for a, b in ((2, E // 2), (E // 2, E - 1)) if halfway else ((2, E - 1),):
                with eng.Fori(a, b) as s:
                    body("loop", s)
                if b == E // 2:
                    halfway()
            body("end", E - 1)
            body("last", E)

        with nc.Block() as block:
            @block.sync
            def _(sp):
                for c in (4, 5):
                    load_chunk(sp, A, H, c, 0)

                def load(c, e):
                    sp.wait_ge(raw_free[c], e)
                    load_chunk(sp, A, H, c, e)

                for c in range(4):
                    load(c, 1)
                with sp.Fori(2, E) as s:
                    for c in range(6):
                        load(c, s if c < 4 else s - 1)
                for c in (4, 5):
                    place = Chunks("last", E).place(c)
                    sp.wait_ge(raw_free[place], E)
                    load_chunk(sp, A, H, c, E - 1, place)

            @block.gpsimd
            def _(pool):
                def load(e, moved):
                    if not first(e):
                        wait_alone(pool, x_turned, e * 2, R.passed)
                    pool.tensor_copy(row_in[:], H.slots[:, 0, ds(e, 1)]).then_inc(rows_set, 1)
                    wait_alone(pool, rows_set, moved + 1, R.passed)
                    pool.indirect_dma_start(
                        out=xe[:], out_offset=None, in_=xf_rows, in_offset=bass.IndirectOffsetOnAxis(ap=row_in[:], axis=0),
                        bounds_check=T - 1, oob_is_err=False).then_inc(xe_in, 16)

                def store(e, moved):
                    if not first(e):
                        wait_alone(pool, y_stored, e * 16, R.passed)
                    pool.tensor_copy(row_out[:], H.slots[:, 1, ds(e, 1)]).then_inc(rows_set, 1)
                    wait_alone(pool, y_done, e * N2 + N2, R.passed)
                    wait_alone(pool, rows_set, moved + 1, R.passed)
                    pool.indirect_dma_start(
                        out=y_rows, out_offset=bass.IndirectOffsetOnAxis(ap=row_out[:], axis=0), in_=y[:], in_offset=None,
                        bounds_check=2 * T - 1, oob_is_err=False).then_inc(y_stored, 16)

                def body(kind, s):
                    if kind in ("first", "loop"):
                        load(s + 1, 2 * s + 1 - (kind != "first"))
                    if kind != "first":
                        store(s - 1, 2 * s + (kind == "loop") - (kind == "last"))

                pool.memset(xe[:], 0.0).then_inc(xe_set, 1)
                pool.wait_ge(xe_set, 1)
                pool.wait_ge(router.slots_done, 1)
                load(0, 0)
                in_steps(pool, body)
                pool.wait_ge(y_stored, 16 * E)

            @block.tensor
            def _(pe):
                def three(out, a_hi, a_lo, b_hi, b_lo, first, last):
                    pe.matmul(out, a_hi, b_hi, start=first, stop=False)
                    pe.matmul(out, a_hi, b_lo, start=False, stop=False)
                    return pe.matmul(out, a_lo, b_hi, start=False, stop=last)

                def turn_x(e):
                    pe.wait_ge(xe_in, e * 16 + 16)
                    pe.wait_ge(x_lo_done, e * 2)
                    for k in range(KD):
                        ins = pe.transpose(px[k // 4][:, k % 4, :], xe[:, k * P:(k + 1) * P], slot_ident)
                        if k % 4 == 3:
                            ins.then_inc(x_turned, 1)

                def up_or_gate(ch, out, cs):
                    for i, c in enumerate(cs):
                        pe.wait_ge(lo_done, ch.order(c) + 1)
                        hi = w_hi[ch.slot(c)][:].rearrange("p (k n) -> p k n", k=4)
                        lo = w_lo[ch.slot(c)][:].rearrange("p (k n) -> p k n", k=4)
                        for k in range(4):
                            kk = 4 * i + k
                            ins = three(out[:], x_hi[:, kk, :], x_lo[:, kk, :], hi[:, k, :], lo[:, k, :],
                                        kk == 0, kk == KD - 1)
                        ins.then_inc(used, 1)

                def body(kind, s):
                    ch = Chunks(kind, s)
                    if kind != "last":
                        pe.wait_ge(x_lo_done, s * 2 + 2)
                        pe.wait_ge(silu_done, s)
                        up_or_gate(ch, pg, (0, 1))
                    if kind != "first":
                        pe.wait_ge(hid_done, s)
                        pe.wait_ge(h_lo_done, s - 1)
                        for k in range(KF):
                            ins = pe.transpose(ph[:, k, :], hid[:, k * P:(k + 1) * P], slot_ident)
                        ins.then_inc(h_turned, 1)
                    if kind != "last":
                        pe.wait_ge(hid_done, s)
                        up_or_gate(ch, pu, (2, 3))
                    if kind in ("first", "loop"):
                        turn_x(s + 1)
                    if kind != "first":
                        pe.wait_ge(h_lo_done, s)
                        pe.wait_ge(y_done, s * N2 - N2)
                        for i, c in enumerate((4, 5)):
                            pe.wait_ge(lo_done, ch.order(c) + 1)
                            hi = w_hi[ch.slot(c)][:].rearrange("p (k n) -> p k n", k=2)
                            lo = w_lo[ch.slot(c)][:].rearrange("p (k n) -> p k n", k=2)
                            for k in range(2):
                                kk = 2 * i + k
                                for m in range(N2):
                                    at = slice(m * 512, m * 512 + 512)
                                    ins = three(py[m][:], h_hi[:, kk, :], h_lo[:, kk, :], hi[:, k, at], lo[:, k, at],
                                                kk == 0, kk == KF - 1)
                            ins.then_inc(used, 1)

                router.tensor(pe)
                turn_x(0)
                in_steps(pe, body)

            def splitting(eng, part, x_part, h_part, mid, end, halfway=None):
                def ahead(kind, s):
                    rows_first = not (isinstance(s, int) and s == 0)
                    for c in (0, 1, 2):
                        part(Chunks(kind, s), c)
                        if c == (0 if rows_first else 2):
                            x_part(s)

                def body(kind, s):
                    ch = Chunks(kind, s)
                    if kind != "last":
                        part(ch, 3)
                    if kind != "first":
                        h_part(s - 1)
                        part(ch, 4)
                        if kind == "last":
                            part(ch, 5)
                    if kind != "last":
                        mid(ch, s)
                        if kind != "first":
                            part(ch, 5)
                    if kind in ("first", "loop"):
                        ahead("loop" if kind == "first" else kind, s + 1)
                    if kind != "first":
                        end(ch, s - 1)

                ahead("first", 0)
                in_steps(eng, body, halfway)

            @block.scalar
            def _(act):
                def part(ch, c):
                    act.wait_ge(raw_in[ch.place(c)], ch.turn(c) * 16 + 16)
                    if not (ch.kind == "first" and c < 3):
                        act.wait_ge(used, ch.order(c) - 2)
                    act.activation(w_hi[ch.slot(c)][:], raw[ch.place(c)], ACT.Copy).then_inc(hi_done, 1)

                def x_part(e):
                    for m in range(2):
                        act.wait_ge(x_turned, e * 2 + m + 1)
                        act.activation(x_hi[:, 4 * m:4 * m + 4, :], px[m][:], ACT.Copy).then_inc(x_hi_done, 1)

                def h_part(e):
                    act.wait_ge(h_turned, e + 1)
                    act.activation(h_hi[:], ph[:], ACT.Copy).then_inc(h_hi_done, 1)

                def silu(ch, e):
                    act.wait_ge(used, ch.order(1) + 1)
                    act.wait_ge(hid_done, e)
                    act.activation(sil[:], pg[:], ACT.Silu).then_inc(silu_done, 1)

                router.scalar(act)
                splitting(act, part, x_part, h_part, silu, lambda ch, e: None)

            @block.vector
            def _(dve):
                def part(ch, c):
                    dve.wait_ge(hi_done, ch.order(c) + 1)
                    s = ch.slot(c)
                    place = ch.place(c)
                    dve.tensor_tensor(w_lo[s][:], raw[place], w_hi[s][:].bitcast(F32), ALU.subtract).then_inc(lo_done, 1)
                    dve.wait_ge(lo_done, ch.order(c) + 1)
                    dve.sem_inc(raw_free[place], 1)

                def x_part(e):
                    for m in range(2):
                        dve.wait_ge(x_hi_done, e * 2 + m + 1)
                        dve.tensor_tensor(x_lo[:, 4 * m:4 * m + 4, :], px[m][:],
                                          x_hi[:, 4 * m:4 * m + 4, :].bitcast(F32), ALU.subtract).then_inc(x_lo_done, 1)

                def h_part(e):
                    dve.wait_ge(h_hi_done, e + 1)
                    dve.tensor_tensor(h_lo[:], ph[:], h_hi[:].bitcast(F32), ALU.subtract).then_inc(h_lo_done, 1)

                def hidden(ch, e):
                    dve.wait_ge(silu_done, e + 1)
                    dve.wait_ge(used, ch.order(3) + 1)
                    dve.wait_ge(h_turned, e)
                    dve.tensor_tensor(hid[:], sil[:], pu[:], ALU.mult).then_inc(hid_done, 1)

                def out(ch, e):
                    dve.wait_ge(used, ch.order(5) + 1)
                    dve.wait_ge(y_stored, e * 16)
                    for m in range(N2):
                        dve.tensor_copy(y[:, m * 512:m * 512 + 512], py[m][:]).then_inc(y_done, 1)

                router.vector(dve)
                splitting(dve, part, x_part, h_part, hidden, out, lambda: router.weigh(dve))


def overflow(nc, A, R, H, xf_rows, y_rows):
    with ExitStack() as ctx:
        sb = lambda n, s, d=F32: ctx.enter_context(nc.sbuf_tensor(f"ov_{n}", s, d))
        sem = lambda n: ctx.enter_context(nc.semaphore(f"ov_{n}"))
        ps = lambda n, s: ctx.enter_context(nc.psum_tensor(f"ov_{n}", s, F32))
        wg, wu, wd = sb("w_gate", [P, KD, FE]), sb("w_up", [P, KD, FE]), sb("w_down", [P, KF, D])
        xt, x_t = sb("rows", [P, D]), sb("rows_t", [P, KD, P])
        sil, hid, hid_t = sb("silu", [P, FE]), sb("hidden", [P, FE]), sb("hidden_t", [P, KF, P])
        px = [ps(f"x_turned{m}", [P, 4, P]) for m in range(2)]
        pg, pu, ph = ps("gate", [P, FE]), ps("up", [P, FE]), ps("h_turned", [P, KF, P])
        py = [ps(f"y{m}", [P, 512]) for m in range(2)]
        w_in, x_in = sem("w_in"), sem("x_in")
        x_turned, x_out = sem("x_turned"), sem("x_out")
        gu_done, silu_done, hid_done = sem("gu_done"), sem("silu_done"), sem("hid_done")
        h_turned, h_out, y_done, added = sem("h_turned"), sem("h_out"), sem("y_done"), sem("added")
        none, none_set, none_out = sb("none", [P, D]), sem("none_set"), sem("none_out")
        w_now, w_copied = sb("w_now", [P, 1]), sem("w_copied")

        def listed(eng, i):
            return eng.value_load(H.over[0:1, ds(i, 1)], min_val=0, max_val=E - 1)

        def over_experts(eng, each):
            n_over = eng.value_load(H.over[0:1, E:E + 1], min_val=0, max_val=E)
            with eng.If(n_over > 0):
                with eng.Fori(0, n_over) as i:
                    each(i)
            eng.nop()

        def over_tiles(eng, i, body):
            with eng.Fori(0, NT) as t:
                body(t, i * NTILE + t + 1, P)
            body(NT, i * NTILE + NT + 1, DEC)

        def start_at_one(eng, *sems):
            for s, per_tile in sems:
                eng.sem_inc(s, per_tile)

        with nc.Block() as block:
            @block.sync
            def _(sp):
                def each(i):
                    e = listed(sp, i)
                    sp.wait_ge(added, i * (2 * NTILE) + 2)
                    for dst, name in ((wg, "w_exp_gate"), (wu, "w_exp_up"), (wd, "w_exp_down")):
                        src = A[name][0, ds(e, 1)].rearrange("o (k p) n -> p (o k) n", p=P)
                        sp.dma_start(dst[:], src).then_inc(w_in, 16)

                    def body(t, g, n):
                        sp.wait_ge(x_turned, g * 2)
                        sp.dma_start(xt[0:n, :], xf_rows[ds(t * P, n), :]).then_inc(x_in, 16)

                    over_tiles(sp, i, body)

                start_at_one(sp, (x_in, 16))
                over_experts(sp, each)

            @block.gpsimd
            def _(pool):
                n_over = pool.value_load(H.over[0:1, E:E + 1], min_val=0, max_val=E)
                with pool.If(n_over > 0):
                    pool.memset(none[:], 0.0).then_inc(none_set, 1)
                    pool.wait_ge(none_set, 1)
                    for t in range(NTILE):
                        n = P if t < NT else DEC
                        for k in range(2):
                            pool.indirect_dma_start(
                                out=y_rows, in_=none[0:n, :], in_offset=None, bounds_check=2 * T - 1, oob_is_err=False,
                                out_offset=bass.IndirectOffsetOnAxis(ap=H.unfilled[k][0:n, t:t + 1], axis=0),
                                ).then_inc(none_out, 16)
                    pool.wait_ge(none_out, 2 * NTILE * 16)
                pool.nop()

            @block.tensor
            def _(pe):
                def each(i):
                    wait_alone(pe, w_in, i * 48 + 48, R.passed)

                    def body(t, g, n):
                        pe.wait_ge(x_in, g * 16 + 16)
                        wait_alone(pe, x_out, g * 2, R.passed)
                        for k in range(KD):
                            ins = pe.transpose(px[k // 4][:, k % 4, 0:n], xt[0:n, k * P:(k + 1) * P], R.ident[0:n, 0:n])
                            if k % 4 == 3:
                                ins.then_inc(x_turned, 1)
                        pe.wait_ge(x_out, g * 2 + 2)
                        pe.wait_ge(hid_done, g)
                        for out, w in ((pg, wg), (pu, wu)):
                            for k in range(KD):
                                ins = pe.matmul(out[0:n, :], x_t[:, k, 0:n], w[:, k, :], start=(k == 0), stop=(k == KD - 1))
                            ins.then_inc(gu_done, 1)
                        pe.wait_ge(h_out, g)
                        wait_alone(pe, hid_done, g + 1, R.passed)
                        for k in range(KF):
                            ins = pe.transpose(ph[:, k, 0:n], hid[0:n, k * P:(k + 1) * P], R.ident[0:n, 0:n])
                        ins.then_inc(h_turned, 1)
                        pe.wait_ge(h_out, g + 1)
                        pe.wait_ge(added, g * 2)
                        for m in range(2):
                            for k in range(KF):
                                ins = pe.matmul(py[m][0:n, :], hid_t[:, k, 0:n], wd[:, k, m * 512:m * 512 + 512],
                                                start=(k == 0), stop=(k == KF - 1))
                            ins.then_inc(y_done, 1)

                    over_tiles(pe, i, body)

                start_at_one(pe, (x_turned, 2), (gu_done, 2), (h_turned, 1), (y_done, 2))
                over_experts(pe, each)

            @block.scalar
            def _(act):
                def each(i):
                    def body(t, g, n):
                        act.wait_ge(gu_done, g * 2)
                        for m in range(2):
                            act.wait_ge(x_turned, g * 2 + m + 1)
                            act.activation(x_t[:, 4 * m:4 * m + 4, 0:n], px[m][:, :, 0:n], ACT.Copy).then_inc(x_out, 1)
                        act.wait_ge(gu_done, g * 2 + 1)
                        act.wait_ge(hid_done, g)
                        act.activation(sil[0:n, :], pg[0:n, :], ACT.Silu).then_inc(silu_done, 1)
                        act.wait_ge(h_turned, g + 1)
                        act.wait_ge(y_done, g * 2)
                        act.activation(hid_t[:, :, 0:n], ph[:, :, 0:n], ACT.Copy).then_inc(h_out, 1)

                    over_tiles(act, i, body)

                start_at_one(act, (x_out, 2), (silu_done, 1), (h_out, 1))
                over_experts(act, each)

            @block.vector
            def _(dve):
                def each(i):
                    e = listed(dve, i)

                    def body(t, g, n):
                        dve.wait_ge(silu_done, g + 1)
                        dve.wait_ge(gu_done, g * 2 + 2)
                        dve.wait_ge(h_turned, g)
                        dve.tensor_tensor(hid[0:n, :], sil[0:n, :], pu[0:n, :], ALU.mult).then_inc(hid_done, 1)
                        wait_alone(dve, added, g * 2, R.passed)
                        dve.tensor_copy(w_now[0:n, :], H.w_over[0:n, ds(t, 1), ds(e, 1)].rearrange("p a b -> p (a b)")
                                        ).then_inc(w_copied, 1)
                        dve.wait_ge(w_copied, g + 1)
                        h_t = tile_at(H.h, t, n)
                        for m in range(2):
                            at = slice(m * 512, m * 512 + 512)
                            dve.wait_ge(y_done, g * 2 + m + 1)
                            dve.scalar_tensor_tensor(out=h_t[:, at], in0=py[m][0:n, :], scalar=w_now[0:n, :],
                                                     in1=h_t[:, at], op0=ALU.mult, op1=ALU.add).then_inc(added, 1)

                    over_tiles(dve, i, body)

                start_at_one(dve, (hid_done, 1), (w_copied, 1), (added, 2))
                over_experts(dve, each)


def combine(nc, A, R, H, y_rows, outs):
    with ExitStack() as ctx:
        sb = lambda n, s, d=F32: ctx.enter_context(nc.sbuf_tensor(f"co_{n}", s, d))
        sem = lambda n: ctx.enter_context(nc.semaphore(f"co_{n}"))
        RING = 3
        yb = [sb(f"y{b}", [P, 2, D]) for b in range(RING)]
        out = [sb(f"out{b}", [P, D]) for b in range(2)]
        g_fin = sb("g_final", [P, D])
        ss, rms, rstd = (sb(n, [P, NTILE]) for n in ("sum_sq", "rms", "rstd"))
        small = sb("small", [ST_N, P])
        pst = ctx.enter_context(nc.psum_tensor("co_stage", [P, 512], F32))
        g_in = sem("g_in")
        y_in = [sem(f"y_in{b}") for b in range(RING)]
        mixed, sq_done, rms_done = sem("mixed"), sem("sq_done"), sem("rms_done")
        rstd_done, out_done = sem("rstd_done"), sem("out_done")
        stored = [sem(f"stored{b}") for b in range(2)]
        st_turned, st_out, st_stored = sem("st_turned"), sem("st_out"), sem("st_stored")
        n_rows = lambda t: P if t < NT else DEC
        y_prompt, y_sample, conv_p, lru_p, conv_s, lru_s = outs

        with nc.Block() as block:
            @block.gpsimd
            def _(pool):
                for t in range(NTILE):
                    b, n = t % RING, n_rows(t)
                    if t >= RING:
                        pool.wait_ge(mixed, 2 * (t - RING + 1))
                    src = y_rows[2 * t * P:2 * (t * P + n), :].rearrange("(n k) d -> n (k d)", k=2)
                    pool.dma_start(yb[b][0:n].rearrange("n k d -> n (k d)"), src).then_inc(y_in[b], 16)

            @block.vector
            def _(dve):
                def finish(t):
                    b, n = t % 2, n_rows(t)
                    dve.wait_ge(rms_done, t + 1)
                    dve.reciprocal(rstd[0:n, t:t + 1], rms[0:n, t:t + 1]).then_inc(rstd_done, 1)
                    dve.wait_ge(rstd_done, t + 1)
                    if t >= 2:
                        dve.wait_ge(stored[b], 16 * (t // 2))
                    dve.scalar_tensor_tensor(out=out[b][0:n, :], in0=H.h[0:n, t, :], scalar=rstd[0:n, t:t + 1],
                                             in1=g_fin[0:n, :], op0=ALU.mult, op1=ALU.mult).then_inc(out_done, 1)

                dve.wait_ge(g_in, 16)
                for t in range(NTILE):
                    b, n = t % RING, n_rows(t)
                    dve.wait_ge(y_in[b], 16 * (t // RING) + 16)
                    for k in range(2):
                        if k:
                            dve.wait_ge(mixed, 2 * t + 1)
                        dve.scalar_tensor_tensor(out=H.h[0:n, t, :], in0=yb[b][0:n, k, :], scalar=H.w[k][0:n, t:t + 1],
                                                 in1=H.h[0:n, t, :], op0=ALU.mult, op1=ALU.add).then_inc(mixed, 1)
                    if t:
                        finish(t - 1)
                finish(NT)

            @block.scalar
            def _(act):
                act.wait_ge(st_turned, 1)
                act.activation(small[:], pst[0:ST_N, 0:P], ACT.Copy).then_inc(st_out, 1)
                for t in range(NTILE):
                    b, n = t % 2, n_rows(t)
                    act.wait_ge(mixed, 2 * t + 2)
                    if t >= 2:
                        act.wait_ge(stored[b], 16 * (t // 2))
                    act.activation(out[b][0:n, :], H.h[0:n, t, :], ACT.Square,
                                   accum_out=ss[0:n, t:t + 1]).then_inc(sq_done, 1)
                    act.wait_ge(sq_done, t + 1)
                    act.activation(rms[0:n, t:t + 1], ss[0:n, t:t + 1], ACT.Sqrt, bias=R.eps[0:n, :],
                                   scale=1.0 / D).then_inc(rms_done, 1)

            @block.tensor
            def _(pe):
                pe.transpose(pst[0:ST_N, 0:P], R.stage[:], R.ident[:]).then_inc(st_turned, 1)

            @block.sync
            def _(sp):
                sp.dma_start(g_fin[:], A["norm_final_g"].partition_broadcast(P)).then_inc(g_in, 16)
                sp.wait_ge(st_out, 1)
                for at, n, dst in ((ST_CONVP, 24, conv_p), (ST_CONVS, 24, conv_s)):
                    sp.dma_start(dst[0, 0].rearrange("j (n p) -> (j n) p", p=P), small[at:at + n, :]).then_inc(st_stored, 16)
                for at, n, dst in ((ST_LRUP, 8, lru_p), (ST_LRUS, 8, lru_s)):
                    sp.dma_start(dst[0, 0].rearrange("(n p) -> n p", p=P), small[at:at + n, :]).then_inc(st_stored, 16)
                for t in range(NTILE):
                    b, n = t % 2, n_rows(t)
                    sp.wait_ge(out_done, t + 1)
                    dst = y_prompt[0, t * P:(t + 1) * P, :] if t < NT else y_sample[0]
                    sp.dma_start(dst, out[b][0:n, :]).then_inc(stored[b], 16)
                for b in range(2):
                    sp.wait_ge(stored[b], 16 * len(range(b, NTILE, 2)))
                sp.wait_ge(st_stored, 64)


class Resident:

    def __init__(self, nc, ctx):
        sb = lambda n, s, d=F32: ctx.enter_context(nc.sbuf_tensor(n, s, d))
        self.passed = ctx.enter_context(nc.semaphore("passed"))
        self.spent = []
        self.const = sb("const", [P, CN_N])
        self.ident = self.const[:, CN_ID:CN_ID + P]
        self.par = sb("par", [P, PR_N])
        self.stage = sb("stage", [P, ST_N])
        self.eps = sb("eps", [P, 1])
        self.u = sb("u", [P, KD * T])
        self.w_out_in = ctx.enter_context(nc.semaphore("w_out_in"))
        self.lam_neg = sb("lam_neg", [P, 8])
        self.lam_pos = sb("lam_pos", [P, 8])

    def spend(self, sem):
        self.spent.append(sem)
        return sem


class Routed:

    def __init__(self, nc, ctx, R):
        sb = lambda n, s, d=F32: ctx.enter_context(nc.sbuf_tensor(f"h_{n}", s, d))
        self.raw = [R.u[:, c * CHUNK_W:(c + 1) * CHUNK_W] for c in range(4)]
        self.raw_in = [ctx.enter_context(nc.semaphore(f"raw_in{c}")) for c in range(6)]
        self.h = sb("residual", [P, NTILE, D])
        self.logits = sb("logits", [P, NTILE, ROUT])
        self.bias = sb("bias", [P, ROUT])
        self.g_ffn = sb("g_ffn", [P, D])
        self.rms, self.rstd = sb("rms", [P, NTILE]), sb("rstd", [P, NTILE])
        self.slots = sb("slots", [SLOTS, 2, E], U32)
        self.unfilled = [sb(f"unfilled{k}", [P, NTILE], U32) for k in range(2)]
        self.w = [sb(f"w{k}", [P, NTILE]) for k in range(2)]
        self.w_over = sb("w_over", [P, NTILE, E])
        self.over = sb("over", [1, E + 1], I32)


def trunk_kernel(nc, A, outs):
    y_prompt, y_sample, conv_p, lru_p, ret_p, conv_s, lru_s, ret_s = outs
    merged_lru = nc.dram_tensor("merged_lru", (KD, P, T), F32).ap()
    merged = nc.dram_tensor("merged", (KD, P, T), F32).ap()
    y_rows = nc.dram_tensor("y_rows", (2 * T, D), F32).ap()
    xf_rows = nc.dram_tensor("xf_rows", (T, D), F32).ap()
    with ExitStack() as ctx:
        R = Resident(nc, ctx)
        with ExitStack() as mixer:
            M = Mixer(nc, mixer, R)
            block = lambda name, col=0: A[name][0][:, col * D:col * D + P]
            first_lru = block("w_in", 0), block("w_in", 1)
            first_merge = block("w_in", 6), block("w_lru_o")
            first_ret = block("w_in", 4), block("w_in", 3)
            first_merge2 = block("w_in", 7), block("w_ret_o")
            normalise(nc, A, R, M, first_lru)
            M.psum.append(M.bank_set(mixer, 1))
            lru(nc, A, R, M, first_merge)
            M.next_stage(KD)
            merge(nc, A, R, M, "ml", 6, "w_lru_o", None, merged_lru, first_ret)
            M.next_stage(KD)
            retention(nc, A, R, M, ret_p[0, 0], ret_s[0, 0], first_merge2)
            M.next_stage(HEADS * 2)
            merge(nc, A, R, M, "mr", 7, "w_ret_o", merged_lru, merged, None)
        H = Routed(nc, ctx, R)
        out_proj(nc, A, R, H, merged, xf_rows)
        experts(nc, A, R, H, xf_rows, y_rows)
        overflow(nc, A, R, H, xf_rows, y_rows)
        combine(nc, A, R, H, y_rows, (y_prompt, y_sample, conv_p, lru_p, conv_s, lru_s))


_INS = ["x_prompt", "x_sample", "cache_conv", "state_lru", "state_ret", "norm_mix_g", "w_in", "conv_w", "conv_b",
        "lru_wa", "lru_ba", "lru_wx", "lru_bx", "lru_lambda", "ret_gn_g", "w_lru_o", "w_ret_o", "w_out", "norm_ffn_g",
        "w_router_group", "b_router_group", "w_router_expert", "b_router_expert", "w_exp_gate", "w_exp_up",
        "w_exp_down", "norm_final_g"]
_OUTS = [(1, SEQ, D), (1, DEC, D), (1, 1, PAD, D), (1, 1, D), (1, 1, HEADS, P, P),
         (1, 1, PAD, D), (1, 1, D), (1, 1, HEADS, P, P)]


def kernel(**inputs):
    import numpy as _np
    import concourse.bacc as _bacc
    from concourse.bass_utils import run_bass_kernel_spmd as _run

    nc = _bacc.Bacc("TRN2", target_bir_lowering=False, num_devices=1)
    arrays, A = {}, {}
    tables, small = shape_tables()
    for name, a in [(n, inputs[n]) for n in _INS] + [("const_tables", tables), ("const_small", small)]:
        a = _np.ascontiguousarray(a)
        arrays[f"in_{name}"] = a
        A[name] = nc.dram_tensor(f"in_{name}", a.shape, mybir.dt.from_np(a.dtype), kind="ExternalInput").ap()
    outs = [nc.dram_tensor(f"out_{i}", shape, F32, kind="ExternalOutput").ap() for i, shape in enumerate(_OUTS)]
    trunk_kernel(nc, A, outs)
    r = _run(nc, [arrays], core_ids=[0])
    return tuple(r.results[0][f"out_{i}"] for i in range(len(_OUTS)))
```
